# Optimizing a Trainium2 kernel written in Bass

```python
import math
import jax
import jax.numpy as jnp
from jax import lax
import numpy as np

D_MODEL = 1024
BATCH = 1
SEQ = 1024
DEPTH = 1
DEC_BATCH = 1
DEC_SEQ = 64
PAST_LEN = 512

CHUNK = 64
HEAD_DIM = 64
A_HEADS = 8
A_KV = 2
IDX_HEADS = 4
IDX_DIM = 64
TOPK_MAX = 256
Q_BLOCK = 128
B_HEADS = 8
B_KV = 2
WINDOW = 128
W_CHUNKS = WINDOW // CHUNK
A_WIDTH = A_HEADS * HEAD_DIM
B_WIDTH = B_HEADS * HEAD_DIM
N_BUCKETS = 32
MAX_DISTANCE = 1024
EPS = 1e-6
NEG = -1e30
COL_NAMES = ('a_q', 'a_k', 'a_v', 'a_z', 'i_q', 'i_k', 'i_w', 'b_q', 'b_k', 'b_v', 'b_z', 'g_a', 'g_b')
COL_SIZES = (A_WIDTH, A_KV * HEAD_DIM, A_KV * HEAD_DIM, A_WIDTH, IDX_HEADS * IDX_DIM, IDX_DIM, IDX_HEADS,
             B_WIDTH, B_KV * HEAD_DIM, B_KV * HEAD_DIM, B_WIDTH, D_MODEL, D_MODEL)
IN_WIDTH = sum(COL_SIZES)

kernel_name = 'hybrid_dsa_swa_stream_step'

def rmsnorm(x, g):
    xf = x.astype(jnp.float32)
    y = xf * lax.rsqrt(jnp.mean(xf * xf, axis=-1, keepdims=True) + EPS)
    return (y * g.astype(jnp.float32)).astype(x.dtype)

def t5_bucket(rel):
    half = N_BUCKETS // 2
    max_exact = half // 2
    n = jnp.abs(rel)
    nf = jnp.maximum(n, 1).astype(jnp.float32)
    large = max_exact + (jnp.log(nf / max_exact) / math.log(MAX_DISTANCE / max_exact)
                         * (half - max_exact)).astype(jnp.int32)
    large = jnp.minimum(large, half - 1)
    return (rel > 0).astype(jnp.int32) * half + jnp.where(n < max_exact, n, large)

def layer_inputs(x, c, norm_g, w_ada, b_ada, w_in, a_qn, a_kn, b_qn, b_kn):
    n, t = x.shape[:2]
    mod = jax.nn.silu(c) @ w_ada + b_ada
    shift, scale, gate = jnp.split(mod[:, None, :], 3, axis=-1)
    h = rmsnorm(x, norm_g) * (1 + scale) + shift
    offs = [int(o) for o in np.cumsum(COL_SIZES)[:-1]]
    p = dict(zip(COL_NAMES, jnp.split(h @ w_in, offs, axis=-1)))
    p['a_q'] = rmsnorm(p['a_q'].reshape(n, t, A_HEADS, HEAD_DIM), a_qn)
    p['a_k'] = rmsnorm(p['a_k'].reshape(n, t, A_KV, HEAD_DIM), a_kn)
    p['a_v'] = p['a_v'].reshape(n, t, A_KV, HEAD_DIM)
    p['i_q'] = p['i_q'].reshape(n, t, IDX_HEADS, IDX_DIM)
    p['b_q'] = rmsnorm(p['b_q'].reshape(n, t, B_HEADS, HEAD_DIM), b_qn)
    p['b_k'] = rmsnorm(p['b_k'].reshape(n, t, B_KV, HEAD_DIM), b_kn)
    p['b_v'] = p['b_v'].reshape(n, t, B_KV, HEAD_DIM)
    return gate, p

def dsa_attend(q, iq, iw, q_pos, k, v, ik, k_pos, k_sel, rel_bias):
    f32 = jnp.float32
    n, tq = q.shape[:2]
    g = A_HEADS // A_KV
    dots = jnp.einsum('nqhd,nkd->nqhk', iq.astype(f32), ik.astype(f32)) * IDX_DIM ** -0.5
    score = jnp.einsum('nqhk,nqh->nqk', jax.nn.relu(dots), iw.astype(f32)) * IDX_HEADS ** -0.5
    q_ch = q_pos // CHUNK
    admissible = (k_pos[None, :] // CHUNK) <= q_ch[:, None]
    score = jnp.where(admissible[None], score, NEG)
    _, sel = lax.top_k(score, k_sel)
    sel_pos = k_pos[sel]
    valid = (sel_pos // CHUNK) <= q_ch[None, :, None]
    take = jax.vmap(lambda rows, idx: rows[idx])
    ks = take(k, sel).astype(f32)
    vs = take(v, sel).astype(f32)
    qg = q.reshape(n, tq, A_KV, g, HEAD_DIM).astype(f32)
    logits = jnp.einsum('nqcgd,nqkcd->nqcgk', qg, ks) * HEAD_DIM ** -0.5
    bias = rel_bias[t5_bucket(sel_pos - q_pos[None, :, None])][..., :A_HEADS].astype(f32)
    logits = logits + jnp.einsum('nqkcg->nqcgk', bias.reshape(n, tq, k_sel, A_KV, g))
    logits = jnp.where(valid[:, :, None, None, :], logits, NEG)
    probs = jax.nn.softmax(logits, axis=-1)
    out = jnp.einsum('nqcgk,nqkcd->nqcgd', probs, vs)
    return out.reshape(n, tq, A_WIDTH).astype(q.dtype)

def dsa_prompt(q, iq, iw, k, v, ik, rel_bias):
    bn, s = q.shape[:2]
    nblk = s // Q_BLOCK
    k_sel = min(TOPK_MAX, s // 4)
    k_pos = jnp.arange(s)

    def to_blocks(t):
        return jnp.moveaxis(t.reshape(bn, nblk, Q_BLOCK, *t.shape[2:]), 1, 0)

    def one(args):
        qb, iqb, iwb, blk = args
        q_pos = blk * Q_BLOCK + jnp.arange(Q_BLOCK)
        return dsa_attend(qb, iqb, iwb, q_pos, k, v, ik, k_pos, k_sel, rel_bias)

    out = lax.map(one, (to_blocks(q), to_blocks(iq), to_blocks(iw), jnp.arange(nblk)))
    return jnp.moveaxis(out, 0, 1).reshape(bn, s, A_WIDTH)

def swa_attend(q, q_pos, k, v, k_pos, sinks, rel_bias):
    f32 = jnp.float32
    g = B_HEADS // B_KV
    qg = q.reshape(*q.shape[:-2], B_KV, g, HEAD_DIM).astype(f32)
    logits = jnp.einsum('...qcgd,...kcd->...cgqk', qg, k.astype(f32)) * HEAD_DIM ** -0.5
    rel = k_pos[..., None, :] - q_pos[..., :, None]
    bias = rel_bias[t5_bucket(rel)][..., A_HEADS:].astype(f32)
    bias = bias.reshape(*bias.shape[:-1], B_KV, g)
    logits = logits + jnp.einsum('...qkcg->...cgqk', bias)
    qch = q_pos[..., :, None] // CHUNK
    kch = k_pos[..., None, :] // CHUNK
    vis = (k_pos[..., None, :] >= 0) & (kch <= qch) & (qch - kch <= W_CHUNKS)
    logits = jnp.where(vis[..., None, None, :, :], logits, NEG)
    sink = sinks.astype(f32).reshape(B_KV, g)[:, :, None]
    m = jnp.maximum(logits.max(axis=-1), sink)
    p = jnp.exp(logits - m[..., None])
    denom = p.sum(axis=-1) + jnp.exp(sink - m)
    o = jnp.einsum('...cgqk,...kcd->...qcgd', p, v.astype(f32))
    o = o / jnp.einsum('...cgq->...qcg', denom)[..., None]
    return o.reshape(*o.shape[:-3], B_WIDTH).astype(q.dtype)

def swa_prompt(q, k, v, sinks, rel_bias):
    bn, s = q.shape[:2]
    nc = s // CHUNK
    pad = W_CHUNKS * CHUNK

    def band(t):
        tp = jnp.pad(t, ((0, 0), (pad, 0)) + ((0, 0),) * (t.ndim - 2))
        tp = tp.reshape(bn, nc + W_CHUNKS, CHUNK, *t.shape[2:])
        return jnp.concatenate([tp[:, j:j + nc] for j in range(W_CHUNKS + 1)], axis=2)

    kb, vb = band(k), band(v)
    kp = jnp.arange(-pad, s).reshape(nc + W_CHUNKS, CHUNK)
    kpos = jnp.concatenate([kp[j:j + nc] for j in range(W_CHUNKS + 1)], axis=1)
    qpos = jnp.arange(s).reshape(nc, CHUNK)
    qc = q.reshape(bn, nc, CHUNK, B_HEADS, HEAD_DIM)
    out = swa_attend(qc, qpos, kb, vb, kpos, sinks, rel_bias)
    return out.reshape(bn, s, B_WIDTH)

def layer_output(x, gate, p, att_a, att_b, w_oa, w_ob, w_out):
    o_a = (att_a * jax.nn.silu(p['a_z'])) @ w_oa
    o_b = (att_b * jax.nn.silu(p['b_z'])) @ w_ob
    merged = jax.nn.sigmoid(p['g_a']) * o_a + jax.nn.sigmoid(p['g_b']) * o_b
    return x + gate * (merged @ w_out)

def setup_inputs(seed: int = 0) -> dict:
    key = jax.random.key(seed)
    ks = jax.random.split(key, 22)
    f32 = jnp.float32

    def nrm(k, shape, s=1.0):
        return s * jax.random.normal(k, shape, f32)

    wc = min(WINDOW, PAST_LEN)
    return {
        'x_prompt': nrm(ks[0], (BATCH, SEQ, D_MODEL)),
        'x_sample': nrm(ks[1], (DEC_BATCH, DEC_SEQ, D_MODEL)),
        'cache_a_k': nrm(ks[2], (DEPTH, DEC_BATCH, PAST_LEN, A_KV, HEAD_DIM)),
        'cache_a_v': nrm(ks[3], (DEPTH, DEC_BATCH, PAST_LEN, A_KV, HEAD_DIM)),
        'cache_a_ik': nrm(ks[4], (DEPTH, DEC_BATCH, PAST_LEN, IDX_DIM)),
        'cache_b_k': nrm(ks[5], (DEPTH, DEC_BATCH, wc, B_KV, HEAD_DIM)),
        'cache_b_v': nrm(ks[6], (DEPTH, DEC_BATCH, wc, B_KV, HEAD_DIM)),
        'c_prompt': nrm(ks[7], (BATCH, D_MODEL)),
        'c_sample': nrm(ks[8], (DEC_BATCH, D_MODEL)),
        'norm_g': 1.0 + nrm(ks[9], (DEPTH, D_MODEL), 0.05),
        'w_ada': nrm(ks[10], (DEPTH, D_MODEL, 3 * D_MODEL), 0.5 * D_MODEL ** -0.5),
        'b_ada': nrm(ks[11], (DEPTH, 3 * D_MODEL), 0.01),
        'w_in': nrm(ks[12], (DEPTH, D_MODEL, IN_WIDTH), D_MODEL ** -0.5),
        'a_q_norm': 1.0 + nrm(ks[13], (DEPTH, HEAD_DIM), 0.05),
        'a_k_norm': 1.0 + nrm(ks[14], (DEPTH, HEAD_DIM), 0.05),
        'b_q_norm': 1.0 + nrm(ks[15], (DEPTH, HEAD_DIM), 0.05),
        'b_k_norm': 1.0 + nrm(ks[16], (DEPTH, HEAD_DIM), 0.05),
        'b_sinks': nrm(ks[17], (DEPTH, B_HEADS)),
        'rel_bias': nrm(ks[18], (N_BUCKETS, A_HEADS + B_HEADS), 0.5),
        'w_oa': nrm(ks[19], (DEPTH, A_WIDTH, D_MODEL), A_WIDTH ** -0.5),
        'w_ob': nrm(ks[20], (DEPTH, B_WIDTH, D_MODEL), B_WIDTH ** -0.5),
        'w_out': nrm(ks[21], (DEPTH, D_MODEL, D_MODEL), D_MODEL ** -0.5),
    }

def reference(x_prompt, x_sample, cache_a_k, cache_a_v, cache_a_ik, cache_b_k, cache_b_v,
              c_prompt, c_sample, norm_g, w_ada, b_ada, w_in, a_q_norm, a_k_norm, b_q_norm,
              b_k_norm, b_sinks, rel_bias, w_oa, w_ob, w_out):
    s_len = x_prompt.shape[1]
    t_len = x_sample.shape[1]
    past = cache_a_k.shape[2]
    wc = cache_b_k.shape[2]
    keep_p = min(WINDOW, s_len)
    pos_s = past + jnp.arange(t_len)
    ka_pos = jnp.arange(past + t_len)
    kb_pos = past - wc + jnp.arange(wc + t_len)
    k_sel_s = min(TOPK_MAX, (past + t_len) // 4)
    xp, xs = x_prompt, x_sample
    l_pa_k, l_pa_v, l_pa_ik, l_pb_k, l_pb_v = [], [], [], [], []
    l_sa_k, l_sa_v, l_sa_ik, l_sb_k, l_sb_v = [], [], [], [], []
    for l in range(DEPTH):
        lw = (norm_g[l], w_ada[l], b_ada[l], w_in[l], a_q_norm[l], a_k_norm[l], b_q_norm[l], b_k_norm[l])
        gate, p = layer_inputs(xp, c_prompt, *lw)
        att_a = dsa_prompt(p['a_q'], p['i_q'], p['i_w'], p['a_k'], p['a_v'], p['i_k'], rel_bias)
        att_b = swa_prompt(p['b_q'], p['b_k'], p['b_v'], b_sinks[l], rel_bias)
        l_pa_k.append(p['a_k'])
        l_pa_v.append(p['a_v'])
        l_pa_ik.append(p['i_k'])
        l_pb_k.append(p['b_k'][:, s_len - keep_p:])
        l_pb_v.append(p['b_v'][:, s_len - keep_p:])
        xp = layer_output(xp, gate, p, att_a, att_b, w_oa[l], w_ob[l], w_out[l])
        gate, p = layer_inputs(xs, c_sample, *lw)
        ka = jnp.concatenate([cache_a_k[l], p['a_k']], axis=1)
        va = jnp.concatenate([cache_a_v[l], p['a_v']], axis=1)
        ika = jnp.concatenate([cache_a_ik[l], p['i_k']], axis=1)
        att_a = dsa_attend(p['a_q'], p['i_q'], p['i_w'], pos_s, ka, va, ika, ka_pos, k_sel_s, rel_bias)
        kb = jnp.concatenate([cache_b_k[l], p['b_k']], axis=1)
        vb = jnp.concatenate([cache_b_v[l], p['b_v']], axis=1)
        att_b = swa_attend(p['b_q'], pos_s, kb, vb, kb_pos, b_sinks[l], rel_bias)
        l_sa_k.append(p['a_k'])
        l_sa_v.append(p['a_v'])
        l_sa_ik.append(p['i_k'])
        l_sb_k.append(kb[:, t_len:])
        l_sb_v.append(vb[:, t_len:])
        xs = layer_output(xs, gate, p, att_a, att_b, w_oa[l], w_ob[l], w_out[l])
    pa_k = jnp.stack(l_pa_k)
    pa_v = jnp.stack(l_pa_v)
    pa_ik = jnp.stack(l_pa_ik)
    pb_k = jnp.stack(l_pb_k)
    pb_v = jnp.stack(l_pb_v)
    sa_k = jnp.stack(l_sa_k)
    sa_v = jnp.stack(l_sa_v)
    sa_ik = jnp.stack(l_sa_ik)
    sb_k = jnp.stack(l_sb_k)
    sb_v = jnp.stack(l_sb_v)
    return (xp, xs, pa_k, pa_v, pa_ik, pb_k, pb_v, sa_k, sa_v, sa_ik, sb_k, sb_v)


_drawn_inputs = setup_inputs


def setup_inputs(seed=0):
    import zlib

    import numpy as np

    out = dict(_drawn_inputs(seed))
    spreads = {}
    factors = {'cache_a_k': 5.068,
     'cache_a_v': 3.998,
     'cache_a_ik': 4.492,
     'b_ada': 4.099,
     'a_q_norm': 8.0,
     'b_q_norm': 43.38,
     'b_sinks': 64.0,
     'rel_bias': 6.302}
    for name, (base, spread) in spreads.items():
        noise = np.random.default_rng([zlib.crc32(name.encode()), seed]).standard_normal(out[name].shape)
        drawn = base * np.exp(spread * noise) if base else spread * noise
        out[name] = jnp.asarray(drawn.astype(out[name].dtype))
    for name, factor in factors.items():
        out[name] = (out[name] * factor).astype(out[name].dtype)
    return out
```

```python
import concourse.bass as bass
from concourse import mybir
from contextlib import ExitStack

F32 = mybir.dt.float32
F32R = mybir.dt.float32r
BF16 = mybir.dt.bfloat16
I32 = mybir.dt.int32
ALU = mybir.AluOpType
ACT = mybir.ActivationFunctionType
AX = mybir.AxisListType

D = 1024
KD = D // 128
SEQ, DEC, PAST, WIN = 1024, 64, 512, 128
TOK = SEQ + DEC
NT = SEQ // 128 + 1
SAMPLE = NT - 1
HD = 64
CHUNK = 64
IDX_W = 4 * HD + HD + 4
NAT_W = 1536
CW = 512
GROUPS = [(0, 384), (384, 384), (768, 320)]
NEG_BIG = 1e30
TAKEN = -3.0e38
KSEL, KSEL_S = 256, (PAST + DEC) // 4
BIAS_L = 1151
EPS = 1e-6
SBUF0 = 16512


def rows_of(t):
    return DEC if t == SAMPLE else 128


def keys_of(t):
    return PAST + DEC if t == SAMPLE else 128 * (t + 1)


def keys_b(t):
    return WIN + DEC if t == SAMPLE else (128 if t == 0 else 256)


def build_program(nc, t):
    ctx = ExitStack()
    with ctx:
        def at(name, shape, dt, offset):
            return nc.alloc_sbuf_tensor_at(name, shape, dt, offset=SBUF0 + offset)

        def sem(name):
            return ctx.enter_context(nc.semaphore(name))

        PS = ctx.enter_context(nc.psum_tensor("PS", [128, 8, 512], F32))

        def bank(b):
            return PS[:, b, :]

        HH = at("HH", [128, KD, TOK], F32R, 0)
        HL = at("HL", [128, KD, TOK], F32R, 34816)
        WB = 69632
        WH = [at(f"WH{i}", [128, KD, CW], F32R, WB + 32768 * i) for i in range(2)]
        WL = [at(f"WL{i}", [128, KD, CW], F32R, WB + 32768 * i + 16384) for i in range(2)]
        RAW = at("RAW", [128, 4, CW], F32, WB + 65536)
        XB = WB + 65536 + 8192
        XT = at("XT", [128, KD, TOK], F32, XB)
        IQT = at("IQT", [128, 4, TOK], F32R, XB)
        IKT = at("IKT", [128, 2, SEQ], F32R, XB + 17408)
        IKTS = at("IKTS", [128, 2, PAST + DEC], F32R, XB + 25600)
        STG = at("STG", [128, 3, CW], F32, XB)
        ZS = at("ZS", [128, 2, 384], F32, XB + 6144)
        ZC = at("ZC", [128, 2, 384], F32, XB + 9216)
        MASK = at("MASK", [128, 5184], BF16, XB + 20480)
        SCB = XB + 34816
        SC = at("SC", [128, 4800], F32, SCB)
        SM = SCB + 19200
        XNAT = [at(f"XN{i}", [128, D], F32, WB + 4096 * i) for i in range(8)] + \
               [at("XN8", [128, D], F32, 61440)]
        WADA = [at(f"WADA{k}", [128, 3 * D], F32, 12288 * k) for k in range(5)] + \
               [at(f"WADA{k}", [128, 3 * D], F32, WB + 32768 + 12288 * (k - 5)) for k in (5, 6)] + \
               [at("WADA7", [128, 3 * D], F32, SCB)]
        ONEH = at("ONEH", [32, BIAS_L], F32, WB + 32768 + 24576)
        BV = at("BV", [16, BIAS_L], F32, SCB + 12288)
        SQJ = at("SQJ", [128, D], F32, 65536)
        off = [SM]

        def small(name, shape, dt=F32, size=None):
            n = 1
            for s in shape[1:]:
                n *= s
            n *= 2 if dt == BF16 else 4
            h = at(name, shape, dt, off[0])
            off[0] += (n + 31) // 32 * 32
            return h

        IDF = small("IDF", [128, 128])
        IDR = small("IDR", [128, 128], F32R)
        IDB = small("IDB", [128, 128], BF16)
        GAM = small("GAM", [128, 4, HD])
        SINK = small("SINK", [128, 8])
        NSINK = small("NSINK", [128, 8])
        CS = small("CS", [128, KD, 2])
        CG = small("CG", [128, KD, 2])
        CSIL = small("CSIL", [128, KD, 2])
        NG = small("NG", [128, KD])
        BADA = small("BADA", [128, 24])
        RELB = small("RELB", [32, 16])
        MOD = small("MOD", [128, 24, 2])
        SCL = small("SCL", [128, KD, 2])
        SS = small("SS", [128, 20])
        RV = small("RV", [128, 20])
        RI = small("RI", [128, 20], I32)
        RT = small("RT", [128, 20])
        RY = small("RY", [128, 20])
        IW = small("IW", [128, NT, 4])
        GROW = small("GROW", [16, 128])
        M8 = small("M8", [128, 2, 8])
        NM = small("NM", [128, 2, 8])
        DEN = small("DEN", [128, 2, 8])
        ES = small("ES", [128, 2, 8])
        SD = small("SD", [128, 8])
        IN2 = [at(f"IN{i}", [128, 6, 2, HD], F32R, off[0] + 3072 * i) for i in range(2)]
        NIDX = at("NIDX", [128, 2, IDX_W], F32, off[0] + 6144)
        CIK = at("CIK", [128, 4, HD], F32, off[0] + 6144 + 2624)
        assert SBUF0 + off[0] + 6144 + 2624 + 1024 <= 229344, off[0]
        BTA = at("BTA", [128, 8, 1024], F32, 0)
        BTB = at("BTB", [128, 8, 256], F32, 32768)
        KTA = at("KTA", [128, 2, 2, SEQ], F32R, 40960)
        KTAS = at("KTAS", [128, 2, 2, PAST + DEC], F32R, 57344)
        KTB = at("KTB", [128, 2, 2, SEQ], F32R, 66560)
        KTBS = at("KTBS", [128, 2, 2, WIN + DEC], F32R, 82944)
        VA = at("VA", [128, 8, 128], F32, 86016)
        VAS = at("VAS", [128, 5, 128], F32, 90112)
        VB = at("VB", [128, 8, 128], F32, 92672)
        VBS = at("VBS", [128, 2, 128], F32, 96768)
        QKV = at("QKV", [128, 2, NAT_W], F32, 97792)
        QS = at("QS", [128, 16, 2, HD], F32R, 110080)
        KS = at("KS", [128, 4, 4, HD], F32R, 118272)
        QT = [at(f"QT{i}", [128, 16, 128], F32R, 122368 + 8192 * i) for i in range(2)]
        ATTN = at("ATTN", [128, 2, 512], F32, 138752)
        XG = at("XG", [128, 20, HD], F32, XB)
        XNB = at("XNB", [128, 20, HD], F32, XB + 5120)
        LG = at("LG", [128, 2, 1024], F32, XB + 10240)
        PB = at("PB", [128, 2, 1024], F32, SCB)
        PT = at("PT", [128, 2, 1024], F32, SCB + 8192)
        KSC = at("KSC", [128, 2, 4, HD], F32R, SCB + 16384)
        ATS = at("ATS", [128, 2, 4, 128], F32, off[0])
        CK = at("CK", [128, 5, 128], F32, off[0] + 4096)
        ZH = at("ZH", [128, KD, TOK], F32R, 0)
        ZL = at("ZL", [128, KD, TOK], F32R, 34816)
        MH = at("MH", [128, KD, TOK], F32R, 69632)
        ML = at("ML", [128, KD, TOK], F32R, 104448)
        AST = at("AST", [128, 2, TOK], F32, 69632)
        ZST = at("ZST", [128, 2, TOK], F32, 69632 + 8704)
        OB = 139264
        WOH = at("WOH", [128, 2, KD, 128], F32R, OB)
        WOL = at("WOL", [128, 2, KD, 128], F32R, OB + 8192)
        ORAW = at("ORAW", [128, 2, KD, 128], F32, OB + 16384)
        GT = at("GT", [128, 3, 2, 384], F32, OB + 24576)
        TM = at("TM", [128, 2, 3, 384], F32, OB + 33792)
        GATE = at("GATE", [128, 2, D], F32, OB + 43008)
        YW = 256
        NYC = D // YW
        UH = [at("UH0", [128, KD, YW], F32R, OB + 16384)] + \
             [at(f"UH{i}", [128, KD, YW], F32R, 16384 * (i - 1)) for i in range(1, NYC)]
        UL = [at("UL0", [128, KD, YW], F32R, 49152)] + \
             [at(f"UL{i}", [128, KD, YW], F32R, 16384 * (i - 1) + 8192) for i in range(1, NYC)]
        URAW = [at(f"URAW{i}", [128, KD, YW], F32, OB + 8192 * i) for i in range(2)]
        XR = at("XR", [128, 3, YW], F32, 57344)
        YT = at("YT", [128, 3, YW], F32, 57344 + 3072)
        YO = at("YO", [128, 3, YW], F32, 57344 + 6144)

        snat = nc.dram_tensor("snat", [TOK, NAT_W], F32).ap()
        gz = nc.dram_tensor("gz", [3 * D, TOK], F32).ap()
        attd = nc.dram_tensor("attd", [D, TOK], F32).ap()
        btad = nc.dram_tensor("btad", [128, 8, 1024], F32).ap()
        btbd = nc.dram_tensor("btbd", [128, 8, 256], F32).ap()
        bvd = nc.dram_tensor("bvd", [16, BIAS_L], F32).ap()
        gated = nc.dram_tensor("gated", [2 * KD, 128], F32).ap()

        consts_in = sem("consts_in")
        x_in = [sem(f"x_in{i}") for i in range(NT)]
        wada_in = [sem(f"wada_in{k}") for k in range(KD)]
        raw_in = [sem(f"raw_in{i}") for i in range(4)]
        ident_ready = sem("ident_ready")
        c_sig = sem("c_sig")
        c_ready = sem("c_ready")
        dve_step = sem("dve_step")
        xn_ready = sem("xn_ready")
        xt_pe = sem("xt_pe")
        xt_evac = sem("xt_evac")
        ada_done = sem("ada_done")
        bias_pe = sem("bias_pe")
        bias_sb = sem("bias_sb")
        mod_ready = sem("mod_ready")
        gate_pe = sem("gate_pe")
        gate_rows = sem("gate_rows")
        scratch_out = sem("scratch_out")
        bias_out = sem("bias_out")
        h_ready = sem("h_ready")
        hh_done = sem("hh_done")
        hl_done = sem("hl_done")
        hi_done = sem("hi_done")
        lo_done = sem("lo_done")
        idx_pe = sem("idx_pe")
        idx_evac = sem("idx_evac")
        idx_hi = sem("idx_hi")
        idx_lo = sem("idx_lo")
        idx_t = sem("idx_t")
        idx_tev = sem("idx_tev")
        ik_out = [sem(f"ik_out{i}") for i in range(2)]
        score_pe = sem("score_pe")
        relu_done = sem("relu_done")
        acc_done = sem("acc_done")
        sel_step = sem("sel_step")
        mask_done = sem("mask_done")
        piece_pe = sem("piece_pe")
        piece_ev = sem("piece_ev")
        z_pool = sem("z_pool")
        stg_out = [sem(f"stg_out{i}") for i in range(3)]
        kv_in = sem("kv_in")
        qkv_in = [sem(f"qkv_in{i}") for i in range(2)]
        sq_done = sem("sq_done")
        xg_ready = sem("xg_ready")
        xn4_ready = sem("xn4_ready")
        qs_hi = sem("qs_hi")
        qs_lo = sem("qs_lo")
        k_out = sem("k_out")
        copy_out = sem("copy_out")
        cache_hi = sem("cache_hi")
        cache_lo = sem("cache_lo")
        qk_pe = sem("qk_pe")
        min_done = sem("min_done")
        exp_done = sem("exp_done")
        tr_pe = sem("tr_pe")
        tev_dve = sem("tev_dve")
        tev_act = sem("tev_act")
        pv_pe = sem("pv_pe")
        sink_sum = sem("sink_sum")
        sink_act = sem("sink_act")
        att_done = sem("att_done")
        att_out = [sem(f"att_out{i}") for i in range(2)]
        az_in = [sem(f"az_in{i}") for i in range(2)]
        az_mul = sem("az_mul")
        az_hi = sem("az_hi")
        az_lo = sem("az_lo")
        oraw_in = [sem(f"oraw_in{i}") for i in range(2)]
        ow_hi = sem("ow_hi")
        ow_lo = sem("ow_lo")
        g_in = [sem(f"g_in{i}") for i in range(3)]
        o_pe = sem("o_pe")
        m_dve = sem("m_dve")
        m_hi = sem("m_hi")
        m_lo = sem("m_lo")
        gate_in = sem("gate_in")
        uraw_in = [sem(f"uraw_in{i}") for i in range(2)]
        u_hi = sem("u_hi")
        u_lo = sem("u_lo")
        xr_in = [sem(f"xr_in{i}") for i in range(3)]
        y_pe = sem("y_pe")
        y_mul = sem("y_mul")
        y_add = sem("y_add")
        y_out = [sem(f"y_out{i}") for i in range(3)]

        SOFF = {}
        o = 0
        for tt in range(2, NT):
            SOFF[tt] = o
            o += keys_of(tt)
        MOFF = {}
        o = 0
        for tt in range(NT):
            MOFF[tt] = o
            o += keys_of(tt)

        def tcols(tt):
            return slice(128 * tt, 128 * tt + rows_of(tt))

        CHUNKS = [("idx", 0, IDX_W)]
        CHUNKS += [("nat", IDX_W + CW * i, CW) for i in range(NAT_W // CW)]
        CHUNKS += [("z", IDX_W + NAT_W + CW * i, CW) for i in range(2)]
        CHUNKS += [("g", IDX_W + NAT_W + D + CW * i, CW) for i in range(4)]
        NCH = len(CHUNKS)
        PIECES = []
        for c in range(1, NCH):
            if CHUNKS[c][0] == "nat":
                PIECES += [(c, j, ("nat", j)) for j in range(NT)]
            else:
                PIECES += [(c, j, (CHUNKS[c][0], j // 3, j % 3)) for j in range(12)]
        NP = len(PIECES)
        PEND = [len([1 for c, _, _ in PIECES if c <= e]) for e in range(NCH)]
        ZP = [p for p, (c, j, w) in enumerate(PIECES) if w[0] == "z"]
        NST = [len([p for p in range(len(PIECES)) if p % 3 == i]) for i in range(3)]

        ITEMS = NT + PAST // 128
        SCORED = [tt for tt in range(2, NT)]
        SHEADS = [(tt, h) for tt in SCORED for h in range(4)]

        UNITS = [(tt, br, h) for tt in range(NT) for br in range(2) for h in range(8)]
        NU = len(UNITS)

        def unit_keys(u):
            tt, br, _ = UNITS[u]
            return keys_b(tt) if br else keys_of(tt)

        S0, S1 = -17, NU + 8
        TP = {s: [] for s in range(S0, S1)}
        for s in range(S0, S1):
            if 0 <= s - 1 < NU:
                for j in range((unit_keys(s - 1) + 511) // 512):
                    TP[s].append(("P", s - 1, j))
        for tt in range(NT):
            base = 16 * (tt - 1)
            for j in range(4):
                TP[base + 8 + j].append(("Q", tt, j))
            for j in range(2):
                TP[base + 12 + j].append(("K", tt, j))
        for i in range(5):
            TP[16 * (2 + i) + 6].append(("C", i, 0))
        for g in range(2 * NT):
            TP[8 * g + 7 + 2 + 3].append(("A", g // 2, g % 2))
        TQ = [(s, x) for s in range(S0, S1) for x in TP[s]]
        TIDX = {x: q for q, (_, x) in enumerate(TQ)}
        PREP0 = {16 * (tt - 1): tt for tt in range(NT)}
        CACHE_STEP = {16 * (2 + i) + 3: i for i in range(5)}

        def prep(s, after):
            return PREP0.get(s - after)

        def k_stores(tt):
            return tt + 1 + (tt >= SAMPLE - 1) + (tt >= SAMPLE)

        def last_t(u):
            return TIDX[("P", u, (unit_keys(u) + 511) // 512 - 1)]

        def t_evac(eng, copy, x, done):
            q = TIDX[x]
            eng.wait_ge(tr_pe, q + 1)
            src = bank(4 + q % 2).rearrange("p (b n) -> p b n", b=4)
            if x[0] == "P":
                u, j = x[1], x[2]
                r, nk = rows_of(UNITS[u][0]), unit_keys(u) - 512 * j
                full, part = min(4, nk // 128), nk % 128 if nk < 512 else 0
                dst = PT[:, u % 2, 512 * j:512 * (j + 1)].rearrange("p (b n) -> p b n", b=4)
                if u >= 2:
                    eng.wait_ge(pv_pe, u - 1)
                if full:
                    last = copy(dst[:, 0:full, 0:r], src[:, 0:full, 0:r])
                if part:
                    last = copy(dst[0:part, full, 0:r], src[0:part, full, 0:r])
            elif x[0] == "Q":
                if x[1] >= 2:
                    eng.wait_ge(qk_pe, 16 * (x[1] - 1))
                r = rows_of(x[1])
                last = copy(QT[x[1] % 2][:, 4 * x[2]:4 * x[2] + 4, 0:r], src[:, :, 0:r])
            elif x[0] == "A":
                g, r = 2 * x[1] + x[2], rows_of(x[1])
                if g >= 2:
                    eng.wait_ge(att_out[g % 2], 16 * (g // 2))
                last = copy(ATS[:, g % 2, :, 0:r], src[:, :, 0:r])
            else:
                if x[0] == "C":
                    dst = KTAS[:, :, :, 128 * x[1]:128 * (x[1] + 1)] if x[1] < 4 else KTBS[:, :, :, 0:WIN]
                elif x[1] == SAMPLE:
                    dst = KTBS[:, :, :, WIN:WIN + DEC] if x[2] else KTAS[:, :, :, PAST:PAST + DEC]
                else:
                    dst = (KTB if x[2] else KTA)[:, :, :, tcols(x[1])]
                r = rows_of(x[1]) if x[0] == "K" else 128
                last = copy(dst, bank(4 + q % 2).rearrange("p (a b n) -> p a b n", a=2, b=2)[:, :, :, 0:r])
            last.then_inc(done, 1)

        def rsqrt_chain(dve, link, out, ss, n, r, scale):
            v, i, tmp = RV[0:r, 0:n], RI[0:r, 0:n], RT[0:r, 0:n]
            link(nc.vector.tensor_scalar(v, ss, scale, EPS, ALU.mult, ALU.add))
            link(nc.vector.tensor_scalar(i, v.bitcast(I32), 1, None, ALU.arith_shift_right))
            link(nc.vector.tensor_scalar(i, i, -1.0, float(0x5F3759DF), ALU.mult, ALU.add))
            y = i.bitcast(F32)
            for step in range(3):
                link(nc.vector.tensor_tensor(tmp, y, y, ALU.mult))
                link(nc.vector.tensor_tensor(tmp, tmp, v, ALU.mult))
                link(nc.vector.tensor_scalar(tmp, tmp, -0.5, 1.5, ALU.mult, ALU.add))
                link(nc.vector.tensor_tensor(out, y, tmp, ALU.mult))
                y = out

        w_all_v = t["w_all"].rearrange("(k p) n -> p k n", p=128)
        N_SMALL = 12
        block = ctx.enter_context(nc.Block())

        @block.sync
        def _(sp):
            def raw_load(n):
                c, k = n // KD, n % KD
                if c >= NCH:
                    return
                if n >= 4:
                    sp.wait_ge(lo_done, n - 3)
                _, c0, cw = CHUNKS[c]
                sp.dma_start(RAW[:, n % 4, 0:cw], w_all_v[:, k, c0:c0 + cw]).then_inc(raw_in[n % 4], 16)

            for dst, src in ((CS[:], t["c_cols"]), (IDF[:], t["ident"]), (NG[:], t["ng_cols"]),
                             (BADA[:], t["bada_cols"]), (RELB[:], t["rel_bias"]), (ONEH[:], t["onehot"]),
                             (GAM[:], t["gammas"]), (SINK[:], t["sinks"])):
                sp.dma_start(dst, src).then_inc(consts_in, 16)
            for i in range(4):
                sp.dma_start(CIK[:, i, :], t["cache_ik"][128 * i:128 * (i + 1), :]).then_inc(consts_in, 16)
            for tt in range(NT):
                r = rows_of(tt)
                src = t["x_sample"] if tt == SAMPLE else t["x_prompt"][tcols(tt), :]
                sp.dma_start(XNAT[tt][0:r, :], src).then_inc(x_in[tt], 16)
            for k in range(KD):
                sp.dma_start(WADA[k][:], t["w_ada"][128 * k:128 * (k + 1), :]).then_inc(wada_in[k], 16)
            for n in range(4):
                raw_load(n)
            sp.wait_ge(bias_sb, 3)
            sp.dma_start(bvd, BV[:, :]).then_inc(scratch_out, 16)
            for n in range(4, 12):
                raw_load(n)
            sp.wait_ge(gate_rows, 1)
            sp.dma_start(gated, GROW[:]).then_inc(scratch_out, 16)
            sp.wait_ge(scratch_out, 32)
            sp.dma_start(btad.rearrange("p h j -> h p j"), bass.AP(bvd.tensor, 127, [[BIAS_L, 8], [-1, 128], [1, 1024]])).then_inc(bias_out, 16)
            sp.dma_start(btbd.rearrange("p h j -> h p j"), bass.AP(bvd.tensor, 8 * BIAS_L + 895, [[BIAS_L, 8], [-1, 128], [1, 256]])).then_inc(bias_out, 16)
            for i in range(ITEMS):
                if i < NT:
                    r = rows_of(i)
                    sp.wait_ge(idx_evac, i + 1)
                    dst = t["sa_ik"] if i == SAMPLE else t["pa_ik"][tcols(i), :]
                    sp.dma_start(dst, NIDX[0:r, i % 2, 256:320]).then_inc(ik_out[i % 2], 16)
                if 1 <= i <= KD:
                    raw_load(KD + i - 1 + 4)
            for p, (c, j, w) in enumerate(PIECES):
                if w[0] == "z":
                    sp.wait_ge(z_pool, ZP.index(p) + 1)
                else:
                    sp.wait_ge(piece_ev, p + 1)
                if w[0] == "nat":
                    r = rows_of(j)
                    sp.dma_start(snat[tcols(j), CW * (c - 1):CW * c], STG[0:r, p % 3, :]).then_inc(stg_out[p % 3], 16)
                else:
                    b = 4 * (c - 4) + w[1]
                    g0, gn = GROUPS[w[2]]
                    sp.dma_start(gz[128 * b:128 * (b + 1), g0:g0 + gn], STG[:, p % 3, 0:gn]).then_inc(stg_out[p % 3], 16)
                if j < KD:
                    raw_load(KD * (c + 1) + j + 4)
            for i in range(3):
                sp.wait_ge(stg_out[i], 16 * NST[i])
            sp.wait_ge(bias_out, 32)
            sp.wait_ge(piece_pe, NP)
            sp.wait_ge(mask_done, NT)
            vp = snat[0:SEQ, :].rearrange("(n p) c -> p n c", p=128)
            sp.dma_start(BTA[:], btad).then_inc(kv_in, 16)
            sp.dma_start(BTB[:], btbd).then_inc(kv_in, 16)
            sp.dma_start(VA[:], vp[:, :, 640:768]).then_inc(kv_in, 16)
            sp.dma_start(VB[:], vp[:, :, 1408:1536]).then_inc(kv_in, 16)
            sp.dma_start(VAS[:, 0:4, :], t["cache_av"].rearrange("(n p) c -> p n c", p=128)).then_inc(kv_in, 16)
            sp.dma_start(VAS[0:DEC, 4, :], snat[SEQ:TOK, 640:768]).then_inc(kv_in, 16)
            sp.dma_start(VBS[:, 0, :], t["cache_bv"]).then_inc(kv_in, 16)
            sp.dma_start(VBS[0:DEC, 1, :], snat[SEQ:TOK, 1408:1536]).then_inc(kv_in, 16)
            sp.dma_start(CK[:, 0:4, :], t["cache_ak"].rearrange("(n p) c -> p n c", p=128)).then_inc(kv_in, 16)
            sp.dma_start(CK[:, 4, :], t["cache_bk"]).then_inc(kv_in, 16)
            for dst, src in ((t["pa_v"], snat[0:SEQ, 640:768]), (t["sa_v"], snat[SEQ:TOK, 640:768]),
                             (t["pb_v"], snat[SEQ - WIN:SEQ, 1408:1536]),
                             (t["sb_v"][0:WIN - DEC, :], t["cache_bv"][DEC:WIN, :]),
                             (t["sb_v"][WIN - DEC:WIN, :], snat[SEQ:TOK, 1408:1536]),
                             (t["sb_k"][0:WIN - DEC, :], t["cache_bk"][DEC:WIN, :])):
                sp.dma_start(dst, src).then_inc(copy_out, 16)
            n_copy = 6
            for s in range(S0, S1):
                tt = prep(s, -1)
                if tt is not None:
                    if tt >= 2:
                        sp.wait_ge(xg_ready, tt - 1)
                        sp.wait_ge(sq_done, tt - 1)
                    sp.dma_start(QKV[0:rows_of(tt), tt % 2, :], snat[tcols(tt), :]).then_inc(qkv_in[tt % 2], 16)
                tt = prep(s, 5)
                if tt is not None:
                    r = rows_of(tt)
                    sp.wait_ge(xn4_ready, tt + 1)
                    dst = t["sa_k"] if tt == SAMPLE else t["pa_k"][tcols(tt), :]
                    sp.dma_start(dst, XNB[0:r, 8:10, :]).then_inc(k_out, 16)
                    if tt == SAMPLE:
                        sp.dma_start(t["sb_k"][WIN - DEC:WIN, :], XNB[0:r, 18:20, :]).then_inc(k_out, 16)
                    if tt == SAMPLE - 1:
                        sp.dma_start(t["pb_k"], XNB[0:r, 18:20, :]).then_inc(k_out, 16)
                for x in TP.get(s - 1, []):
                    if x[0] == "A":
                        q = TIDX[x]
                        tt, br = x[1], x[2]
                        g = 2 * tt + br
                        sp.wait_ge(tev_dve if q % 2 == 0 else tev_act, q // 2 + 1)
                        sp.dma_start(attd[512 * br:512 * (br + 1), tcols(tt)].rearrange("(b p) n -> p b n", p=128),
                                     ATS[:, g % 2, :, 0:rows_of(tt)]).then_inc(att_out[g % 2], 16)
            sp.wait_ge(pv_pe, NU)
            for i in range(2):
                sp.wait_ge(att_out[i], 16 * NT)
            def o_load(j):
                if j >= KD:
                    return
                if j >= 2:
                    sp.wait_ge(ow_lo, j - 1)
                sp.dma_start(ORAW[:, j % 2, :, :], t["w_o"].rearrange("(k p) n -> p k n", p=128)[:, :, 128 * j:128 * (j + 1)]).then_inc(oraw_in[j % 2], 16)

            for j in range(2):
                o_load(j)
            for k in range(KD):
                if k >= 2:
                    sp.wait_ge(az_lo, k - 1)
                sp.dma_start(AST[:, k % 2, :], attd[128 * k:128 * (k + 1), :]).then_inc(az_in[k % 2], 16)
                sp.dma_start(ZST[:, k % 2, :], gz[128 * k:128 * (k + 1), :]).then_inc(az_in[k % 2], 16)
            for j in range(2):
                sp.dma_start(GATE[:, j, :], bass.AP(gated.tensor, 128 * j, [[0, 128], [256, KD], [1, 128]])).then_inc(gate_in, 16)

            for i in range(3 * KD):
                j, g = i // 3, i % 3
                if i >= 3:
                    sp.wait_ge(m_dve, i - 2)
                g0, gn = GROUPS[g]
                for b in range(2):
                    sp.dma_start(GT[:, i % 3, b, 0:gn], gz[D * (1 + b) + 128 * j:D * (1 + b) + 128 * (j + 1), g0:g0 + gn]).then_inc(g_in[i % 3], 16)
                if g == 2:
                    o_load(j + 2)
            sp.wait_ge(o_pe, 3 * KD)
            wout_v = t["w_out"].rearrange("(k p) n -> p k n", p=128)
            for c in range(2):
                sp.dma_start(URAW[c][:], wout_v[:, :, YW * c:YW * (c + 1)]).then_inc(uraw_in[c], 16)

            def x_load(i):
                if i >= NYC * NT:
                    return
                c, tt = i // NT, i % NT
                if i >= 3:
                    sp.wait_ge(y_add, i - 2)
                src = t["x_sample"] if tt == SAMPLE else t["x_prompt"][tcols(tt), :]
                sp.dma_start(XR[0:rows_of(tt), i % 3, :], src[:, YW * c:YW * (c + 1)]).then_inc(xr_in[i % 3], 16)

            for i in range(3):
                x_load(i)
            for i in range(NYC * NT):
                c, tt = i // NT, i % NT
                if tt == 0 and 1 <= c and c + 1 < NYC:
                    sp.wait_ge(u_lo, KD * c)
                    sp.dma_start(URAW[(c + 1) % 2][:], wout_v[:, :, YW * (c + 1):YW * (c + 2)]).then_inc(uraw_in[(c + 1) % 2], 16)
                x_load(i + 3)
                sp.wait_ge(y_add, i + 1)
                dst = t["y_sample"] if tt == SAMPLE else t["y_prompt"][tcols(tt), :]
                sp.dma_start(dst[:, YW * c:YW * (c + 1)], YO[0:rows_of(tt), i % 3, :]).then_inc(y_out[i % 3], 16)
            for i in range(3):
                sp.wait_ge(y_out[i], 16 * NYC * NT // 3)
            sp.wait_ge(ik_out[0], 16 * 5)
            sp.wait_ge(ik_out[1], 16 * 4)
            sp.wait_ge(copy_out, 16 * n_copy)
            sp.wait_ge(k_out, 16 * k_stores(SAMPLE))

        def u_low(pool, c):
            for k in range(KD):
                pool.wait_ge(u_hi, KD * c + k + 1)
                nc.gpsimd.tensor_tensor(UL[c][:, k, :], URAW[c % 2][:, k, :], UH[c][:, k, :].bitcast(F32), ALU.subtract).then_inc(u_lo, 1)

        @block.gpsimd
        def _(pool):
            def w_lo(n):
                c, k = n // KD, n % KD
                if c >= NCH:
                    return
                cw = CHUNKS[c][2]
                pool.wait_ge(hi_done, n + 1)
                nc.gpsimd.tensor_tensor(WL[c % 2][:, k, 0:cw], RAW[:, n % 4, 0:cw],
                                        WH[c % 2][:, k, 0:cw].bitcast(F32), ALU.subtract).then_inc(lo_done, 1)

            for n in range(KD):
                w_lo(n)
            for i in range(ITEMS):
                slot = IN2[i % 2]
                r = rows_of(i) if i < NT else 128
                pool.wait_ge(idx_hi, i + 1)
                if i < NT:
                    nc.gpsimd.tensor_tensor(slot[0:r, 0:4, 1, :], NIDX[0:r, i % 2, 0:256].rearrange("p (h d) -> p h d", h=4),
                                            slot[0:r, 0:4, 0, :].bitcast(F32), ALU.subtract)
                    k_nat = NIDX[0:r, i % 2, 256:320]
                else:
                    k_nat = CIK[:, i - NT, :]
                for b in range(2):
                    last = nc.gpsimd.tensor_tensor(slot[0:r, 5, b, :], k_nat, slot[0:r, 4, 0, :].bitcast(F32), ALU.subtract)
                last.then_inc(idx_lo, 1)
                if 1 <= i <= KD:
                    w_lo(KD + i - 1)
            for p, (c, j, w) in enumerate(PIECES):
                if w[0] == "z":
                    z = ZP.index(p)
                    gn = GROUPS[w[2]][1]
                    pool.wait_ge(piece_ev, p + 1)
                    if p >= 3:
                        pool.wait_ge(stg_out[p % 3], 16 * (p // 3))
                    nc.gpsimd.tensor_tensor(STG[:, p % 3, 0:gn], ZS[:, z % 2, 0:gn], ZC[:, z % 2, 0:gn], ALU.mult).then_inc(z_pool, 1)
                if j < KD:
                    w_lo(KD * (c + 1) + j)
            pool.wait_ge(piece_pe, NP)
            pool.wait_ge(mask_done, NT)
            for s in range(S0, S1):
                tt = prep(s, 1)
                if tt is not None:
                    r = rows_of(tt)
                    q = QKV[0:r, tt % 2, :]
                    pool.wait_ge(qkv_in[tt % 2], 16 * (tt // 2 + 1))
                    if tt >= 1:
                        pool.wait_ge(xn4_ready, tt)
                    for g, (c0, h0, n) in enumerate(((0, 0, 8), (512, 8, 2), (768, 10, 8), (1280, 18, 2))):
                        last = nc.gpsimd.tensor_tensor(
                            XG[0:r, h0:h0 + n, :], q[:, c0:c0 + 64 * n].rearrange("p (h d) -> p h d", h=n),
                            GAM[0:r, g:g + 1, :].broadcast_to([r, n, HD]), ALU.mult)
                    last.then_inc(xg_ready, 1)
                tt = prep(s, 5)
                if tt is not None:
                    r = rows_of(tt)
                    pool.wait_ge(qs_hi, tt + 1)
                    for br in range(2):
                        nc.gpsimd.tensor_tensor(QS[0:r, 8 * br:8 * br + 8, 1, :], XNB[0:r, 10 * br:10 * br + 8, :],
                                                QS[0:r, 8 * br:8 * br + 8, 0, :].bitcast(F32), ALU.subtract)
                    for b in range(2):
                        for br in range(2):
                            last = nc.gpsimd.tensor_tensor(KS[0:r, 2 * br:2 * br + 2, 2 + b, :], XNB[0:r, 10 * br + 8:10 * br + 10, :],
                                                           KS[0:r, 2 * br:2 * br + 2, 0, :].bitcast(F32), ALU.subtract)
                    last.then_inc(qs_lo, 1)
                if s in CACHE_STEP:
                    i = CACHE_STEP[s]
                    pool.wait_ge(cache_hi, i + 1)
                    for b in range(2):
                        last = nc.gpsimd.tensor_tensor(KSC[:, :, 2 + b, :], CK[:, i, :].rearrange("p (h d) -> p h d", h=2),
                                                       KSC[:, :, 0, :].bitcast(F32), ALU.subtract)
                    last.then_inc(cache_lo, 1)
            for j in range(2):
                pool.wait_ge(ow_hi, j + 1)
                nc.gpsimd.tensor_tensor(WOL[:, j % 2, :, :], ORAW[:, j % 2, :, :], WOH[:, j % 2, :, :].bitcast(F32), ALU.subtract).then_inc(ow_lo, 1)
            for i in range(3 * KD):
                j, g = i // 3, i % 3
                g0, gn = GROUPS[g]
                pool.wait_ge(m_hi, i + 1)
                nc.gpsimd.tensor_tensor(ML[:, j, g0:g0 + gn], TM[:, i % 2, 2, 0:gn], MH[:, j, g0:g0 + gn].bitcast(F32), ALU.subtract).then_inc(m_lo, 1)
                if g == 2 and j + 2 < KD:
                    pool.wait_ge(ow_hi, j + 3)
                    nc.gpsimd.tensor_tensor(WOL[:, j % 2, :, :], ORAW[:, j % 2, :, :], WOH[:, j % 2, :, :].bitcast(F32), ALU.subtract).then_inc(ow_lo, 1)
            for i in range(NYC * NT):
                c, tt = i // NT, i % NT
                if i == 0:
                    u_low(pool, 0)
                if tt == 0 and c + 1 < NYC:
                    u_low(pool, c + 1)
                r = rows_of(tt)
                pool.wait_ge(y_mul, i + 1)
                pool.wait_ge(xr_in[i % 3], 16 * (i // 3 + 1))
                if i >= 3:
                    pool.wait_ge(y_out[i % 3], 16 * (i // 3))
                nc.gpsimd.tensor_tensor(YO[0:r, i % 3, :], YT[0:r, i % 3, :], XR[0:r, i % 3, :], ALU.add).then_inc(y_add, 1)

        @block.scalar
        def _(act):
            def w_hi(n):
                c, k = n // KD, n % KD
                if c >= NCH:
                    return
                cw = CHUNKS[c][2]
                act.wait_ge(raw_in[n % 4], 16 * (n // 4 + 1))
                if k == 0 and c == 2:
                    act.wait_ge(idx_pe, NT)
                if k == 0 and c >= 3:
                    act.wait_ge(piece_pe, PEND[c - 2])
                nc.scalar.activation(WH[c % 2][:, k, 0:cw], RAW[:, n % 4, 0:cw], ACT.Copy).then_inc(hi_done, 1)

            act.wait_ge(consts_in, 16 * N_SMALL)
            nc.scalar.activation(CG[:], CS[:], ACT.Sigmoid).then_inc(c_sig, 1)
            for q in range(2 * NT):
                tt, half = q // 2, q % 2
                r = rows_of(tt)
                act.wait_ge(xt_pe, q + 1)
                nc.scalar.activation(XT[:, 4 * half:4 * half + 4, tcols(tt)],
                                     bank(q % 4).rearrange("p (k n) -> p k n", k=4)[:, :, 0:r], ACT.Copy).then_inc(xt_evac, 1)
            for n in range(KD):
                w_hi(n)
            for k in range(KD):
                act.wait_ge(h_ready, k + 1)
                nc.scalar.activation(HH[:, k, :], XT[:, k, :], ACT.Copy).then_inc(hh_done, 1)
            def relus(tt):
                for h in range(4):
                    n = SHEADS.index((tt, h))
                    r, nk = rows_of(tt), keys_of(tt)
                    act.wait_ge(score_pe, n + 1)
                    v = PS[0:r, 4 + 2 * (n % 2):6 + 2 * (n % 2), :].rearrange("p b n -> p (b n)")[:, 0:nk]
                    nc.scalar.activation(v, v, ACT.Relu, scale=HD ** -0.5 * 0.5).then_inc(relu_done, 1)

            for i in range(ITEMS + 1):
                if i < NT:
                    r = rows_of(i)
                    act.wait_ge(idx_pe, i + 1)
                    if i >= 2:
                        act.wait_ge(ik_out[i % 2], 16 * (i // 2))
                        act.wait_ge(idx_lo, i - 1)
                    nc.scalar.activation(NIDX[0:r, i % 2, :], bank(i % 2)[0:r, 0:IDX_W], ACT.Copy).then_inc(idx_evac, 1)
                if 1 <= i <= KD:
                    w_hi(KD + i - 1)
                if i >= 1:
                    j = i - 1
                    r = rows_of(j) if j < NT else 128
                    act.wait_ge(idx_t, j + 1)
                    if j < NT:
                        nc.scalar.activation(IQT[:, :, tcols(j)], bank(2).rearrange("p (h n) -> p h n", h=4)[:, :, 0:r], ACT.Copy)
                    if j < SAMPLE:
                        dst = IKT[:, :, tcols(j)]
                    elif j == SAMPLE:
                        dst = IKTS[:, :, PAST:PAST + DEC]
                    else:
                        dst = IKTS[:, :, 128 * (j - NT):128 * (j - NT + 1)]
                    nc.scalar.activation(dst, bank(3)[:, 0:256].rearrange("p (h n) -> p h n", h=2)[:, :, 0:r], ACT.Copy).then_inc(idx_tev, 1)
                    if 2 <= j < SAMPLE:
                        relus(j)
            relus(SAMPLE)
            for p, (c, j, w) in enumerate(PIECES):
                act.wait_ge(piece_pe, p + 1)
                if w[0] != "z" and p >= 3:
                    act.wait_ge(stg_out[p % 3], 16 * (p // 3))
                if w[0] == "nat":
                    r = rows_of(j)
                    nc.scalar.activation(STG[0:r, p % 3, :], bank(p % 4)[0:r, :], ACT.Copy).then_inc(piece_ev, 1)
                else:
                    gn = GROUPS[w[2]][1]
                    if w[0] == "g":
                        nc.scalar.activation(STG[:, p % 3, 0:gn], bank(p % 4)[:, 0:gn], ACT.Sigmoid).then_inc(piece_ev, 1)
                    else:
                        z = ZP.index(p)
                        if z >= 2:
                            act.wait_ge(z_pool, z - 1)
                        nc.scalar.activation(ZS[:, z % 2, 0:gn], bank(p % 4)[:, 0:gn], ACT.Sigmoid)
                        nc.scalar.activation(ZC[:, z % 2, 0:gn], bank(p % 4)[:, 0:gn], ACT.Copy).then_inc(piece_ev, 1)
                if j < KD:
                    w_hi(KD * (c + 1) + j)
            act.wait_ge(kv_in, 160)
            act.wait_ge(piece_pe, NP)
            act.wait_ge(mask_done, NT)
            for s in range(S0, S1):
                if 0 <= s < NU:
                    u = s
                    tt, br, h = UNITS[u]
                    r, nk = rows_of(tt), unit_keys(u)
                    act.wait_ge(min_done, u + 1)
                    if u >= 2:
                        act.wait_ge(tr_pe, last_t(u - 2) + 1)
                    nc.scalar.activation(PB[0:r, u % 2, 0:nk], LG[0:r, u % 2, 0:nk], ACT.Exp, scale=-1.0,
                                         bias=NM[0:r, br, h:h + 1], accum_out=DEN[0:r, br, h:h + 1]).then_inc(exp_done, 1)
                if s % 16 == 0 and 16 <= s <= NU:
                    g = s // 16 - 1
                    act.wait_ge(sink_sum, g + 1)
                    nc.scalar.activation(ES[0:rows_of(g), 0, :], SD[0:rows_of(g), :], ACT.Exp).then_inc(sink_act, 1)
                tt = prep(s, 5)
                if tt is not None:
                    r = rows_of(tt)
                    act.wait_ge(xn4_ready, tt + 1)
                    if tt >= 1:
                        act.wait_ge(tr_pe, TIDX[("K", tt - 1, 1)] + 1)
                        act.wait_ge(qs_lo, tt)
                    for b in range(2):
                        nc.scalar.activation(QS[0:r, 8 * b:8 * b + 8, 0, :], XNB[0:r, 10 * b:10 * b + 8, :], ACT.Copy)
                        for d in range(2):
                            last = nc.scalar.activation(KS[0:r, 2 * b:2 * b + 2, d, :], XNB[0:r, 10 * b + 8:10 * b + 10, :], ACT.Copy)
                    last.then_inc(qs_hi, 1)
                if s in CACHE_STEP:
                    i = CACHE_STEP[s]
                    if i >= 1:
                        act.wait_ge(tr_pe, TIDX[("C", i - 1, 0)] + 1)
                    for d in range(2):
                        last = nc.scalar.activation(KSC[:, :, d, :], CK[:, i, :].rearrange("p (h d) -> p h d", h=2), ACT.Copy)
                    last.then_inc(cache_hi, 1)
                for x in TP[s]:
                    if TIDX[x] % 2 == 1:
                        t_evac(act, nc.scalar.copy, x, tev_act)
            for j in range(2):
                act.wait_ge(oraw_in[j], 16)
                nc.scalar.activation(WOH[:, j, :, :], ORAW[:, j, :, :], ACT.Copy).then_inc(ow_hi, 1)
            for k in range(KD):
                act.wait_ge(az_mul, k + 1)
                nc.scalar.activation(ZH[:, k, :], AST[:, k % 2, :], ACT.Copy).then_inc(az_hi, 1)
            for i in range(3 * KD):
                j, g = i // 3, i % 3
                g0, gn = GROUPS[g]
                act.wait_ge(m_dve, i + 1)
                nc.scalar.activation(MH[:, j, g0:g0 + gn], TM[:, i % 2, 2, 0:gn], ACT.Copy).then_inc(m_hi, 1)
                if g == 2 and j + 2 < KD:
                    act.wait_ge(oraw_in[j % 2], 16 * (j // 2 + 2))
                    act.wait_ge(o_pe, i + 1)
                    nc.scalar.activation(WOH[:, j % 2, :, :], ORAW[:, j % 2, :, :], ACT.Copy).then_inc(ow_hi, 1)
            for c in range(NYC):
                act.wait_ge(uraw_in[c % 2], 16 * (c // 2 + 1))
                for k in range(KD):
                    nc.scalar.activation(UH[c][:, k, :], URAW[c % 2][:, k, :], ACT.Copy).then_inc(u_hi, 1)

        @block.vector
        def _(dve):
            V = nc.vector
            steps = [0]

            def link(ins):
                steps[0] += 1
                ins.then_inc(dve_step, 1)
                dve.wait_ge(dve_step, steps[0])

            dve.wait_ge(consts_in, 16 * N_SMALL)
            V.tensor_copy(IDR[:], IDF[:])
            V.tensor_copy(IDB[:], IDF[:]).then_inc(ident_ready, 1)
            V.tensor_scalar(NSINK[:], SINK[:], -1.0, None, ALU.mult)
            dve.wait_ge(c_sig, 1)
            V.tensor_tensor(CSIL[:], CS[:], CG[:], ALU.mult).then_inc(c_ready, 1)
            link(V.memset(SS[:], 1.0))
            for i in range(3):
                n = min(512, BIAS_L - 512 * i)
                dve.wait_ge(bias_pe, i + 1)
                V.tensor_scalar(BV[:, 512 * i:512 * i + n], bank(5 + i)[0:16, 0:n], -1.0, None, ALU.mult).then_inc(bias_sb, 1)
            for a, b in ((0, 4), (4, NT)):
                for tt in range(a, b):
                    r = rows_of(tt)
                    dve.wait_ge(x_in[tt], 16)
                    link(V.tensor_tensor_reduce(out=SQJ[0:r, :], in0=XNAT[tt][0:r, :], in1=XNAT[tt][0:r, :], scale=1.0,
                                                scalar=0.0, op0=ALU.mult, op1=ALU.add, accum_out=SS[0:r, tt:tt + 1]))
                rsqrt_chain(dve, link, RY[:, a:b], SS[:, a:b], b - a, 128, 1.0 / D)
                for tt in range(a, b):
                    r = rows_of(tt)
                    V.tensor_scalar(XNAT[tt][0:r, :], XNAT[tt][0:r, :], RY[0:r, tt:tt + 1], None, ALU.mult).then_inc(xn_ready, 1)
            dve.wait_ge(ada_done, 1)
            V.tensor_tensor(MOD[:], bank(4)[:, 0:48].rearrange("p (c j) -> p c j", j=2),
                            BADA[:].unsqueeze(2).broadcast_to([128, 24, 2]), ALU.add).then_inc(mod_ready, 1)
            dve.wait_ge(mod_ready, 1)
            steps[0] += 1
            V.scalar_tensor_tensor(out=SCL[:], in0=MOD[:, 8:16, :], scalar=1.0, in1=NG[:].unsqueeze(2).broadcast_to([128, KD, 2]),
                                   op0=ALU.add, op1=ALU.mult).then_inc(dve_step, 1)
            dve.wait_ge(dve_step, steps[0])
            dve.wait_ge(xt_evac, 2 * NT)

            def h_low(k):
                dve.wait_ge(hh_done, k + 1)
                V.tensor_tensor(HL[:, k, :], XT[:, k, :], HH[:, k, :].bitcast(F32), ALU.subtract).then_inc(hl_done, 1)

            for k in range(KD):
                V.tensor_scalar(XT[:, k, 0:SEQ], XT[:, k, 0:SEQ], SCL[:, k, 0:1], MOD[:, k, 0:1], ALU.mult, ALU.add)
                V.tensor_scalar(XT[:, k, SEQ:TOK], XT[:, k, SEQ:TOK], SCL[:, k, 1:2], MOD[:, k, 1:2], ALU.mult, ALU.add).then_inc(h_ready, 1)
                if k >= 1:
                    h_low(k - 1)
            h_low(KD - 1)
            dve.wait_ge(gate_pe, 1)
            V.tensor_copy(GROW[:], bank(7)[0:16, 0:128]).then_inc(gate_rows, 1)
            def scores(tt):
                r, nk = rows_of(tt), keys_of(tt)
                out = SC[0:r, SOFF[tt]:SOFF[tt] + nk]
                for h in range(4):
                    n = SHEADS.index((tt, h))
                    v = PS[0:r, 4 + 2 * (n % 2):6 + 2 * (n % 2), :].rearrange("p b n -> p (b n)")[:, 0:nk]
                    dve.wait_ge(relu_done, n + 1)
                    if h == 0:
                        last = V.tensor_scalar(out, v, IW[0:r, tt, 0:1], None, ALU.mult)
                    else:
                        dve.wait_ge(acc_done, n)
                        last = V.scalar_tensor_tensor(out=out, in0=v, scalar=IW[0:r, tt, h:h + 1], in1=out, op0=ALU.mult, op1=ALU.add)
                    last.then_inc(acc_done, 1)
                if tt != SAMPLE:
                    dve.wait_ge(acc_done, SHEADS.index((tt, 3)) + 1)
                    link(V.memset(SC[0:CHUNK, SOFF[tt] + nk - CHUNK:SOFF[tt] + nk], -NEG_BIG))

            for i in range(ITEMS + 1):
                if i < ITEMS:
                    slot = IN2[i % 2]
                    r = rows_of(i) if i < NT else 128
                    if i >= 2:
                        dve.wait_ge(idx_t, i - 1)
                    if i < NT:
                        dve.wait_ge(idx_evac, i + 1)
                        V.tensor_copy(slot[0:r, 0:4, 0, :], NIDX[0:r, i % 2, 0:256].rearrange("p (h d) -> p h d", h=4))
                        V.tensor_copy(IW[0:r, i, :], NIDX[0:r, i % 2, 320:324])
                        k_nat = NIDX[0:r, i % 2, 256:320]
                    else:
                        k_nat = CIK[:, i - NT, :]
                    V.tensor_copy(slot[0:r, 4, :, :], k_nat.unsqueeze(1).broadcast_to([r, 2, HD])).then_inc(idx_hi, 1)
                if 2 <= i - 1 < SAMPLE:
                    scores(i - 1)
            scores(SAMPLE)
            dve.wait_ge(acc_done, len(SHEADS))
            def pick_rounds(tiles, rounds, unroll):
                n = len(tiles)
                with dve.Fori(0, rounds // unroll):
                    for un in range(unroll):
                        for a, tt in enumerate(tiles):
                            r, w = rows_of(tt), SC[0:rows_of(tt), SOFF[tt]:SOFF[tt] + keys_of(tt)]
                            if un > 0:
                                dve.wait_ge(sel_step, 2 * n * un - n + a + 1)
                            V.max(M8[0:r, a, :], w).then_inc(sel_step, 1)
                        for a, tt in enumerate(tiles):
                            r, w = rows_of(tt), SC[0:rows_of(tt), SOFF[tt]:SOFF[tt] + keys_of(tt)]
                            dve.wait_ge(sel_step, 2 * n * un + a + 1)
                            V.match_replace(w, M8[0:r, a, :], w, TAKEN).then_inc(sel_step, 1)
                    dve.wait_ge(sel_step, 2 * n * unroll)
                    dve.sem_clear(sel_step)
                for tt in tiles:
                    mask(tt)

            def mask(tt):
                r, nk = rows_of(tt), keys_of(tt)
                V.tensor_scalar(MASK[0:r, MOFF[tt]:MOFF[tt] + nk], SC[0:r, SOFF[tt]:SOFF[tt] + nk],
                                -2.0e38, NEG_BIG, ALU.is_gt, ALU.mult).then_inc(mask_done, 1)

            for tt in range(2):
                nk = keys_of(tt)
                link(V.memset(MASK[:, MOFF[tt]:MOFF[tt] + nk], 0.0))
                V.memset(MASK[0:CHUNK, MOFF[tt] + nk - CHUNK:MOFF[tt] + nk], NEG_BIG).then_inc(mask_done, 1)
            for pair in ((2, 3), (4, 5), (6, 7)):
                pick_rounds(pair, KSEL // 8, 4)
            pick_rounds((SAMPLE,), KSEL_S // 8, 3)
            dve.wait_ge(kv_in, 160)
            dve.wait_ge(piece_pe, NP)
            dve.wait_ge(mask_done, NT)
            V.memset(BTB[0:CHUNK, :, 192:256], NEG_BIG)
            link(V.memset(BTB[CHUNK:128, :, 0:64], NEG_BIG))
            for s in range(S0, S1):
                if 0 <= s < NU:
                    u = s
                    tt, br, h = UNITS[u]
                    r, nk = rows_of(tt), unit_keys(u)
                    if br == 0:
                        j0 = 384 if tt == SAMPLE else 896 - 128 * tt
                        bias, init = BTA[0:r, h, j0:j0 + nk], 3.0e38
                    else:
                        j0 = 128 if tt == 0 else 0
                        bias, init = BTB[0:r, h, j0:j0 + nk], NSINK[0:r, h:h + 1]
                    dve.wait_ge(qk_pe, u + 1)
                    if u >= 2:
                        dve.wait_ge(exp_done, u - 1)
                    v = PS[0:r, 2 * (u % 2):2 * (u % 2) + 2, :].rearrange("p b n -> p (b n)")[:, 0:nk]
                    V.tensor_tensor_reduce(out=LG[0:r, u % 2, 0:nk], in0=v, in1=bias, scale=1.0, scalar=init,
                                           op0=ALU.add, op1=ALU.min, accum_out=NM[0:r, br, h:h + 1]).then_inc(min_done, 1)
                if s % 16 == 0 and 16 <= s <= NU:
                    g = s // 16 - 1
                    r = rows_of(g)
                    dve.wait_ge(min_done, 16 * (g + 1))
                    if g >= 1:
                        dve.wait_ge(sink_act, g)
                    V.tensor_tensor(SD[0:r, :], NM[0:r, 1, :], SINK[0:r, :], ALU.add).then_inc(sink_sum, 1)
                for x in TP[s]:
                    if TIDX[x] % 2 == 0:
                        t_evac(dve, V.tensor_copy, x, tev_dve)
                tt = prep(s, 1)
                if tt is not None:
                    r = rows_of(tt)
                    q = QKV[0:r, tt % 2, :].rearrange("p (b c) -> p b c", b=2)[:, :, 0:640]
                    dve.wait_ge(qkv_in[tt % 2], 16 * (tt // 2 + 1))
                    if tt >= 1:
                        dve.wait_ge(k_out, 16 * k_stores(tt - 1))
                        dve.wait_ge(qs_lo, tt)
                    V.tensor_tensor(XNB[0:r, :, :].rearrange("p (b h) d -> p b (h d)", b=2), q, q, ALU.mult).then_inc(sq_done, 1)
                tt = prep(s, 2)
                if tt is not None:
                    r = rows_of(tt)
                    dve.wait_ge(sq_done, tt + 1)
                    link(V.tensor_reduce(SS[0:r, :], XNB[0:r, :, :], AX.X, ALU.add))
                tt = prep(s, 3)
                if tt is not None:
                    r = rows_of(tt)
                    rsqrt_chain(dve, link, RY[0:r, :], SS[0:r, :], 20, r, 1.0 / HD)
                    ry = RY[0:r, :].rearrange("p (b h) -> p b h", b=2)[:, :, 0:8]
                    link(V.tensor_scalar(ry, ry, -HD ** -0.5, None, ALU.mult))
                tt = prep(s, 4)
                if tt is not None:
                    r = rows_of(tt)
                    dve.wait_ge(xg_ready, tt + 1)
                    V.tensor_tensor(XNB[0:r, :, :], XG[0:r, :, :], RY[0:r, :].unsqueeze(2).broadcast_to([r, 20, HD]), ALU.mult).then_inc(xn4_ready, 1)
                if (s - 9) % 8 == 0 and 9 <= s <= NU + 1:
                    g = (s - 9) // 8
                    tt, br = g // 2, g % 2
                    r = rows_of(tt)
                    dve.wait_ge(exp_done, 8 * (g + 1))
                    if br:
                        dve.wait_ge(sink_act, tt + 1)
                        link(V.tensor_tensor(DEN[0:r, 1, :], DEN[0:r, 1, :], ES[0:r, 0, :], ALU.add))
                    link(V.reciprocal(RT[0:r, 0:8], DEN[0:r, br, :]))
                    dve.wait_ge(pv_pe, 8 * (g + 1))
                    if g >= 2:
                        dve.wait_ge(tr_pe, TIDX[("A", (g - 2) // 2, br)] + 1)
                    V.tensor_tensor(ATTN[0:r, br, :].rearrange("p (h d) -> p h d", h=8),
                                    bank(6 + br)[0:r, :].rearrange("p (h d) -> p h d", h=8),
                                    RT[0:r, 0:8].unsqueeze(2).broadcast_to([r, 8, HD]), ALU.mult).then_inc(att_done, 1)
            def az_low(k):
                dve.wait_ge(az_hi, k + 1)
                V.tensor_tensor(ZL[:, k, :], AST[:, k % 2, :], ZH[:, k, :].bitcast(F32), ALU.subtract).then_inc(az_lo, 1)

            for k in range(KD):
                dve.wait_ge(az_in[k % 2], 32 * (k // 2 + 1))
                V.tensor_tensor(AST[:, k % 2, :], AST[:, k % 2, :], ZST[:, k % 2, :], ALU.mult).then_inc(az_mul, 1)
                if k >= 1:
                    az_low(k - 1)
            az_low(KD - 1)
            for i in range(3 * KD):
                j, g = i // 3, i % 3
                gn = GROUPS[g][1]
                dve.wait_ge(o_pe, i + 1)
                dve.wait_ge(g_in[i % 3], 32 * (i // 3 + 1))
                if i >= 2:
                    dve.wait_ge(m_lo, i - 1)
                V.tensor_tensor(TM[:, i % 2, 0, 0:gn], bank(2 * (i % 2))[:, 0:gn], GT[:, i % 3, 0, 0:gn], ALU.mult)
                link(V.tensor_tensor(TM[:, i % 2, 1, 0:gn], bank(2 * (i % 2) + 1)[:, 0:gn], GT[:, i % 3, 1, 0:gn], ALU.mult))
                V.tensor_tensor(TM[:, i % 2, 2, 0:gn], TM[:, i % 2, 0, 0:gn], TM[:, i % 2, 1, 0:gn], ALU.add).then_inc(m_dve, 1)
            dve.wait_ge(gate_in, 32)
            for i in range(NYC * NT):
                c, tt = i // NT, i % NT
                r = rows_of(tt)
                dve.wait_ge(y_pe, i + 1)
                if i >= 3:
                    dve.wait_ge(y_add, i - 2)
                V.tensor_tensor(YT[0:r, i % 3, :], bank(4 + i % 3)[0:r, 0:YW],
                                GATE[0:r, int(tt == SAMPLE), YW * c:YW * (c + 1)], ALU.mult).then_inc(y_mul, 1)

        @block.tensor
        def _(pe):
            T = nc.tensor

            def three(out, wh, wl, mh, ml, first, last):
                T.matmul(out, wh, mh, start=first, stop=False)
                T.matmul(out, wh, ml, start=False, stop=False)
                return T.matmul(out, wl, mh, start=False, stop=last)

            pe.wait_ge(consts_in, 16 * N_SMALL)
            for i in range(3):
                n = min(512, BIAS_L - 512 * i)
                T.matmul(bank(5 + i)[0:16, 0:n], RELB[:], ONEH[:, 512 * i:512 * i + n], start=True, stop=True).then_inc(bias_pe, 1)
            for q in range(2 * NT):
                tt, half = q // 2, q % 2
                r = rows_of(tt)
                pe.wait_ge(xn_ready, tt + 1)
                if q >= 4:
                    pe.wait_ge(xt_evac, q - 3)
                for b in range(4):
                    k = 4 * half + b
                    last = T.transpose(bank(q % 4)[:, 128 * b:128 * b + r], XNAT[tt][0:r, 128 * k:128 * (k + 1)], IDF[0:r, 0:r])
                last.then_inc(xt_pe, 1)
            pe.wait_ge(c_ready, 1)
            for k in range(KD):
                pe.wait_ge(wada_in[k], 16)
                for c in range(24):
                    last = T.matmul(bank(4)[:, 2 * c:2 * c + 2], WADA[k][:, 128 * c:128 * (c + 1)], CSIL[:, k, :],
                                    start=(k == 0 and c == 0), stop=(k == KD - 1 and c == 23), skip_group_check=True)
            last.then_inc(ada_done, 1)
            def score(tt):
                r, nk = rows_of(tt), keys_of(tt)
                keys = IKTS if tt == SAMPLE else IKT
                for h in range(4):
                    n = SHEADS.index((tt, h))
                    if n >= 2:
                        pe.wait_ge(acc_done, n - 1)
                    for b in range(0, nk, 512):
                        m = min(512, nk - b)
                        out = PS[0:r, 4 + 2 * (n % 2) + b // 512, 0:m]
                        for part in range(2):
                            last = T.matmul(out, IQT[:, h, tcols(tt)], keys[:, part, b:b + m], start=(part == 0), stop=(part == 1))
                    last.then_inc(score_pe, 1)

            pe.wait_ge(mod_ready, 1)
            T.transpose(bank(7)[0:16, 0:128], MOD[:, 16:24, :].rearrange("p k j -> p (k j)"), IDF[:]).then_inc(gate_pe, 1)
            pe.wait_ge(hl_done, KD)
            pe.wait_ge(lo_done, KD)
            pe.wait_ge(ident_ready, 1)
            pe.wait_ge(gate_rows, 1)
            for i in range(ITEMS + 1):
                if i < NT:
                    r = rows_of(i)
                    if i >= 2:
                        pe.wait_ge(idx_evac, i - 1)
                    for k in range(KD):
                        last = three(bank(i % 2)[0:r, 0:IDX_W], HH[:, k, tcols(i)], HL[:, k, tcols(i)],
                                     WH[0][:, k, 0:IDX_W], WL[0][:, k, 0:IDX_W], k == 0, k == KD - 1)
                    last.then_inc(idx_pe, 1)
                if i >= 1:
                    j = i - 1
                    r = rows_of(j) if j < NT else 128
                    pe.wait_ge(idx_lo, j + 1)
                    if j >= 1:
                        pe.wait_ge(idx_tev, j)
                    slot = IN2[j % 2]
                    for h in range(6):
                        if h < 4 and j >= NT:
                            continue
                        dst = bank(2)[:, 128 * h:128 * h + r] if h < 4 else bank(3)[:, 128 * (h - 4):128 * (h - 4) + r]
                        last = T.transpose(dst.bitcast(F32R), slot[0:r, h, :, :].rearrange("p a d -> p (a d)"), IDR[0:r, 0:r])
                    last.then_inc(idx_t, 1)
                    if 2 <= j < SAMPLE:
                        pe.wait_ge(idx_tev, j + 1)
                        score(j)
            pe.wait_ge(idx_tev, ITEMS)
            score(SAMPLE)
            for p, (c, j, w) in enumerate(PIECES):
                if j == 0:
                    pe.wait_ge(lo_done, KD * (c + 1))
                if p >= 4:
                    pe.wait_ge(piece_ev, p - 3)
                H, L = WH[c % 2], WL[c % 2]
                for k in range(KD):
                    if w[0] == "nat":
                        last = three(bank(p % 4)[0:rows_of(j), :], HH[:, k, tcols(j)], HL[:, k, tcols(j)],
                                     H[:, k, :], L[:, k, :], k == 0, k == KD - 1)
                    else:
                        g0, gn = GROUPS[w[2]]
                        bc = slice(128 * w[1], 128 * (w[1] + 1))
                        last = three(bank(p % 4)[:, 0:gn], H[:, k, bc], L[:, k, bc],
                                     HH[:, k, g0:g0 + gn], HL[:, k, g0:g0 + gn], k == 0, k == KD - 1)
                last.then_inc(piece_pe, 1)
            pe.wait_ge(piece_ev, NP)
            pe.wait_ge(mask_done, NT)
            pe.wait_ge(kv_in, 160)
            for s in range(S0, S1):
                if 0 <= s < NU:
                    u = s
                    tt, br, h = UNITS[u]
                    r, nk = rows_of(tt), unit_keys(u)
                    if h == 0:
                        q = TIDX[("K", tt, 1)]
                        pe.wait_ge(tev_dve, q // 2 + 1)
                        pe.wait_ge(tev_act, (q + 1) // 2)
                    if u >= 2:
                        pe.wait_ge(min_done, u - 1)
                    if br == 0:
                        keys, k0 = (KTAS if tt == SAMPLE else KTA), 0
                    else:
                        keys, k0 = (KTBS, 0) if tt == SAMPLE else (KTB, 128 * max(tt - 1, 0))
                    for b in range(0, nk, 512):
                        m = min(512, nk - b)
                        out = PS[0:r, 2 * (u % 2) + b // 512, 0:m]
                        for part in range(2):
                            last = T.matmul(out, QT[tt % 2][:, 8 * br + h, 0:r], keys[:, h // 4, part, k0 + b:k0 + b + m],
                                            start=(part == 0), stop=(part == 1 and br == 1))
                        if br == 0:
                            last = T.matmul(out, IDB[0:r, 0:r], MASK[0:r, MOFF[tt] + b:MOFF[tt] + b + m], start=False, stop=True)
                    last.then_inc(qk_pe, 1)
                for x in TP[s]:
                    q = TIDX[x]
                    if q >= 2:
                        pe.wait_ge(tev_dve if q % 2 == 0 else tev_act, q // 2)
                    out = bank(4 + q % 2)
                    if x[0] == "P":
                        u = x[1]
                        tt = UNITS[u][0]
                        r, nk = rows_of(tt), unit_keys(u)
                        pe.wait_ge(exp_done, u + 1)
                        for b in range(4 * x[2], min(4 * x[2] + 4, (nk + 127) // 128)):
                            m = min(128, nk - 128 * b)
                            last = T.transpose(out[0:m, 128 * (b % 4):128 * (b % 4) + r], PB[0:r, u % 2, 128 * b:128 * b + m], IDF[0:r, 0:r])
                    elif x[0] == "A":
                        g, r = 2 * x[1] + x[2], rows_of(x[1])
                        pe.wait_ge(att_done, g + 1)
                        for b in range(4):
                            last = T.transpose(out[:, 128 * b:128 * b + r], ATTN[0:r, x[2], 128 * b:128 * (b + 1)], IDF[0:r, 0:r])
                    else:
                        if x[0] == "C":
                            r = 128
                            pe.wait_ge(cache_lo, x[1] + 1)
                            src = [KSC[:, kv, 2 * p:2 * p + 2, :] for kv in range(2) for p in range(2)]
                        else:
                            r = rows_of(x[1])
                            pe.wait_ge(qs_lo, x[1] + 1)
                            if x[0] == "Q":
                                src = [QS[0:r, 4 * x[2] + b, :, :] for b in range(4)]
                            else:
                                src = [KS[0:r, 2 * x[2] + kv, 2 * p:2 * p + 2, :] for kv in range(2) for p in range(2)]
                        for b in range(4):
                            last = T.transpose(out[:, 128 * b:128 * b + r].bitcast(F32R), src[b].rearrange("p a d -> p (a d)"), IDR[0:r, 0:r])
                    last.then_inc(tr_pe, 1)
                if 0 <= s - 2 < NU:
                    u = s - 2
                    tt, br, h = UNITS[u]
                    r, nk = rows_of(tt), unit_keys(u)
                    q = last_t(u)
                    pe.wait_ge(tev_dve, q // 2 + 1)
                    pe.wait_ge(tev_act, (q + 1) // 2)
                    g = 2 * tt + br
                    if h == 0 and g >= 2:
                        pe.wait_ge(att_done, g - 1)
                    kb = (nk + 127) // 128
                    kv = slice(HD * (h // 4), HD * (h // 4) + HD)
                    for b in range(kb):
                        m = min(128, nk - 128 * b)
                        if br == 0:
                            v = VAS[0:m, b, kv] if tt == SAMPLE else VA[0:m, b, kv]
                        else:
                            v = VBS[0:m, b, kv] if tt == SAMPLE else VB[0:m, max(tt - 1, 0) + b, kv]
                        last = T.matmul(bank(6 + br)[0:r, HD * h:HD * (h + 1)], PT[0:m, u % 2, 128 * b:128 * b + r], v,
                                        start=(b == 0), stop=(b == kb - 1))
                    last.then_inc(pv_pe, 1)
            pe.wait_ge(az_lo, KD)
            for i in range(3 * KD):
                j, g = i // 3, i % 3
                g0, gn = GROUPS[g]
                if g == 0:
                    pe.wait_ge(ow_lo, j + 1)
                if i >= 2:
                    pe.wait_ge(m_dve, i - 1)
                for b in range(2):
                    for k in range(4 * b, 4 * b + 4):
                        last = three(bank(2 * (i % 2) + b)[:, 0:gn], WOH[:, j % 2, k, :], WOL[:, j % 2, k, :],
                                     ZH[:, k, g0:g0 + gn], ZL[:, k, g0:g0 + gn], k == 4 * b, k == 4 * b + 3)
                last.then_inc(o_pe, 1)
            pe.wait_ge(m_lo, 3 * KD)
            for i in range(NYC * NT):
                c, tt = i // NT, i % NT
                if tt == 0:
                    pe.wait_ge(u_lo, KD * (c + 1))
                if i >= 3:
                    pe.wait_ge(y_mul, i - 2)
                for k in range(KD):
                    last = three(bank(4 + i % 3)[0:rows_of(tt), 0:YW], MH[:, k, tcols(tt)], ML[:, k, tcols(tt)],
                                 UH[c][:, k, :], UL[c][:, k, :], k == 0, k == KD - 1)
                last.then_inc(y_pe, 1)

    return nc


_OUTS = [((1, SEQ, D)), ((1, DEC, D)),
         (1, 1, SEQ, 2, HD), (1, 1, SEQ, 2, HD), (1, 1, SEQ, HD), (1, 1, WIN, 2, HD), (1, 1, WIN, 2, HD),
         (1, 1, DEC, 2, HD), (1, 1, DEC, 2, HD), (1, 1, DEC, HD), (1, 1, WIN, 2, HD), (1, 1, WIN, 2, HD)]
_OUT_NAMES = ["y_prompt", "y_sample", "pa_k", "pa_v", "pa_ik", "pb_k", "pb_v", "sa_k", "sa_v", "sa_ik", "sb_k", "sb_v"]
_OUT_SHAPES = [(SEQ, D), (DEC, D), (SEQ, 128), (SEQ, 128), (SEQ, HD), (WIN, 128), (WIN, 128),
               (DEC, 128), (DEC, 128), (DEC, HD), (WIN, 128), (WIN, 128)]


def kernel(**inputs):
    import numpy as np
    import concourse.bacc as bacc
    from concourse.bass_utils import run_bass_kernel_spmd

    f = np.float32
    x = {n: np.ascontiguousarray(a) for n, a in inputs.items()}
    w_in = x["w_in"][0]
    spans = ((1280, 1604), (0, 768), (1604, 2372), (768, 1280), (2372, 2884), (2884, 4932))

    def cols(v):
        return np.ascontiguousarray(v.reshape(-1, 128).T)

    rel = np.arange(BIAS_L) - (SEQ - 1)
    n = np.abs(rel)
    large = 8 + (np.log(np.maximum(n, 1).astype(f) / f(8)) / f(np.log(128.0)) * f(8)).astype(np.int32)
    bucket = (rel > 0) * 16 + np.where(n < 8, n, np.minimum(large, 15))
    onehot = (np.arange(32)[:, None] == bucket[None, :]).astype(f)
    arrays = {
        "x_prompt": x["x_prompt"][0], "x_sample": x["x_sample"][0],
        "w_all": np.concatenate([w_in[:, a:b] for a, b in spans], axis=1),
        "w_ada": x["w_ada"][0], "w_o": np.concatenate([x["w_oa"][0], x["w_ob"][0]], axis=0), "w_out": x["w_out"][0],
        "cache_ak": x["cache_a_k"].reshape(PAST, 128), "cache_av": x["cache_a_v"].reshape(PAST, 128),
        "cache_ik": x["cache_a_ik"].reshape(PAST, HD),
        "cache_bk": x["cache_b_k"].reshape(WIN, 128), "cache_bv": x["cache_b_v"].reshape(WIN, 128),
        "c_cols": np.ascontiguousarray(np.stack([cols(x["c_prompt"]), cols(x["c_sample"])], axis=2)),
        "ng_cols": cols(x["norm_g"]), "bada_cols": cols(x["b_ada"]),
        "gammas": np.ascontiguousarray(np.broadcast_to(
            np.stack([x[k][0] for k in ("a_q_norm", "a_k_norm", "b_q_norm", "b_k_norm")])[None], (128, 4, HD))),
        "sinks": np.ascontiguousarray(np.broadcast_to(x["b_sinks"], (128, 8))),
        "rel_bias": x["rel_bias"], "ident": np.eye(128, dtype=f), "onehot": onehot,
    }
    nc = bacc.Bacc("TRN2", target_bir_lowering=False, num_devices=1)
    t, ins = {}, {}
    for name, a in arrays.items():
        a = np.ascontiguousarray(a)
        ins[f"in_{name}"] = a
        t[name] = nc.dram_tensor(f"in_{name}", a.shape, mybir.dt.from_np(a.dtype), kind="ExternalInput").ap()
    for name, shape in zip(_OUT_NAMES, _OUT_SHAPES):
        t[name] = nc.dram_tensor(f"out_{name}", shape, F32, kind="ExternalOutput").ap()
    build_program(nc, t)
    r = run_bass_kernel_spmd(nc, [ins], core_ids=[0]).results[0]
    return tuple(np.asarray(r[f"out_{name}"]).reshape(shape) for name, shape in zip(_OUT_NAMES, _OUTS))
```

```python
import concourse.bass as bass
from concourse import mybir
from contextlib import ExitStack

F32 = mybir.dt.float32
F32R = mybir.dt.float32r
BF16 = mybir.dt.bfloat16
I32 = mybir.dt.int32
ALU = mybir.AluOpType
ACT = mybir.ActivationFunctionType
AX = mybir.AxisListType

D = 1024
KD = D // 128
SEQ, DEC, PAST, WIN = 1024, 64, 512, 128
TOK = SEQ + DEC
NT = SEQ // 128 + 1
SAMPLE = NT - 1
HD = 64
CHUNK = 64
IDX_W = 4 * HD + HD + 4
NAT_W = 1536
CW = 512
GROUPS = [(0, 384), (384, 384), (768, 320)]
NEG_BIG = 1e30
TAKEN = -3.0e38
KSEL, KSEL_S = 256, (PAST + DEC) // 4
BIAS_L = 1151
EPS = 1e-6
SBUF0 = 16512


def rows_of(t):
    return DEC if t == SAMPLE else 128


def keys_of(t):
    return PAST + DEC if t == SAMPLE else 128 * (t + 1)


def keys_b(t):
    return WIN + DEC if t == SAMPLE else (128 if t == 0 else 256)


def build_program(nc, t):
    ctx = ExitStack()
    with ctx:
        def at(name, shape, dt, offset):
            return nc.alloc_sbuf_tensor_at(name, shape, dt, offset=SBUF0 + offset)

        def sem(name):
            return ctx.enter_context(nc.semaphore(name))

        PS = ctx.enter_context(nc.psum_tensor("PS", [128, 8, 512], F32))

        def bank(b):
            return PS[:, b, :]

        HH = at("HH", [128, KD, TOK], F32R, 0)
        HL = at("HL", [128, KD, TOK], F32R, 34816)
        WB = 69632
        WH = [at(f"WH{i}", [128, KD, CW], F32R, WB + 32768 * i) for i in range(2)]
        WL = [at(f"WL{i}", [128, KD, CW], F32R, WB + 32768 * i + 16384) for i in range(2)]
        RAW = at("RAW", [128, 4, CW], F32, WB + 65536)
        XB = WB + 65536 + 8192
        XT = at("XT", [128, KD, TOK], F32, XB)
        IQT = at("IQT", [128, 4, TOK], F32R, XB)
        IKT = at("IKT", [128, 2, SEQ], F32R, XB + 17408)
        IKTS = at("IKTS", [128, 2, PAST + DEC], F32R, XB + 25600)
        STG = at("STG", [128, 3, CW], F32, XB)
        ZS = at("ZS", [128, 2, 384], F32, XB + 6144)
        ZC = at("ZC", [128, 2, 384], F32, XB + 9216)
        MASK = at("MASK", [128, 5184], BF16, XB + 24448)
        SCB = XB + 34816
        SC = at("SC", [128, 4800], F32, SCB)
        SM = SCB + 19200
        XNAT = [at(f"XN{i}", [128, D], F32, WB + 4096 * i) for i in range(8)] + \
               [at("XN8", [128, D], F32, 61440)]
        WADA = [at(f"WADA{k}", [128, 3 * D], F32, 12288 * k) for k in range(5)] + \
               [at(f"WADA{k}", [128, 3 * D], F32, WB + 32768 + 12288 * (k - 5)) for k in (5, 6)] + \
               [at("WADA7", [128, 3 * D], F32, SCB)]
        ONEH = at("ONEH", [32, BIAS_L], F32, WB + 32768 + 24576)
        BV = at("BV", [16, BIAS_L], F32, SCB + 12288)
        SQJ = at("SQJ", [128, D], F32, 65536)
        MROW = at("MROW", [2, 2 * D], F32, 61440)
        MROWG = at("MROWG", [2, D], F32, WB + 32768 + 24576)
        off = [SM]

        def small(name, shape, dt=F32, size=None):
            n = 1
            for s in shape[1:]:
                n *= s
            n *= 2 if dt == BF16 else 4
            h = at(name, shape, dt, off[0])
            off[0] += (n + 31) // 32 * 32
            return h

        IDF = small("IDF", [128, 128])
        IDR = small("IDR", [128, 128], F32R)
        IDB = small("IDB", [128, 128], BF16)
        GAM = small("GAM", [128, 4, HD])
        SINK = small("SINK", [128, 8])
        NSINK = small("NSINK", [128, 8])
        CS = small("CS", [128, KD, 2])
        CG = small("CG", [128, KD, 2])
        CSIL = small("CSIL", [128, KD, 2])
        NG = small("NG", [128, KD])
        BADA = small("BADA", [128, 24])
        RELB = small("RELB", [32, 16])
        MOD = small("MOD", [128, 24, 2])
        SCL = small("SCL", [128, KD, 2])
        SS = small("SS", [128, NT])
        RV = small("RV", [128, NT])
        RI = small("RI", [128, NT], I32)
        RT = small("RT", [128, NT])
        RY = small("RY", [128, NT])
        IW = small("IW", [128, NT, 4])
        GROW = small("GROW", [16, 128])
        M8 = small("M8", [128, 2, 8])
        NM = small("NM", [128, 2, 8])
        DEN = small("DEN", [128, 2, 8])
        ES = small("ES", [128, 2, 8])
        SD = small("SD", [128, 8])
        RDEN = small("RDEN", [128, 8])
        IN2 = [at(f"IN{i}", [128, 6, 2, HD], F32R, off[0] + 3072 * i) for i in range(2)]
        NIDX = at("NIDX", [128, 2, IDX_W], F32, off[0] + 6144)
        CIK = at("CIK", [128, 4, HD], F32, off[0] + 6144 + 2624)
        SSQ = at("SSQ", [128, NT * 20], F32, off[0] + 9792)
        RVQ = at("RVQ", [128, NT * 20], F32, off[0])
        RIQ = at("RIQ", [128, NT * 20], I32, off[0] + 768)
        RTQ = at("RTQ", [128, NT * 20], F32, off[0] + 1536)
        RYQ = at("RYQ", [128, NT * 20], F32, XB + 23552)
        assert SBUF0 + off[0] + 9792 + 720 <= 229344, off[0]
        BTA = at("BTA", [128, 8, 1024], F32, 0)
        BTB = at("BTB", [128, 8, 256], F32, 32768)
        KTA = at("KTA", [128, 2, 2, SEQ], F32R, 40960)
        KTAS = at("KTAS", [128, 2, 2, PAST + DEC], F32R, 57344)
        QKV = at("QKV", [128, 2, NAT_W], F32, WB)
        QS = at("QS", [128, 16, 2, HD], F32R, WB + 12288)
        KS = at("KS", [128, 4, 4, HD], F32R, WB + 20480)
        QT = [at("QT0", [128, 16, 128], F32R, WB + 24576), at("QT1", [128, 16, 128], F32R, WB + 65536)]
        KTB = at("KTB", [128, 2, 2, SEQ], F32R, 102400)
        KTBS = at("KTBS", [128, 2, 2, WIN + DEC], F32R, 118784)
        VA = at("VA", [128, 8, 128], F32, 121856)
        VAS = at("VAS", [128, 5, 128], F32, 125952)
        VB = at("VB", [128, 8, 128], F32, 128512)
        VBS = at("VBS", [128, 2, 128], F32, 132608)
        XNB = at("XNB", [128, 20, HD], F32, XB + 6144)
        XG = at("XG", [128, 20, HD], F32, XB + 12288)
        LG = [at("LG0", [128, 1024], F32, XB), at("LG1", [128, 1024], F32, XB + 17408)]
        ATTN = [at("ATTN0", [128, 512], F32, XB + 4096), at("ATTN1", [128, 512], F32, 66560)]
        PB = [at("PB0", [128, 1024], F32, SCB), at("PB1", [128, 1024], F32, SCB + 4096), at("PB2", [128, 1024], F32, off[0] + 4096)]
        ZT = at("ZT", [128, 4, 128], F32, XB + 21504)
        PT = at("PT", [128, 2, 1024], F32, SCB + 8192)
        KSC = at("KSC", [128, 2, 4, HD], F32R, SCB + 16384)
        ATS = at("ATS", [128, 2, 4, 128], F32, off[0])
        CK = at("CK", [128, 5, 128], F32, off[0] + 8192)
        ZH = at("ZH", [128, KD, TOK], F32R, 0)
        ZL = at("ZL", [128, KD, TOK], F32R, 34816)
        MH = at("MH", [128, KD, TOK], F32R, 69632)
        ML = at("ML", [128, KD, TOK], F32R, 104448)
        ZST = [at(f"ZST{g}", [128, KD, GROUPS[g][1]], F32, (WB, WB + 12288, 102400)[g]) for g in range(3)]
        WOH = [at("WOH0", [128, KD, 128], F32R, 135168), at("WOH1", [128, KD, 128], F32R, XB)]
        WOL = [at("WOL0", [128, KD, 128], F32R, 139264), at("WOL1", [128, KD, 128], F32R, XB + 4096)]
        ORAW = at("ORAW", [128, 2, KD, 128], F32, XB + 8192)
        GT = at("GT", [128, 3, 2, 384], F32, XB + 16384)
        TM = at("TM", [128, 2, 3, 384], F32, XB + 25600)
        GATE = at("GATE", [128, 2, D], F32, SCB)
        YW = 256
        NYC = D // YW
        UH = [at("UH0", [128, KD, YW], F32R, SCB + 8192)] + \
             [at(f"UH{i}", [128, KD, YW], F32R, 16384 * (i - 1)) for i in range(1, NYC)]
        UL = [at("UL0", [128, KD, YW], F32R, off[0])] + \
             [at(f"UL{i}", [128, KD, YW], F32R, 16384 * (i - 1) + 8192) for i in range(1, NYC)]
        UQ = [at("UQ0", [128, 2, YW], F32, SCB + 16384), at("UQ1", [128, 2, YW], F32, off[0] + 8192)]
        URAW = [at(f"URAW{i}", [128, KD, YW], F32, XB + 8192 * i) for i in range(2)]
        XR = at("XR", [128, 3, YW], F32, 57344)
        YT = at("YT", [128, 3, YW], F32, 57344 + 3072)
        YO = at("YO", [128, 3, YW], F32, 57344 + 6144)

        snat = nc.dram_tensor("snat", [TOK, NAT_W], F32).ap()
        gz = nc.dram_tensor("gz", [3 * D, TOK], F32).ap()
        attd = nc.dram_tensor("attd", [D, TOK], F32).ap()
        btad = nc.dram_tensor("btad", [128, 8, 1024], F32).ap()
        btbd = nc.dram_tensor("btbd", [128, 8, 256], F32).ap()
        bvd = nc.dram_tensor("bvd", [16, BIAS_L], F32).ap()
        gated = nc.dram_tensor("gated", [2 * KD, 128], F32).ap()

        consts_in = sem("consts_in")
        x_in = [sem(f"x_in{i}") for i in range(NT)]
        wada_in = [sem(f"wada_in{k}") for k in range(KD)]
        raw_in = [sem(f"raw_in{i}") for i in range(4)]
        ident_ready = sem("ident_ready")
        c_sig = sem("c_sig")
        c_ready = sem("c_ready")
        dve_step = sem("dve_step")
        xn_ready = sem("xn_ready")
        xt_pe = sem("xt_pe")
        xt_evac = sem("xt_evac")
        ada_done = sem("ada_done")
        bias_pe = sem("bias_pe")
        bias_sb = sem("bias_sb")
        mrow_act = sem("mrow_act")
        mrow_ready = sem("mrow_ready")
        mod_pe = sem("mod_pe")
        mod_ready = sem("mod_ready")
        gate_pe = sem("gate_pe")
        gate_rows = sem("gate_rows")
        scratch_out = sem("scratch_out")
        bias_out = sem("bias_out")
        h_ready = sem("h_ready")
        hh_done = sem("hh_done")
        hl_done = sem("hl_done")
        hi_done = sem("hi_done")
        lo_done = sem("lo_done")
        idx_pe = sem("idx_pe")
        idx_evac = sem("idx_evac")
        idx_hi = sem("idx_hi")
        idx_lo = sem("idx_lo")
        idx_t = sem("idx_t")
        idx_tev = sem("idx_tev")
        ik_out = [sem(f"ik_out{i}") for i in range(2)]
        score_pe = sem("score_pe")
        relu_done = sem("relu_done")
        acc_done = sem("acc_done")
        sel_step = sem("sel_step")
        mask_done = sem("mask_done")
        piece_pe = sem("piece_pe")
        piece_ev = sem("piece_ev")
        nat_copied = sem("nat_copied")
        z_pool = sem("z_pool")
        stg_out = [sem(f"stg_out{i}") for i in range(3)]
        kva_in = sem("kva_in")
        kvb_in = sem("kvb_in")
        rest_in = sem("rest_in")
        zt_in = sem("zt_in")
        qkv_in = [sem(f"qkv_in{i}") for i in range(2)]
        rms_ready = sem("rms_ready")
        xg_ready = sem("xg_ready")
        xn4_ready = sem("xn4_ready")
        qs_hi = sem("qs_hi")
        qs_lo = sem("qs_lo")
        k_out = sem("k_out")
        copy_out = sem("copy_out")
        cache_hi = sem("cache_hi")
        cache_lo = sem("cache_lo")
        qk_pe = sem("qk_pe")
        min_done = sem("min_done")
        exp_done = sem("exp_done")
        tr_pe = sem("tr_pe")
        tev_dve = sem("tev_dve")
        tev_act = sem("tev_act")
        pv_pe = sem("pv_pe")
        sink_sum = sem("sink_sum")
        sink_act = sem("sink_act")
        att_done = sem("att_done")
        att_out = [sem(f"att_out{i}") for i in range(2)]
        z_in = [sem(f"z_in{i}") for i in range(3)]
        uq_in = [sem(f"uq_in{i}") for i in range(2)]
        az_hi = sem("az_hi")
        az_lo = sem("az_lo")
        oraw_in = [sem(f"oraw_in{i}") for i in range(2)]
        ow_hi = sem("ow_hi")
        ow_lo = sem("ow_lo")
        g_in = [sem(f"g_in{i}") for i in range(3)]
        o_pe = sem("o_pe")
        m_dve = sem("m_dve")
        m_hi = sem("m_hi")
        m_lo = sem("m_lo")
        gate_in = sem("gate_in")
        uraw_in = [sem(f"uraw_in{i}") for i in range(2)]
        u_hi = sem("u_hi")
        u_lo = sem("u_lo")
        xr_in = [sem(f"xr_in{i}") for i in range(3)]
        y_pe = sem("y_pe")
        y_mul = sem("y_mul")
        y_add = sem("y_add")
        y_out = [sem(f"y_out{i}") for i in range(3)]

        SOFF = {}
        o = 0
        for tt in range(2, NT):
            SOFF[tt] = o
            o += keys_of(tt)
        MOFF = {}
        o = 0
        for tt in range(NT):
            MOFF[tt] = o
            o += keys_of(tt)

        def tcols(tt):
            return slice(128 * tt, 128 * tt + rows_of(tt))

        CHUNKS = [("idx", 0, IDX_W)]
        CHUNKS += [("nat", IDX_W + CW * i, CW) for i in range(NAT_W // CW)]
        CHUNKS += [("z", IDX_W + NAT_W + CW * i, CW) for i in range(2)]
        CHUNKS += [("g", IDX_W + NAT_W + D + CW * i, CW) for i in range(4)]
        NCH = len(CHUNKS)
        PIECES = []
        for c in range(1, NCH):
            if CHUNKS[c][0] == "nat":
                PIECES += [(c, j, ("nat", j)) for j in range(NT)]
            else:
                PIECES += [(c, j, (CHUNKS[c][0], j // 3, j % 3)) for j in range(12)]
        NP = len(PIECES)
        PEND = [len([1 for c, _, _ in PIECES if c <= e]) for e in range(NCH)]
        ZP = [p for p, (c, j, w) in enumerate(PIECES) if w[0] == "z"]
        NST = [len([p for p in range(len(PIECES)) if p % 3 == i]) for i in range(3)]

        ITEMS = NT + PAST // 128
        SCORED = [tt for tt in range(2, NT)]
        SHEADS = [(tt, h) for tt in SCORED for h in range(4)]

        UNITS = [(tt, br, h) for tt in range(NT) for br in range(2) for h in range(8)]
        NU = len(UNITS)

        def unit_keys(u):
            tt, br, _ = UNITS[u]
            return keys_b(tt) if br else keys_of(tt)

        S0, S1 = -22, NU + 9
        TP = {s: [] for s in range(S0, S1)}
        for s in range(S0, S1):
            if 0 <= s - 2 < NU:
                for j in range((unit_keys(s - 2) + 511) // 512):
                    TP[s].append(("P", s - 2, j))
        for tt in range(NT):
            base = 16 * (tt - 1)
            for j in range(4):
                TP[base + 9 + j].append(("Q", tt, j))
            for j in range(2):
                TP[base + 13 + j].append(("K", tt, j))
        for i in range(5):
            TP[16 * (2 + i) + 6].append(("C", i, 0))
        for g in range(2 * NT):
            TP[8 * g + 15].append(("A", g // 2, g % 2))
        TQ = [(s, x) for s in range(S0, S1) for x in TP[s]]
        TIDX = {x: q for q, (_, x) in enumerate(TQ)}
        PREP0 = {16 * (tt - 1): tt for tt in range(NT)}
        CACHE_STEP = {16 * (2 + i): i for i in range(5)}

        LOAD_AT, NORM_AT, SPLIT_AT = -6, -4, 4

        def prep(s, after):
            return PREP0.get(s - after)

        def k_stores(tt):
            return tt + 1 + (tt >= SAMPLE - 1) + (tt >= SAMPLE)

        EV = []
        for q, (_, x) in enumerate(TQ):
            EV.append("V" if x[0] == "A" or sum(e == "V" for e in EV) <= sum(e == "S" for e in EV) else "S")

        def evacs(q):
            return EV[:q + 1].count("V"), EV[:q + 1].count("S")

        def wait_evacs(eng, q):
            v, a = evacs(q)
            if v:
                eng.wait_ge(tev_dve, v)
            if a:
                eng.wait_ge(tev_act, a)

        def wait_evac(eng, q):
            eng.wait_ge(tev_dve if EV[q] == "V" else tev_act, evacs(q)[EV[q] == "S"])

        def last_t(u):
            return TIDX[("P", u, (unit_keys(u) + 511) // 512 - 1)]

        def t_evac(eng, copy, x, done):
            q = TIDX[x]
            eng.wait_ge(tr_pe, q + 1)
            src = bank(4 + q % 2).rearrange("p (b n) -> p b n", b=4)
            if x[0] == "P":
                u, j = x[1], x[2]
                r, nk = rows_of(UNITS[u][0]), unit_keys(u) - 512 * j
                full, part = min(4, nk // 128), nk % 128 if nk < 512 else 0
                dst = PT[:, u % 2, 512 * j:512 * (j + 1)].rearrange("p (b n) -> p b n", b=4)
                if u >= 2:
                    eng.wait_ge(pv_pe, u - 1)
                if full:
                    last = copy(dst[:, 0:full, 0:r], src[:, 0:full, 0:r])
                if part:
                    last = copy(dst[0:part, full, 0:r], src[0:part, full, 0:r])
            elif x[0] == "Q":
                if x[1] >= 2:
                    eng.wait_ge(qk_pe, 16 * (x[1] - 1))
                r = rows_of(x[1])
                last = copy(QT[x[1] % 2][:, 4 * x[2]:4 * x[2] + 4, 0:r], src[:, :, 0:r])
            elif x[0] == "A":
                g, r = 2 * x[1] + x[2], rows_of(x[1])
                if g >= 2:
                    eng.wait_ge(att_out[g % 2], 16 * (g // 2))
                eng.wait_ge(zt_in, 16 * (g + 1))
                last = nc.vector.tensor_tensor(ATS[:, g % 2, :, 0:r], src[:, :, 0:r], ZT[:, :, 0:r], ALU.mult)
            else:
                if x[0] == "C":
                    dst = KTAS[:, :, :, 128 * x[1]:128 * (x[1] + 1)] if x[1] < 4 else KTBS[:, :, :, 0:WIN]
                elif x[1] == SAMPLE:
                    dst = KTBS[:, :, :, WIN:WIN + DEC] if x[2] else KTAS[:, :, :, PAST:PAST + DEC]
                else:
                    dst = (KTB if x[2] else KTA)[:, :, :, tcols(x[1])]
                r = rows_of(x[1]) if x[0] == "K" else 128
                last = copy(dst, bank(4 + q % 2).rearrange("p (a b n) -> p a b n", a=2, b=2)[:, :, :, 0:r])
            last.then_inc(done, 1)

        def rsqrt_chain(link, out, ss, v, i, tmp, scale):
            link(nc.vector.tensor_scalar(v, ss, scale, EPS, ALU.mult, ALU.add))
            link(nc.vector.tensor_scalar(i, v.bitcast(I32), 1, None, ALU.arith_shift_right))
            link(nc.vector.tensor_scalar(i, i, -1.0, float(0x5F3759DF), ALU.mult, ALU.add))
            for step in range(3):
                y = out if step else i.bitcast(F32)
                link(nc.vector.tensor_tensor(tmp, y, y, ALU.mult))
                link(nc.vector.tensor_tensor(tmp, tmp, v, ALU.mult))
                link(nc.vector.tensor_scalar(tmp, tmp, -0.5, 1.5, ALU.mult, ALU.add))
                link(nc.vector.tensor_tensor(out, y, tmp, ALU.mult))

        w_all_v = t["w_all"].rearrange("(k p) n -> p k n", p=128)
        N_SMALL = 12
        block = ctx.enter_context(nc.Block())

        @block.sync
        def _(sp):
            def raw_load(n):
                c, k = n // KD, n % KD
                if c >= NCH:
                    return
                if n >= 4:
                    sp.wait_ge(lo_done, n - 3)
                _, c0, cw = CHUNKS[c]
                sp.dma_start(RAW[:, n % 4, 0:cw], w_all_v[:, k, c0:c0 + cw]).then_inc(raw_in[n % 4], 16)

            for dst, src in ((CS[:], t["c_cols"]), (IDF[:], t["ident"]), (NG[:], t["ng_cols"]),
                             (BADA[:], t["bada_cols"]), (RELB[:], t["rel_bias"]), (ONEH[:], t["onehot"]),
                             (GAM[:], t["gammas"]), (SINK[:], t["sinks"])):
                sp.dma_start(dst, src).then_inc(consts_in, 16)
            for i in range(4):
                sp.dma_start(CIK[:, i, :], t["cache_ik"][128 * i:128 * (i + 1), :]).then_inc(consts_in, 16)
            for tt in range(NT):
                r = rows_of(tt)
                src = t["x_sample"] if tt == SAMPLE else t["x_prompt"][tcols(tt), :]
                sp.dma_start(XNAT[tt][0:r, :], src).then_inc(x_in[tt], 16)
            for k in range(KD):
                sp.dma_start(WADA[k][:], t["w_ada"][128 * k:128 * (k + 1), :]).then_inc(wada_in[k], 16)
            for n in range(4):
                raw_load(n)
            sp.wait_ge(bias_sb, 3)
            sp.dma_start(bvd, BV[:, :]).then_inc(scratch_out, 16)
            for n in range(4, 12):
                raw_load(n)
            sp.wait_ge(gate_rows, 1)
            sp.dma_start(gated, GROW[:]).then_inc(scratch_out, 16)
            sp.wait_ge(scratch_out, 32)
            sp.dma_start(btad.rearrange("p h j -> h p j"), bass.AP(bvd.tensor, 127, [[BIAS_L, 8], [-1, 128], [1, 1024]])).then_inc(bias_out, 16)
            sp.dma_start(btbd.rearrange("p h j -> h p j"), bass.AP(bvd.tensor, 8 * BIAS_L + 895, [[BIAS_L, 8], [-1, 128], [1, 256]])).then_inc(bias_out, 16)
            for i in range(ITEMS):
                if i < NT:
                    r = rows_of(i)
                    sp.wait_ge(idx_evac, i + 1)
                    dst = t["sa_ik"] if i == SAMPLE else t["pa_ik"][tcols(i), :]
                    sp.dma_start(dst, NIDX[0:r, i % 2, 256:320]).then_inc(ik_out[i % 2], 16)
                if 1 <= i <= KD:
                    raw_load(KD + i - 1 + 4)
            for p, (c, j, w) in enumerate(PIECES):
                if w[0] == "nat":
                    sp.wait_ge(nat_copied, p + 1)
                elif w[0] == "z":
                    sp.wait_ge(z_pool, ZP.index(p) + 1)
                else:
                    sp.wait_ge(piece_ev, p + 1)
                if w[0] == "nat":
                    r = rows_of(j)
                    sp.dma_start(snat[tcols(j), CW * (c - 1):CW * c], STG[0:r, p % 3, :]).then_inc(stg_out[p % 3], 16)
                else:
                    b = 4 * (c - 4) + w[1]
                    g0, gn = GROUPS[w[2]]
                    sp.dma_start(gz[128 * b:128 * (b + 1), g0:g0 + gn], STG[:, p % 3, 0:gn]).then_inc(stg_out[p % 3], 16)
                if j < KD:
                    raw_load(KD * (c + 1) + j + 4)
                if c == NCH - 1 and j == 0:
                    sp.wait_ge(piece_pe, PEND[NCH - 2])
                    for i in range(3):
                        sp.wait_ge(stg_out[i], 16 * (PEND[3] // 3))
                    for tt in range(2):
                        sp.dma_start(QKV[:, tt, :], snat[tcols(tt), :]).then_inc(qkv_in[tt], 16)
                    for dst, src in ((t["pa_v"], snat[0:SEQ, 640:768]), (t["sa_v"], snat[SEQ:TOK, 640:768]),
                                     (t["pb_v"], snat[SEQ - WIN:SEQ, 1408:1536]),
                                     (t["sb_v"][0:WIN - DEC, :], t["cache_bv"][DEC:WIN, :]),
                                     (t["sb_v"][WIN - DEC:WIN, :], snat[SEQ:TOK, 1408:1536]),
                                     (t["sb_k"][0:WIN - DEC, :], t["cache_bk"][DEC:WIN, :])):
                        sp.dma_start(dst, src).then_inc(copy_out, 16)
            sp.wait_ge(bias_out, 32)
            sp.wait_ge(mask_done, NT)
            sp.wait_ge(piece_pe, NP)
            vp = snat[0:SEQ, :].rearrange("(n p) c -> p n c", p=128)
            sp.dma_start(BTA[:, :, 896:1024], btad[:, :, 896:1024]).then_inc(kva_in, 16)
            sp.dma_start(VA[:, 0:2, :], vp[:, 0:2, 640:768]).then_inc(kva_in, 16)
            sp.dma_start(BTB[:], btbd).then_inc(kvb_in, 16)
            sp.dma_start(VB[:], vp[:, :, 1408:1536]).then_inc(kvb_in, 16)
            sp.wait_ge(kvb_in, 32)
            for dst, src in ((VA[:, 2:8, :], vp[:, 2:8, 640:768]), (BTA[:, :, 0:896], btad[:, :, 0:896]),
                             (CK[:, 0:4, :], t["cache_ak"].rearrange("(n p) c -> p n c", p=128)), (CK[:, 4, :], t["cache_bk"]),
                             (VAS[:, 0:4, :], t["cache_av"].rearrange("(n p) c -> p n c", p=128)),
                             (VAS[0:DEC, 4, :], snat[SEQ:TOK, 640:768]),
                             (VBS[:, 0, :], t["cache_bv"]), (VBS[0:DEC, 1, :], snat[SEQ:TOK, 1408:1536])):
                sp.dma_start(dst, src).then_inc(rest_in, 16)
            for i in range(3):
                sp.wait_ge(stg_out[i], 16 * NST[i])
            wo_v = t["w_o"].rearrange("(k p) n -> p k n", p=128)
            att_v = attd.rearrange("(k p) n -> p k n", p=128)
            wout_v = t["w_out"].rearrange("(k p) n -> p k n", p=128)

            def o_load(j):
                if j >= KD:
                    return
                if j >= 2:
                    sp.wait_ge(ow_lo, j - 1)
                sp.dma_start(ORAW[:, j % 2, :, :], wo_v[:, :, 128 * j:128 * (j + 1)]).then_inc(oraw_in[j % 2], 16)

            def z_load(g):
                for i in range(2):
                    sp.wait_ge(att_out[i], 16 * min(3 * (g + 1), NT))
                g0, gn = GROUPS[g]
                sp.dma_start(ZST[g][:], att_v[:, :, g0:g0 + gn]).then_inc(z_in[g], 16)

            def early_loads():
                sp.wait_ge(qs_lo, NT)
                sp.wait_ge(tr_pe, TIDX[("K", SAMPLE, 1)] + 1)
                sp.wait_ge(k_out, 16 * k_stores(SAMPLE))
                sp.wait_ge(xn4_ready, NT)
                z_load(0)
                z_load(1)
                for j in range(2):
                    o_load(j)

            for s in range(S0, S1):
                if s == NU - 14:
                    early_loads()
                tt = prep(s, LOAD_AT)
                if tt is not None and tt >= 2:
                    sp.wait_ge(xg_ready, tt - 1)
                    sp.dma_start(QKV[0:rows_of(tt), tt % 2, :], snat[tcols(tt), :]).then_inc(qkv_in[tt % 2], 16)
                if s % 8 == 0 and 8 <= s < NU + 8:
                    g = s // 8 - 1
                    if g >= 1:
                        wait_evac(sp, TIDX[("A", (g - 1) // 2, (g - 1) % 2)])
                    sp.dma_start(ZT[:, :, 0:rows_of(g // 2)],
                                 gz[512 * (g % 2):512 * (g % 2) + 512, tcols(g // 2)].rearrange("(b p) n -> p b n", p=128)).then_inc(zt_in, 16)
                tt = prep(s, SPLIT_AT)
                if tt is not None:
                    r = rows_of(tt)
                    sp.wait_ge(xn4_ready, tt + 1)
                    dst = t["sa_k"] if tt == SAMPLE else t["pa_k"][tcols(tt), :]
                    sp.dma_start(dst, XNB[0:r, 8:10, :]).then_inc(k_out, 16)
                    if tt == SAMPLE:
                        sp.dma_start(t["sb_k"][WIN - DEC:WIN, :], XNB[0:r, 18:20, :]).then_inc(k_out, 16)
                    if tt == SAMPLE - 1:
                        sp.dma_start(t["pb_k"], XNB[0:r, 18:20, :]).then_inc(k_out, 16)
                for x in TP.get(s - 1, []):
                    if x[0] == "A":
                        tt, br = x[1], x[2]
                        g = 2 * tt + br
                        wait_evac(sp, TIDX[x])
                        sp.dma_start(attd[512 * br:512 * (br + 1), tcols(tt)].rearrange("(b p) n -> p b n", p=128),
                                     ATS[:, g % 2, :, 0:rows_of(tt)]).then_inc(att_out[g % 2], 16)
            z_load(2)
            for j in range(2):
                sp.dma_start(GATE[:, j, :], bass.AP(gated.tensor, 128 * j, [[0, 128], [256, KD], [1, 128]])).then_inc(gate_in, 16)
            for i in range(3 * KD):
                j, g = i // 3, i % 3
                if i >= 3:
                    sp.wait_ge(m_dve, i - 2)
                g0, gn = GROUPS[g]
                for b in range(2):
                    sp.dma_start(GT[:, i % 3, b, 0:gn], gz[D * (1 + b) + 128 * j:D * (1 + b) + 128 * (j + 1), g0:g0 + gn]).then_inc(g_in[i % 3], 16)
                if g == 2:
                    o_load(j + 2)
                if g == 1 and 2 <= j < 6:
                    q = j - 2
                    if q >= 2:
                        sp.wait_ge(u_lo, 2 * (q - 1))
                    sp.dma_start(UQ[q % 2][:], wout_v[:, 2 * q:2 * q + 2, 0:YW]).then_inc(uq_in[q % 2], 16)
            sp.wait_ge(o_pe, 3 * KD)

            def u_load(c):
                if c >= 3:
                    sp.wait_ge(u_lo, KD * (c - 1))
                sp.dma_start(URAW[c % 2][:], wout_v[:, :, YW * c:YW * (c + 1)]).then_inc(uraw_in[c % 2], 16)

            def x_load(i):
                if i >= NYC * NT:
                    return
                c, tt = i // NT, i % NT
                if i >= 3:
                    sp.wait_ge(y_add, i - 2)
                src = t["x_sample"] if tt == SAMPLE else t["x_prompt"][tcols(tt), :]
                sp.dma_start(XR[0:rows_of(tt), i % 3, :], src[:, YW * c:YW * (c + 1)]).then_inc(xr_in[i % 3], 16)

            for i in range(3):
                x_load(i)
            u_load(1)
            u_load(2)
            for i in range(NYC * NT):
                c, tt = i // NT, i % NT
                if i == NT + 4:
                    u_load(3)
                x_load(i + 3)
                sp.wait_ge(y_add, i + 1)
                dst = t["y_sample"] if tt == SAMPLE else t["y_prompt"][tcols(tt), :]
                sp.dma_start(dst[:, YW * c:YW * (c + 1)], YO[0:rows_of(tt), i % 3, :]).then_inc(y_out[i % 3], 16)
            for i in range(3):
                sp.wait_ge(y_out[i], 16 * NYC * NT // 3)
            sp.wait_ge(ik_out[0], 16 * 5)
            sp.wait_ge(ik_out[1], 16 * 4)
            sp.wait_ge(copy_out, 16 * 6)
            sp.wait_ge(k_out, 16 * k_stores(SAMPLE))

        def u_low(pool, c):
            for k in range(KD):
                pool.wait_ge(u_hi, KD * c + k + 1)
                nc.gpsimd.tensor_tensor(UL[c][:, k, :], URAW[c % 2][:, k, :], UH[c][:, k, :].bitcast(F32), ALU.subtract).then_inc(u_lo, 1)

        @block.gpsimd
        def _(pool):
            def w_lo(n):
                c, k = n // KD, n % KD
                if c >= NCH:
                    return
                cw = CHUNKS[c][2]
                pool.wait_ge(hi_done, n + 1)
                nc.gpsimd.tensor_tensor(WL[c % 2][:, k, 0:cw], RAW[:, n % 4, 0:cw],
                                        WH[c % 2][:, k, 0:cw].bitcast(F32), ALU.subtract).then_inc(lo_done, 1)

            for n in range(KD):
                w_lo(n)
            for i in range(ITEMS):
                slot = IN2[i % 2]
                r = rows_of(i) if i < NT else 128
                pool.wait_ge(idx_hi, i + 1)
                if i < NT:
                    nc.gpsimd.tensor_tensor(slot[0:r, 0:4, 1, :], NIDX[0:r, i % 2, 0:256].rearrange("p (h d) -> p h d", h=4),
                                            slot[0:r, 0:4, 0, :].bitcast(F32), ALU.subtract)
                    k_nat = NIDX[0:r, i % 2, 256:320]
                else:
                    k_nat = CIK[:, i - NT, :]
                for b in range(2):
                    last = nc.gpsimd.tensor_tensor(slot[0:r, 5, b, :], k_nat, slot[0:r, 4, 0, :].bitcast(F32), ALU.subtract)
                last.then_inc(idx_lo, 1)
                if 1 <= i <= KD:
                    w_lo(KD + i - 1)
            for p, (c, j, w) in enumerate(PIECES):
                if w[0] == "z":
                    z = ZP.index(p)
                    gn = GROUPS[w[2]][1]
                    pool.wait_ge(piece_ev, p + 1)
                    if p >= 3:
                        pool.wait_ge(stg_out[p % 3], 16 * (p // 3))
                    nc.gpsimd.tensor_tensor(STG[:, p % 3, 0:gn], ZS[:, z % 2, 0:gn], ZC[:, z % 2, 0:gn], ALU.mult).then_inc(z_pool, 1)
                if j < KD:
                    w_lo(KD * (c + 1) + j)
            pool.wait_ge(z_pool, len(ZP))
            pool.wait_ge(rms_ready, 1)
            for s in range(S0, S1):
                tt = prep(s, NORM_AT)
                if tt is not None:
                    r = rows_of(tt)
                    q = QKV[0:r, tt % 2, :]
                    pool.wait_ge(qkv_in[tt % 2], 16 * (tt // 2 + 1))
                    for g, (c0, h0, n) in enumerate(((0, 0, 8), (512, 8, 2), (768, 10, 8), (1280, 18, 2))):
                        last = nc.gpsimd.tensor_tensor(
                            XG[0:r, h0:h0 + n, :], q[:, c0:c0 + 64 * n].rearrange("p (h d) -> p h d", h=n),
                            GAM[0:r, g:g + 1, :].broadcast_to([r, n, HD]), ALU.mult)
                    last.then_inc(xg_ready, 1)
                    pool.wait_ge(xg_ready, tt + 1)
                    if tt >= 1:
                        pool.wait_ge(k_out, 16 * k_stores(tt - 1))
                        pool.wait_ge(qs_lo, tt)
                    nc.gpsimd.tensor_tensor(XNB[0:r, :, :], XG[0:r, :, :],
                                            RYQ[0:r, 20 * tt:20 * tt + 20].unsqueeze(2).broadcast_to([r, 20, HD]), ALU.mult).then_inc(xn4_ready, 1)
                tt = prep(s, SPLIT_AT)
                if tt is not None:
                    r = rows_of(tt)
                    pool.wait_ge(qs_hi, tt + 1)
                    for br in range(2):
                        nc.gpsimd.tensor_tensor(QS[0:r, 8 * br:8 * br + 8, 1, :], XNB[0:r, 10 * br:10 * br + 8, :],
                                                QS[0:r, 8 * br:8 * br + 8, 0, :].bitcast(F32), ALU.subtract)
                    for b in range(2):
                        for br in range(2):
                            last = nc.gpsimd.tensor_tensor(KS[0:r, 2 * br:2 * br + 2, 2 + b, :], XNB[0:r, 10 * br + 8:10 * br + 10, :],
                                                           KS[0:r, 2 * br:2 * br + 2, 0, :].bitcast(F32), ALU.subtract)
                    last.then_inc(qs_lo, 1)
                if s in CACHE_STEP:
                    i = CACHE_STEP[s]
                    pool.wait_ge(cache_hi, i + 1)
                    for b in range(2):
                        last = nc.gpsimd.tensor_tensor(KSC[:, :, 2 + b, :], CK[:, i, :].rearrange("p (h d) -> p h d", h=2),
                                                       KSC[:, :, 0, :].bitcast(F32), ALU.subtract)
                    last.then_inc(cache_lo, 1)
            for j in range(2):
                pool.wait_ge(ow_hi, j + 1)
                nc.gpsimd.tensor_tensor(WOL[j % 2][:], ORAW[:, j % 2, :, :], WOH[j % 2][:].bitcast(F32), ALU.subtract).then_inc(ow_lo, 1)
            for i in range(3 * KD):
                j, g = i // 3, i % 3
                g0, gn = GROUPS[g]
                pool.wait_ge(m_hi, i + 1)
                nc.gpsimd.tensor_tensor(ML[:, j, g0:g0 + gn], TM[:, i % 2, 2, 0:gn], MH[:, j, g0:g0 + gn].bitcast(F32), ALU.subtract).then_inc(m_lo, 1)
                if g == 2 and j + 2 < KD:
                    pool.wait_ge(ow_hi, j + 3)
                    nc.gpsimd.tensor_tensor(WOL[j % 2][:], ORAW[:, j % 2, :, :], WOH[j % 2][:].bitcast(F32), ALU.subtract).then_inc(ow_lo, 1)
                if g == 1 and 2 <= j < 6:
                    q = j - 2
                    pool.wait_ge(u_hi, 2 * (q + 1))
                    nc.gpsimd.tensor_tensor(UL[0][:, 2 * q:2 * q + 2, :], UQ[q % 2][:], UH[0][:, 2 * q:2 * q + 2, :].bitcast(F32), ALU.subtract).then_inc(u_lo, 2)
            u_low(pool, 1)
            for i in range(NYC * NT):
                c, tt = i // NT, i % NT
                if tt == 4 and c + 2 < NYC:
                    u_low(pool, c + 2)
                r = rows_of(tt)
                pool.wait_ge(y_mul, i + 1)
                pool.wait_ge(xr_in[i % 3], 16 * (i // 3 + 1))
                if i >= 3:
                    pool.wait_ge(y_out[i % 3], 16 * (i // 3))
                nc.gpsimd.tensor_tensor(YO[0:r, i % 3, :], YT[0:r, i % 3, :], XR[0:r, i % 3, :], ALU.add).then_inc(y_add, 1)

        @block.scalar
        def _(act):
            def w_hi(n):
                c, k = n // KD, n % KD
                if c >= NCH:
                    return
                cw = CHUNKS[c][2]
                act.wait_ge(raw_in[n % 4], 16 * (n // 4 + 1))
                if k == 0 and c == 2:
                    act.wait_ge(idx_pe, NT)
                if k == 0 and c >= 3:
                    act.wait_ge(piece_pe, PEND[c - 2])
                nc.scalar.activation(WH[c % 2][:, k, 0:cw], RAW[:, n % 4, 0:cw], ACT.Copy).then_inc(hi_done, 1)

            act.wait_ge(consts_in, 16 * N_SMALL)
            nc.scalar.activation(CG[:], CS[:], ACT.Sigmoid).then_inc(c_sig, 1)
            for q in range(2 * NT):
                tt, half = q // 2, q % 2
                r = rows_of(tt)
                act.wait_ge(xt_pe, q + 1)
                nc.scalar.activation(XT[:, 4 * half:4 * half + 4, tcols(tt)],
                                     bank(q % 2).rearrange("p (k n) -> p k n", k=4)[:, :, 0:r], ACT.Copy).then_inc(xt_evac, 1)
            for n in range(KD):
                w_hi(n)
            act.wait_ge(ada_done, 1)
            nc.scalar.copy(MROW[:, D:2 * D], PS[0:2, 4:6, :].rearrange("p b n -> p (b n)")).then_inc(mrow_act, 1)
            for k in range(KD):
                act.wait_ge(h_ready, k + 1)
                nc.scalar.activation(HH[:, k, :], XT[:, k, :], ACT.Copy).then_inc(hh_done, 1)
            def relus(tt):
                for h in range(4):
                    n = SHEADS.index((tt, h))
                    r, nk = rows_of(tt), keys_of(tt)
                    act.wait_ge(score_pe, n + 1)
                    v = PS[0:r, 4 + 2 * (n % 2):6 + 2 * (n % 2), :].rearrange("p b n -> p (b n)")[:, 0:nk]
                    nc.scalar.activation(v, v, ACT.Relu, scale=HD ** -0.5 * 0.5).then_inc(relu_done, 1)

            for i in range(ITEMS + 1):
                if i < NT:
                    r = rows_of(i)
                    act.wait_ge(idx_pe, i + 1)
                    if i >= 2:
                        act.wait_ge(ik_out[i % 2], 16 * (i // 2))
                        act.wait_ge(idx_lo, i - 1)
                    nc.scalar.activation(NIDX[0:r, i % 2, :], bank(i % 2)[0:r, 0:IDX_W], ACT.Copy).then_inc(idx_evac, 1)
                if 1 <= i <= KD:
                    w_hi(KD + i - 1)
                if i >= 1:
                    j = i - 1
                    r = rows_of(j) if j < NT else 128
                    act.wait_ge(idx_t, j + 1)
                    if j < NT:
                        nc.scalar.activation(IQT[:, :, tcols(j)], bank(2).rearrange("p (h n) -> p h n", h=4)[:, :, 0:r], ACT.Copy)
                    if j < SAMPLE:
                        dst = IKT[:, :, tcols(j)]
                    elif j == SAMPLE:
                        dst = IKTS[:, :, PAST:PAST + DEC]
                    else:
                        dst = IKTS[:, :, 128 * (j - NT):128 * (j - NT + 1)]
                    nc.scalar.activation(dst, bank(3)[:, 0:256].rearrange("p (h n) -> p h n", h=2)[:, :, 0:r], ACT.Copy).then_inc(idx_tev, 1)
                    if 2 <= j < SAMPLE:
                        relus(j)
            relus(SAMPLE)
            def high_parts(tt):
                r = rows_of(tt)
                act.wait_ge(xn4_ready, tt + 1)
                if tt >= 1:
                    act.wait_ge(tr_pe, TIDX[("K", tt - 1, 1)] + 1)
                    act.wait_ge(qs_lo, tt)
                for b in range(2):
                    nc.scalar.activation(QS[0:r, 8 * b:8 * b + 8, 0, :], XNB[0:r, 10 * b:10 * b + 8, :], ACT.Copy)
                    for d in range(2):
                        last = nc.scalar.activation(KS[0:r, 2 * b:2 * b + 2, d, :], XNB[0:r, 10 * b + 8:10 * b + 10, :], ACT.Copy)
                last.then_inc(qs_hi, 1)

            def nat_evac(c, j, p):
                r = rows_of(j)
                nc.scalar.activation(STG[0:r, p % 3, :], bank(p % 4)[0:r, :], ACT.Copy).then_inc(nat_copied, 1)
                act.wait_ge(nat_copied, p + 1)
                blocks = [b for b in range(8) if (8 * (c - 1) + b) % 12 < 10]
                for b in blocks:
                    f = 8 * (c - 1) + b
                    head = 10 * (f // 12) + f % 12
                    v = bank(p % 4)[0:r, HD * b:HD * (b + 1)]
                    last = nc.scalar.activation(v, v, ACT.Square, accum_out=SSQ[0:r, 20 * j + head:20 * j + head + 1])
                last.then_inc(piece_ev, 1)

            for p, (c, j, w) in enumerate(PIECES):
                act.wait_ge(piece_pe, p + 1)
                if w[0] != "z" and p >= 3:
                    act.wait_ge(stg_out[p % 3], 16 * (p // 3))
                if w[0] == "nat":
                    nat_evac(c, j, p)
                else:
                    gn = GROUPS[w[2]][1]
                    if w[0] == "g":
                        nc.scalar.activation(STG[:, p % 3, 0:gn], bank(p % 4)[:, 0:gn], ACT.Sigmoid).then_inc(piece_ev, 1)
                    else:
                        z = ZP.index(p)
                        if z >= 2:
                            act.wait_ge(z_pool, z - 1)
                        nc.scalar.activation(ZS[:, z % 2, 0:gn], bank(p % 4)[:, 0:gn], ACT.Sigmoid)
                        nc.scalar.activation(ZC[:, z % 2, 0:gn], bank(p % 4)[:, 0:gn], ACT.Copy).then_inc(piece_ev, 1)
                if j < KD:
                    w_hi(KD * (c + 1) + j)
                if c == NCH - 1 and j == 9:
                    high_parts(0)
            for s in range(S0, S1):
                if s == 0:
                    act.wait_ge(kva_in, 32)
                    act.wait_ge(mask_done, NT)
                if s == 16:
                    act.wait_ge(rest_in, 128)
                for x in TP[s]:
                    if EV[TIDX[x]] == "S":
                        t_evac(act, nc.scalar.copy, x, tev_act)
                if 0 <= s < NU:
                    u = s
                    tt, br, h = UNITS[u]
                    r, nk = rows_of(tt), unit_keys(u)
                    act.wait_ge(min_done, u + 1)
                    if u >= 3:
                        act.wait_ge(tr_pe, last_t(u - 3) + 1)
                    nc.scalar.activation(PB[u % 3][0:r, 0:nk], LG[u % 2][0:r, 0:nk], ACT.Exp, scale=-1.0,
                                         bias=NM[0:r, br, h:h + 1], accum_out=DEN[0:r, br, h:h + 1]).then_inc(exp_done, 1)
                if s % 16 == 0 and 16 <= s <= NU:
                    g = s // 16 - 1
                    act.wait_ge(sink_sum, g + 1)
                    nc.scalar.activation(ES[0:rows_of(g), 0, :], SD[0:rows_of(g), :], ACT.Exp).then_inc(sink_act, 1)
                tt = prep(s, SPLIT_AT)
                if tt is not None and tt >= 1:
                    high_parts(tt)
                if s in CACHE_STEP:
                    i = CACHE_STEP[s]
                    if i >= 1:
                        act.wait_ge(tr_pe, TIDX[("C", i - 1, 0)] + 1)
                    for d in range(2):
                        last = nc.scalar.activation(KSC[:, :, d, :], CK[:, i, :].rearrange("p (h d) -> p h d", h=2), ACT.Copy)
                    last.then_inc(cache_hi, 1)
            act.wait_ge(oraw_in[0], 16)
            act.wait_ge(qk_pe, NU)
            nc.scalar.activation(WOH[0][:], ORAW[:, 0, :, :], ACT.Copy).then_inc(ow_hi, 1)
            act.wait_ge(pv_pe, NU)
            for g in range(3):
                g0, gn = GROUPS[g]
                act.wait_ge(z_in[g], 16)
                for half in range(2):
                    ks = slice(4 * half, 4 * half + 4)
                    nc.scalar.activation(ZH[:, ks, g0:g0 + gn], ZST[g][:, ks, :], ACT.Copy).then_inc(az_hi, 1)
                if g == 1:
                    act.wait_ge(oraw_in[1], 16)
                    nc.scalar.activation(WOH[1][:], ORAW[:, 1, :, :], ACT.Copy).then_inc(ow_hi, 1)
            for i in range(3 * KD):
                j, g = i // 3, i % 3
                g0, gn = GROUPS[g]
                act.wait_ge(m_dve, i + 1)
                nc.scalar.activation(MH[:, j, g0:g0 + gn], TM[:, i % 2, 2, 0:gn], ACT.Copy).then_inc(m_hi, 1)
                if g == 2 and j + 2 < KD:
                    act.wait_ge(oraw_in[j % 2], 16 * (j // 2 + 2))
                    act.wait_ge(o_pe, i + 1)
                    nc.scalar.activation(WOH[j % 2][:], ORAW[:, j % 2, :, :], ACT.Copy).then_inc(ow_hi, 1)
                if g == 1 and 2 <= j < 6:
                    q = j - 2
                    act.wait_ge(uq_in[q % 2], 16 * (q // 2 + 1))
                    nc.scalar.activation(UH[0][:, 2 * q:2 * q + 2, :], UQ[q % 2][:], ACT.Copy).then_inc(u_hi, 2)
            for c in range(1, NYC):
                act.wait_ge(uraw_in[c % 2], 16 * ((c + 1) // 2))
                for k in range(KD):
                    nc.scalar.activation(UH[c][:, k, :], URAW[c % 2][:, k, :], ACT.Copy).then_inc(u_hi, 1)

        @block.vector
        def _(dve):
            V = nc.vector
            steps = [0]

            def link(ins):
                steps[0] += 1
                ins.then_inc(dve_step, 1)
                dve.wait_ge(dve_step, steps[0])

            dve.wait_ge(consts_in, 16 * N_SMALL)
            V.tensor_copy(IDR[:], IDF[:])
            V.tensor_copy(IDB[:], IDF[:]).then_inc(ident_ready, 1)
            V.tensor_scalar(NSINK[:], SINK[:], -1.0, None, ALU.mult)
            dve.wait_ge(c_sig, 1)
            V.tensor_tensor(CSIL[:], CS[:], CG[:], ALU.mult).then_inc(c_ready, 1)
            link(V.memset(SS[:], 1.0))
            V.memset(SSQ[:], 1.0)
            for i in range(3):
                n = min(512, BIAS_L - 512 * i)
                dve.wait_ge(bias_pe, i + 1)
                V.tensor_scalar(BV[:, 512 * i:512 * i + n], bank(5 + i)[0:16, 0:n], -1.0, None, ALU.mult).then_inc(bias_sb, 1)
            for a, b in ((0, 4), (4, NT)):
                for tt in range(a, b):
                    r = rows_of(tt)
                    dve.wait_ge(x_in[tt], 16)
                    link(V.tensor_tensor_reduce(out=SQJ[0:r, :], in0=XNAT[tt][0:r, :], in1=XNAT[tt][0:r, :], scale=1.0,
                                                scalar=0.0, op0=ALU.mult, op1=ALU.add, accum_out=SS[0:r, tt:tt + 1]))
                rsqrt_chain(link, RY[:, a:b], SS[:, a:b], RV[:, a:b], RI[:, a:b], RT[:, a:b], 1.0 / D)
                for tt in range(a, b):
                    r = rows_of(tt)
                    V.tensor_scalar(XNAT[tt][0:r, :], XNAT[tt][0:r, :], RY[0:r, tt:tt + 1], None, ALU.mult).then_inc(xn_ready, 1)
            dve.wait_ge(ada_done, 1)
            V.tensor_copy(MROW[:, 0:D], PS[0:2, 2:4, :].rearrange("p b n -> p (b n)")).then_inc(mrow_ready, 1)
            V.tensor_copy(MROWG[:, :], PS[0:2, 6:8, :].rearrange("p b n -> p (b n)")).then_inc(mrow_ready, 1)
            dve.wait_ge(mod_pe, 1)
            V.tensor_tensor(MOD[:], bank(0)[:, 0:48].rearrange("p (c j) -> p c j", j=2),
                            BADA[:].unsqueeze(2).broadcast_to([128, 24, 2]), ALU.add).then_inc(mod_ready, 1)
            dve.wait_ge(mod_ready, 1)
            steps[0] += 1
            V.scalar_tensor_tensor(out=SCL[:], in0=MOD[:, 8:16, :], scalar=1.0, in1=NG[:].unsqueeze(2).broadcast_to([128, KD, 2]),
                                   op0=ALU.add, op1=ALU.mult).then_inc(dve_step, 1)
            dve.wait_ge(dve_step, steps[0])
            dve.wait_ge(xt_evac, 2 * NT)

            def h_low(k):
                dve.wait_ge(hh_done, k + 1)
                V.tensor_tensor(HL[:, k, :], XT[:, k, :], HH[:, k, :].bitcast(F32), ALU.subtract).then_inc(hl_done, 1)

            for k in range(KD):
                V.tensor_scalar(XT[:, k, 0:SEQ], XT[:, k, 0:SEQ], SCL[:, k, 0:1], MOD[:, k, 0:1], ALU.mult, ALU.add)
                V.tensor_scalar(XT[:, k, SEQ:TOK], XT[:, k, SEQ:TOK], SCL[:, k, 1:2], MOD[:, k, 1:2], ALU.mult, ALU.add).then_inc(h_ready, 1)
                if k >= 1:
                    h_low(k - 1)
            h_low(KD - 1)
            dve.wait_ge(gate_pe, 1)
            V.tensor_copy(GROW[:], bank(7)[0:16, 0:128]).then_inc(gate_rows, 1)
            def scores(tt):
                r, nk = rows_of(tt), keys_of(tt)
                out = SC[0:r, SOFF[tt]:SOFF[tt] + nk]
                for h in range(4):
                    n = SHEADS.index((tt, h))
                    v = PS[0:r, 4 + 2 * (n % 2):6 + 2 * (n % 2), :].rearrange("p b n -> p (b n)")[:, 0:nk]
                    dve.wait_ge(relu_done, n + 1)
                    if h == 0:
                        last = V.tensor_scalar(out, v, IW[0:r, tt, 0:1], None, ALU.mult)
                    else:
                        dve.wait_ge(acc_done, n)
                        last = V.scalar_tensor_tensor(out=out, in0=v, scalar=IW[0:r, tt, h:h + 1], in1=out, op0=ALU.mult, op1=ALU.add)
                    last.then_inc(acc_done, 1)
                if tt != SAMPLE:
                    dve.wait_ge(acc_done, SHEADS.index((tt, 3)) + 1)
                    link(V.memset(SC[0:CHUNK, SOFF[tt] + nk - CHUNK:SOFF[tt] + nk], -NEG_BIG))

            for i in range(ITEMS + 1):
                if i < ITEMS:
                    slot = IN2[i % 2]
                    r = rows_of(i) if i < NT else 128
                    if i >= 2:
                        dve.wait_ge(idx_t, i - 1)
                    if i < NT:
                        dve.wait_ge(idx_evac, i + 1)
                        V.tensor_copy(slot[0:r, 0:4, 0, :], NIDX[0:r, i % 2, 0:256].rearrange("p (h d) -> p h d", h=4))
                        V.tensor_copy(IW[0:r, i, :], NIDX[0:r, i % 2, 320:324])
                        k_nat = NIDX[0:r, i % 2, 256:320]
                    else:
                        k_nat = CIK[:, i - NT, :]
                    V.tensor_copy(slot[0:r, 4, :, :], k_nat.unsqueeze(1).broadcast_to([r, 2, HD])).then_inc(idx_hi, 1)
                if 2 <= i - 1 < SAMPLE:
                    scores(i - 1)
            scores(SAMPLE)
            dve.wait_ge(acc_done, len(SHEADS))
            def pick_rounds(tiles, rounds, unroll):
                n = len(tiles)
                with dve.Fori(0, rounds // unroll):
                    for un in range(unroll):
                        for a, tt in enumerate(tiles):
                            r, w = rows_of(tt), SC[0:rows_of(tt), SOFF[tt]:SOFF[tt] + keys_of(tt)]
                            if un > 0:
                                dve.wait_ge(sel_step, 2 * n * un - n + a + 1)
                            V.max(M8[0:r, a, :], w).then_inc(sel_step, 1)
                        for a, tt in enumerate(tiles):
                            r, w = rows_of(tt), SC[0:rows_of(tt), SOFF[tt]:SOFF[tt] + keys_of(tt)]
                            dve.wait_ge(sel_step, 2 * n * un + a + 1)
                            V.match_replace(w, M8[0:r, a, :], w, TAKEN).then_inc(sel_step, 1)
                    dve.wait_ge(sel_step, 2 * n * unroll)
                    dve.sem_clear(sel_step)
                for tt in tiles:
                    mask(tt)

            def mask(tt):
                r, nk = rows_of(tt), keys_of(tt)
                V.tensor_scalar(MASK[0:r, MOFF[tt]:MOFF[tt] + nk], SC[0:r, SOFF[tt]:SOFF[tt] + nk],
                                -2.0e38, NEG_BIG, ALU.is_gt, ALU.mult).then_inc(mask_done, 1)

            for tt in range(2):
                nk = keys_of(tt)
                link(V.memset(MASK[:, MOFF[tt]:MOFF[tt] + nk], 0.0))
                V.memset(MASK[0:CHUNK, MOFF[tt] + nk - CHUNK:MOFF[tt] + nk], NEG_BIG).then_inc(mask_done, 1)
            for pair in ((2, 3), (4, 5), (6, 7)):
                pick_rounds(pair, KSEL // 8, 4)
            dve.wait_ge(piece_ev, PEND[3])
            rsqrt_chain(link, RYQ[:], SSQ[:], RVQ[:], RIQ[:], RTQ[:], 1.0 / HD)
            ry = RYQ[:].rearrange("p (t h) -> p t h", h=10)[:, :, 0:8]
            V.tensor_scalar(ry, ry, -HD ** -0.5, None, ALU.mult).then_inc(rms_ready, 1)
            pick_rounds((SAMPLE,), KSEL_S // 8, 3)
            for s in range(S0, S1):
                if s == 0:
                    dve.wait_ge(kva_in, 32)
                    dve.wait_ge(mask_done, NT)
                if s == 6:
                    dve.wait_ge(kvb_in, 32)
                    V.memset(BTB[0:CHUNK, :, 192:256], NEG_BIG)
                    link(V.memset(BTB[CHUNK:128, :, 0:64], NEG_BIG))
                if s == 16:
                    dve.wait_ge(rest_in, 128)
                if 0 <= s < NU:
                    u = s
                    tt, br, h = UNITS[u]
                    r, nk = rows_of(tt), unit_keys(u)
                    if br == 0:
                        j0 = 384 if tt == SAMPLE else 896 - 128 * tt
                        bias, init = BTA[0:r, h, j0:j0 + nk], 3.0e38
                    else:
                        j0 = 128 if tt == 0 else 0
                        bias, init = BTB[0:r, h, j0:j0 + nk], NSINK[0:r, h:h + 1]
                    dve.wait_ge(qk_pe, u + 1)
                    if u >= 2:
                        dve.wait_ge(exp_done, u - 1)
                    v = PS[0:r, 2 * (u % 2):2 * (u % 2) + 2, :].rearrange("p b n -> p (b n)")[:, 0:nk]
                    V.tensor_tensor_reduce(out=LG[u % 2][0:r, 0:nk], in0=v, in1=bias, scale=1.0, scalar=init,
                                           op0=ALU.add, op1=ALU.min, accum_out=NM[0:r, br, h:h + 1]).then_inc(min_done, 1)
                if s % 16 == 0 and 16 <= s <= NU:
                    g = s // 16 - 1
                    r = rows_of(g)
                    dve.wait_ge(min_done, 16 * (g + 1))
                    if g >= 1:
                        dve.wait_ge(sink_act, g)
                    V.tensor_tensor(SD[0:r, :], NM[0:r, 1, :], SINK[0:r, :], ALU.add).then_inc(sink_sum, 1)
                for x in TP[s]:
                    if EV[TIDX[x]] == "V":
                        t_evac(dve, V.tensor_copy, x, tev_dve)
                if (s - 11) % 8 == 0 and 11 <= s <= NU + 3:
                    g = (s - 11) // 8
                    tt, br = g // 2, g % 2
                    r = rows_of(tt)
                    dve.wait_ge(exp_done, 8 * (g + 1))
                    if br:
                        dve.wait_ge(sink_act, tt + 1)
                        link(V.tensor_tensor(DEN[0:r, 1, :], DEN[0:r, 1, :], ES[0:r, 0, :], ALU.add))
                    link(V.reciprocal(RDEN[0:r, :], DEN[0:r, br, :]))
                    dve.wait_ge(pv_pe, 8 * (g + 1))
                    if g >= 2:
                        dve.wait_ge(tr_pe, TIDX[("A", (g - 2) // 2, br)] + 1)
                    V.tensor_tensor(ATTN[br][0:r, :].rearrange("p (h d) -> p h d", h=8),
                                    bank(6 + br)[0:r, :].rearrange("p (h d) -> p h d", h=8),
                                    RDEN[0:r, :].unsqueeze(2).broadcast_to([r, 8, HD]), ALU.mult).then_inc(att_done, 1)
            for q in range(6):
                g, ks = q // 2, slice(4 * (q % 2), 4 * (q % 2) + 4)
                g0, gn = GROUPS[g]
                dve.wait_ge(az_hi, q + 1)
                V.tensor_tensor(ZL[:, ks, g0:g0 + gn], ZST[g][:, ks, :], ZH[:, ks, g0:g0 + gn].bitcast(F32), ALU.subtract).then_inc(az_lo, 1)
            for i in range(3 * KD):
                j, g = i // 3, i % 3
                gn = GROUPS[g][1]
                dve.wait_ge(o_pe, i + 1)
                dve.wait_ge(g_in[i % 3], 32 * (i // 3 + 1))
                if i >= 2:
                    dve.wait_ge(m_lo, i - 1)
                V.tensor_tensor(TM[:, i % 2, 0, 0:gn], bank(2 * (i % 2))[:, 0:gn], GT[:, i % 3, 0, 0:gn], ALU.mult)
                link(V.tensor_tensor(TM[:, i % 2, 1, 0:gn], bank(2 * (i % 2) + 1)[:, 0:gn], GT[:, i % 3, 1, 0:gn], ALU.mult))
                V.tensor_tensor(TM[:, i % 2, 2, 0:gn], TM[:, i % 2, 0, 0:gn], TM[:, i % 2, 1, 0:gn], ALU.add).then_inc(m_dve, 1)
            dve.wait_ge(gate_in, 32)
            for i in range(NYC * NT):
                c, tt = i // NT, i % NT
                r = rows_of(tt)
                dve.wait_ge(y_pe, i + 1)
                if i >= 3:
                    dve.wait_ge(y_add, i - 2)
                V.tensor_tensor(YT[0:r, i % 3, :], bank(4 + i % 3)[0:r, 0:YW],
                                GATE[0:r, int(tt == SAMPLE), YW * c:YW * (c + 1)], ALU.mult).then_inc(y_mul, 1)

        @block.tensor
        def _(pe):
            T = nc.tensor

            def three(out, wh, wl, mh, ml, first, last):
                T.matmul(out, wh, mh, start=first, stop=False)
                T.matmul(out, wh, ml, start=False, stop=False)
                return T.matmul(out, wl, mh, start=False, stop=last)

            pe.wait_ge(consts_in, 16 * N_SMALL)
            for i in range(3):
                n = min(512, BIAS_L - 512 * i)
                T.matmul(bank(5 + i)[0:16, 0:n], RELB[:], ONEH[:, 512 * i:512 * i + n], start=True, stop=True).then_inc(bias_pe, 1)
            for q in range(2 * NT):
                tt, half = q // 2, q % 2
                r = rows_of(tt)
                pe.wait_ge(xn_ready, tt + 1)
                if q >= 2:
                    pe.wait_ge(xt_evac, q - 1)
                for b in range(4):
                    k = 4 * half + b
                    last = T.transpose(bank(q % 2)[:, 128 * b:128 * b + r], XNAT[tt][0:r, 128 * k:128 * (k + 1)], IDF[0:r, 0:r])
                last.then_inc(xt_pe, 1)
            pe.wait_ge(c_ready, 1)
            pe.wait_ge(bias_sb, 3)
            for k in range(KD):
                pe.wait_ge(wada_in[k], 16)
                for c in range(6):
                    last = T.matmul(bank(2 + c)[0:2, :], CSIL[:, k, :], WADA[k][:, 512 * c:512 * (c + 1)],
                                    start=(k == 0), stop=(k == KD - 1))
            last.then_inc(ada_done, 1)
            pe.wait_ge(xt_evac, 2 * NT)
            for c in range(24):
                if c == 0:
                    pe.wait_ge(mrow_ready, 1)
                if c == 8:
                    pe.wait_ge(mrow_act, 1)
                if c == 16:
                    pe.wait_ge(mrow_ready, 2)
                src = MROW[:, 128 * c:128 * (c + 1)] if c < 16 else MROWG[:, 128 * (c - 16):128 * (c - 15)]
                last = T.transpose(bank(0)[:, 2 * c:2 * c + 2], src, IDF[0:2, 0:2])
            last.then_inc(mod_pe, 1)
            def score(tt):
                r, nk = rows_of(tt), keys_of(tt)
                keys = IKTS if tt == SAMPLE else IKT
                for h in range(4):
                    n = SHEADS.index((tt, h))
                    if n >= 2:
                        pe.wait_ge(acc_done, n - 1)
                    for b in range(0, nk, 512):
                        m = min(512, nk - b)
                        out = PS[0:r, 4 + 2 * (n % 2) + b // 512, 0:m]
                        for part in range(2):
                            last = T.matmul(out, IQT[:, h, tcols(tt)], keys[:, part, b:b + m], start=(part == 0), stop=(part == 1))
                    last.then_inc(score_pe, 1)

            pe.wait_ge(mod_ready, 1)
            T.transpose(bank(7)[0:16, 0:128], MOD[:, 16:24, :].rearrange("p k j -> p (k j)"), IDF[:]).then_inc(gate_pe, 1)
            pe.wait_ge(hl_done, KD)
            pe.wait_ge(lo_done, KD)
            pe.wait_ge(ident_ready, 1)
            pe.wait_ge(gate_rows, 1)
            for i in range(ITEMS + 1):
                if i < NT:
                    r = rows_of(i)
                    if i >= 2:
                        pe.wait_ge(idx_evac, i - 1)
                    for k in range(KD):
                        last = three(bank(i % 2)[0:r, 0:IDX_W], HH[:, k, tcols(i)], HL[:, k, tcols(i)],
                                     WH[0][:, k, 0:IDX_W], WL[0][:, k, 0:IDX_W], k == 0, k == KD - 1)
                    last.then_inc(idx_pe, 1)
                if i >= 1:
                    j = i - 1
                    r = rows_of(j) if j < NT else 128
                    pe.wait_ge(idx_lo, j + 1)
                    if j >= 1:
                        pe.wait_ge(idx_tev, j)
                    slot = IN2[j % 2]
                    for h in range(6):
                        if h < 4 and j >= NT:
                            continue
                        dst = bank(2)[:, 128 * h:128 * h + r] if h < 4 else bank(3)[:, 128 * (h - 4):128 * (h - 4) + r]
                        last = T.transpose(dst.bitcast(F32R), slot[0:r, h, :, :].rearrange("p a d -> p (a d)"), IDR[0:r, 0:r])
                    last.then_inc(idx_t, 1)
                    if 2 <= j < SAMPLE:
                        pe.wait_ge(idx_tev, j + 1)
                        score(j)
            pe.wait_ge(idx_tev, ITEMS)
            score(SAMPLE)
            for p, (c, j, w) in enumerate(PIECES):
                if j == 0:
                    pe.wait_ge(lo_done, KD * (c + 1))
                if p >= 4:
                    pe.wait_ge(piece_ev, p - 3)
                H, L = WH[c % 2], WL[c % 2]
                for k in range(KD):
                    if w[0] == "nat":
                        last = three(bank(p % 4)[0:rows_of(j), :], HH[:, k, tcols(j)], HL[:, k, tcols(j)],
                                     H[:, k, :], L[:, k, :], k == 0, k == KD - 1)
                    else:
                        g0, gn = GROUPS[w[2]]
                        bc = slice(128 * w[1], 128 * (w[1] + 1))
                        last = three(bank(p % 4)[:, 0:gn], H[:, k, bc], L[:, k, bc],
                                     HH[:, k, g0:g0 + gn], HL[:, k, g0:g0 + gn], k == 0, k == KD - 1)
                last.then_inc(piece_pe, 1)
            pe.wait_ge(piece_ev, NP)
            pe.wait_ge(mask_done, NT)
            for s in range(S0, S1):
                if s == 0:
                    pe.wait_ge(kva_in, 32)
                if s == 8:
                    pe.wait_ge(kvb_in, 32)
                if s == 16:
                    pe.wait_ge(rest_in, 128)
                if 0 <= s < NU:
                    u = s
                    tt, br, h = UNITS[u]
                    r, nk = rows_of(tt), unit_keys(u)
                    if h == 0:
                        wait_evacs(pe, TIDX[("K", tt, 1)])
                    if u >= 2:
                        pe.wait_ge(min_done, u - 1)
                    if br == 0:
                        keys, k0 = (KTAS if tt == SAMPLE else KTA), 0
                    else:
                        keys, k0 = (KTBS, 0) if tt == SAMPLE else (KTB, 128 * max(tt - 1, 0))
                    for b in range(0, nk, 512):
                        m = min(512, nk - b)
                        out = PS[0:r, 2 * (u % 2) + b // 512, 0:m]
                        for part in range(2):
                            last = T.matmul(out, QT[tt % 2][:, 8 * br + h, 0:r], keys[:, h // 4, part, k0 + b:k0 + b + m],
                                            start=(part == 0), stop=(part == 1 and br == 1))
                        if br == 0:
                            last = T.matmul(out, IDB[0:r, 0:r], MASK[0:r, MOFF[tt] + b:MOFF[tt] + b + m], start=False, stop=True)
                    last.then_inc(qk_pe, 1)
                for x in TP[s]:
                    q = TIDX[x]
                    if q >= 2:
                        wait_evac(pe, q - 2)
                    out = bank(4 + q % 2)
                    if x[0] == "P":
                        u = x[1]
                        tt = UNITS[u][0]
                        r, nk = rows_of(tt), unit_keys(u)
                        pe.wait_ge(exp_done, u + 1)
                        for b in range(4 * x[2], min(4 * x[2] + 4, (nk + 127) // 128)):
                            m = min(128, nk - 128 * b)
                            last = T.transpose(out[0:m, 128 * (b % 4):128 * (b % 4) + r], PB[u % 3][0:r, 128 * b:128 * b + m], IDF[0:r, 0:r])
                    elif x[0] == "A":
                        g, r = 2 * x[1] + x[2], rows_of(x[1])
                        pe.wait_ge(att_done, g + 1)
                        for b in range(4):
                            last = T.transpose(out[:, 128 * b:128 * b + r], ATTN[x[2]][0:r, 128 * b:128 * (b + 1)], IDF[0:r, 0:r])
                    else:
                        if x[0] == "C":
                            r = 128
                            pe.wait_ge(cache_lo, x[1] + 1)
                            src = [KSC[:, kv, 2 * p:2 * p + 2, :] for kv in range(2) for p in range(2)]
                        else:
                            r = rows_of(x[1])
                            pe.wait_ge(qs_lo, x[1] + 1)
                            if x[0] == "Q":
                                src = [QS[0:r, 4 * x[2] + b, :, :] for b in range(4)]
                            else:
                                src = [KS[0:r, 2 * x[2] + kv, 2 * p:2 * p + 2, :] for kv in range(2) for p in range(2)]
                        for b in range(4):
                            last = T.transpose(out[:, 128 * b:128 * b + r].bitcast(F32R), src[b].rearrange("p a d -> p (a d)"), IDR[0:r, 0:r])
                    last.then_inc(tr_pe, 1)
                if 0 <= s - 3 < NU:
                    u = s - 3
                    tt, br, h = UNITS[u]
                    r, nk = rows_of(tt), unit_keys(u)
                    wait_evacs(pe, last_t(u))
                    g = 2 * tt + br
                    if h == 0 and g >= 2:
                        pe.wait_ge(att_done, g - 1)
                    kb = (nk + 127) // 128
                    kv = slice(HD * (h // 4), HD * (h // 4) + HD)
                    for b in range(kb):
                        m = min(128, nk - 128 * b)
                        if br == 0:
                            v = VAS[0:m, b, kv] if tt == SAMPLE else VA[0:m, b, kv]
                        else:
                            v = VBS[0:m, b, kv] if tt == SAMPLE else VB[0:m, max(tt - 1, 0) + b, kv]
                        last = T.matmul(bank(6 + br)[0:r, HD * h:HD * (h + 1)], PT[0:m, u % 2, 128 * b:128 * b + r], v,
                                        start=(b == 0), stop=(b == kb - 1))
                    last.then_inc(pv_pe, 1)
            for i in range(3 * KD):
                j, g = i // 3, i % 3
                g0, gn = GROUPS[g]
                if g == 0:
                    pe.wait_ge(ow_lo, j + 1)
                if i < 3:
                    pe.wait_ge(az_lo, 2 * (i + 1))
                if i >= 2:
                    pe.wait_ge(m_dve, i - 1)
                for b in range(2):
                    for k in range(4 * b, 4 * b + 4):
                        last = three(bank(2 * (i % 2) + b)[:, 0:gn], WOH[j % 2][:, k, :], WOL[j % 2][:, k, :],
                                     ZH[:, k, g0:g0 + gn], ZL[:, k, g0:g0 + gn], k == 4 * b, k == 4 * b + 3)
                last.then_inc(o_pe, 1)
            pe.wait_ge(m_lo, 3 * KD)
            for i in range(NYC * NT):
                c, tt = i // NT, i % NT
                if tt == 0:
                    pe.wait_ge(u_lo, KD * (c + 1))
                if i >= 3:
                    pe.wait_ge(y_mul, i - 2)
                for k in range(KD):
                    last = three(bank(4 + i % 3)[0:rows_of(tt), 0:YW], MH[:, k, tcols(tt)], ML[:, k, tcols(tt)],
                                 UH[c][:, k, :], UL[c][:, k, :], k == 0, k == KD - 1)
                last.then_inc(y_pe, 1)

    return nc


_OUTS = [((1, SEQ, D)), ((1, DEC, D)),
         (1, 1, SEQ, 2, HD), (1, 1, SEQ, 2, HD), (1, 1, SEQ, HD), (1, 1, WIN, 2, HD), (1, 1, WIN, 2, HD),
         (1, 1, DEC, 2, HD), (1, 1, DEC, 2, HD), (1, 1, DEC, HD), (1, 1, WIN, 2, HD), (1, 1, WIN, 2, HD)]
_OUT_NAMES = ["y_prompt", "y_sample", "pa_k", "pa_v", "pa_ik", "pb_k", "pb_v", "sa_k", "sa_v", "sa_ik", "sb_k", "sb_v"]
_OUT_SHAPES = [(SEQ, D), (DEC, D), (SEQ, 128), (SEQ, 128), (SEQ, HD), (WIN, 128), (WIN, 128),
               (DEC, 128), (DEC, 128), (DEC, HD), (WIN, 128), (WIN, 128)]


def kernel(**inputs):
    import numpy as np
    import concourse.bacc as bacc
    from concourse.bass_utils import run_bass_kernel_spmd

    f = np.float32
    x = {n: np.ascontiguousarray(a) for n, a in inputs.items()}
    w_in = x["w_in"][0]
    spans = ((1280, 1604), (0, 768), (1604, 2372), (768, 1280), (2372, 2884), (2884, 4932))

    def cols(v):
        return np.ascontiguousarray(v.reshape(-1, 128).T)

    rel = np.arange(BIAS_L) - (SEQ - 1)
    n = np.abs(rel)
    large = 8 + (np.log(np.maximum(n, 1).astype(f) / f(8)) / f(np.log(128.0)) * f(8)).astype(np.int32)
    bucket = (rel > 0) * 16 + np.where(n < 8, n, np.minimum(large, 15))
    onehot = (np.arange(32)[:, None] == bucket[None, :]).astype(f)
    arrays = {
        "x_prompt": x["x_prompt"][0], "x_sample": x["x_sample"][0],
        "w_all": np.concatenate([w_in[:, a:b] for a, b in spans], axis=1),
        "w_ada": x["w_ada"][0], "w_o": np.concatenate([x["w_oa"][0], x["w_ob"][0]], axis=0), "w_out": x["w_out"][0],
        "cache_ak": x["cache_a_k"].reshape(PAST, 128), "cache_av": x["cache_a_v"].reshape(PAST, 128),
        "cache_ik": x["cache_a_ik"].reshape(PAST, HD),
        "cache_bk": x["cache_b_k"].reshape(WIN, 128), "cache_bv": x["cache_b_v"].reshape(WIN, 128),
        "c_cols": np.ascontiguousarray(np.stack([cols(x["c_prompt"]), cols(x["c_sample"])], axis=2)),
        "ng_cols": cols(x["norm_g"]), "bada_cols": cols(x["b_ada"]),
        "gammas": np.ascontiguousarray(np.broadcast_to(
            np.stack([x[k][0] for k in ("a_q_norm", "a_k_norm", "b_q_norm", "b_k_norm")])[None], (128, 4, HD))),
        "sinks": np.ascontiguousarray(np.broadcast_to(x["b_sinks"], (128, 8))),
        "rel_bias": x["rel_bias"], "ident": np.eye(128, dtype=f), "onehot": onehot,
    }
    nc = bacc.Bacc("TRN2", target_bir_lowering=False, num_devices=1)
    t, ins = {}, {}
    for name, a in arrays.items():
        a = np.ascontiguousarray(a)
        ins[f"in_{name}"] = a
        t[name] = nc.dram_tensor(f"in_{name}", a.shape, mybir.dt.from_np(a.dtype), kind="ExternalInput").ap()
    for name, shape in zip(_OUT_NAMES, _OUT_SHAPES):
        t[name] = nc.dram_tensor(f"out_{name}", shape, F32, kind="ExternalOutput").ap()
    build_program(nc, t)
    r = run_bass_kernel_spmd(nc, [ins], core_ids=[0]).results[0]
    return tuple(np.asarray(r[f"out_{name}"]).reshape(shape) for name, shape in zip(_OUT_NAMES, _OUTS))
```

```python
import concourse.bass as bass
from concourse import mybir
from contextlib import ExitStack

F32 = mybir.dt.float32
F32R = mybir.dt.float32r
BF16 = mybir.dt.bfloat16
I32 = mybir.dt.int32
ALU = mybir.AluOpType
ACT = mybir.ActivationFunctionType
AX = mybir.AxisListType

D = 1024
KD = D // 128
SEQ, DEC, PAST, WIN = 1024, 64, 512, 128
TOK = SEQ + DEC
NT = SEQ // 128 + 1
SAMPLE = NT - 1
HD = 64
CHUNK = 64
IDX_W = 4 * HD + HD + 4
NAT_W = 1536
CW = 512
GROUPS = [(0, 384), (384, 384), (768, 320)]
NEG_BIG = 1e30
TAKEN = -3.0e38
KSEL, KSEL_S = 256, (PAST + DEC) // 4
BIAS_L = 1151
EPS = 1e-6
SBUF0 = 16512


def rows_of(t):
    return DEC if t == SAMPLE else 128


def keys_of(t):
    return PAST + DEC if t == SAMPLE else 128 * (t + 1)


def keys_b(t):
    return WIN + DEC if t == SAMPLE else (128 if t == 0 else 256)


def build_program(nc, t):
    ctx = ExitStack()
    with ctx:
        def at(name, shape, dt, offset):
            return nc.alloc_sbuf_tensor_at(name, shape, dt, offset=SBUF0 + offset)

        def sem(name):
            return ctx.enter_context(nc.semaphore(name))

        PS = ctx.enter_context(nc.psum_tensor("PS", [128, 8, 512], F32))

        def bank(b):
            return PS[:, b, :]

        HH = at("HH", [128, KD, TOK], F32R, 0)
        HL = at("HL", [128, KD, TOK], F32R, 34816)
        WB = 69632
        WH = [at(f"WH{i}", [128, KD, CW], F32R, WB + 32768 * i) for i in range(2)]
        WL = [at(f"WL{i}", [128, KD, CW], F32R, WB + 32768 * i + 16384) for i in range(2)]
        RAW = at("RAW", [128, 4, CW], F32, WB + 65536)
        XB = WB + 65536 + 8192
        XT = at("XT", [128, KD, TOK], F32, XB)
        IQT = at("IQT", [128, 4, TOK], F32R, XB)
        IKT = at("IKT", [128, 2, SEQ], F32R, XB + 17408)
        IKTS = at("IKTS", [128, 2, PAST + DEC], F32R, XB + 25600)
        STG2 = at("STG2", [128, 2, CW], F32, XB + 30208)
        STG = at("STG", [128, 3, CW], F32, XB)
        ZS = at("ZS", [128, 2, 384], F32, XB + 6144)
        ZC = at("ZC", [128, 2, 384], F32, XB + 9216)
        MASK = at("MASK", [128, 5184], BF16, XB + 24448)
        SCB = XB + 34816
        SC = at("SC", [128, 4800], F32, SCB)
        SM = SCB + 19200
        XNAT = [at(f"XN{i}", [128, D], F32, WB + 4096 * i) for i in range(8)] + \
               [at("XN8", [128, D], F32, 61440)]
        WADA = [at(f"WADA{k}", [128, 3 * D], F32, 12288 * k) for k in range(5)] + \
               [at(f"WADA{k}", [128, 3 * D], F32, WB + 32768 + 12288 * (k - 5)) for k in (5, 6)] + \
               [at("WADA7", [128, 3 * D], F32, SCB)]
        ONEH = at("ONEH", [32, BIAS_L], F32, WB + 32768 + 24576)
        BV = at("BV", [16, BIAS_L], F32, SCB + 12288)
        SQJ = at("SQJ", [128, D], F32, 65536)
        MROW = at("MROW", [2, 2 * D], F32, 61440)
        MROWG = at("MROWG", [2, D], F32, WB + 32768 + 24576)
        off = [SM]

        def small(name, shape, dt=F32):
            n = 1
            for s in shape[1:]:
                n *= s
            n *= 2 if dt == BF16 else 4
            h = at(name, shape, dt, off[0])
            off[0] += (n + 31) // 32 * 32
            return h

        IDF = small("IDF", [128, 128])
        IDR = small("IDR", [128, 128], F32R)
        IDB = small("IDB", [128, 128], BF16)
        GAM = small("GAM", [128, 4, HD])
        SINK = small("SINK", [128, 8])
        NSINK = small("NSINK", [128, 8])
        CS = small("CS", [128, KD, 2])
        CG = small("CG", [128, KD, 2])
        CSIL = small("CSIL", [128, KD, 2])
        NG = small("NG", [128, KD])
        BADA = small("BADA", [128, 24])
        RELB = small("RELB", [32, 16])
        MOD = small("MOD", [128, 24, 2])
        SCL = small("SCL", [128, KD, 2])
        SS = small("SS", [128, NT])
        RV = small("RV", [128, NT])
        RI = small("RI", [128, NT], I32)
        RT = small("RT", [128, NT])
        RY = small("RY", [128, NT])
        IW = small("IW", [128, NT, 4])
        GROW = small("GROW", [16, 128])
        M8 = small("M8", [128, 2, 8])
        NM = small("NM", [128, 2, 8])
        DEN = small("DEN", [128, 2, 8])
        ES = small("ES", [128, 2, 8])
        SD = small("SD", [128, 8])
        RDEN = small("RDEN", [128, 8])
        IN2 = [at(f"IN{i}", [128, 6, 2, HD], F32R, off[0] + 3072 * i) for i in range(2)]
        NIDX = at("NIDX", [128, 2, IDX_W], F32, off[0] + 6144)
        CIK = at("CIK", [128, 4, HD], F32, off[0] + 6144 + 2624)
        SSQ = at("SSQ", [128, NT * 20], F32, off[0] + 9792)
        RVQ = at("RVQ", [128, NT * 20], F32, off[0])
        RIQ = at("RIQ", [128, NT * 20], I32, off[0] + 768)
        RTQ = at("RTQ", [128, NT * 20], F32, off[0] + 1536)
        RYQ = at("RYQ", [128, NT * 20], F32, XB + 23552)
        assert SBUF0 + off[0] + 9792 + 720 <= 229344, off[0]
        BTA = at("BTA", [128, 8, 1024], F32, 0)
        BTB = at("BTB", [128, 8, 256], F32, 32768)
        KTA = at("KTA", [128, 2, 2, SEQ], F32R, 40960)
        KTAS = at("KTAS", [128, 2, 2, PAST + DEC], F32R, 57344)
        QKV = at("QKV", [128, 2, NAT_W], F32, WB)
        QS = at("QS", [128, 16, 2, HD], F32R, WB + 12288)
        KS = at("KS", [128, 4, 4, HD], F32R, WB + 20480)
        QT = [at("QT0", [128, 16, 128], F32R, WB + 24576), at("QT1", [128, 16, 128], F32R, WB + 65536)]
        BT0 = at("BT0", [128, 8, 128], F32, WB + 65536)
        VA0 = at("VA0", [128, 128], F32, SCB + 18432)
        KTB = at("KTB", [128, 2, 2, SEQ], F32R, 102400)
        KTBS = at("KTBS", [128, 2, 2, WIN + DEC], F32R, 118784)
        VA = at("VA", [128, 8, 128], F32, 121856)
        VAS = at("VAS", [128, 5, 128], F32, 125952)
        VB = at("VB", [128, 8, 128], F32, 128512)
        VBS = at("VBS", [128, 2, 128], F32, 132608)
        XNB = at("XNB", [128, 20, HD], F32, XB + 6144)
        XG = at("XG", [128, 20, HD], F32, XB + 12288)
        LG = [at("LG0", [128, 1024], F32, XB), at("LG1", [128, 1024], F32, XB + 17408)]
        ATTN = [at("ATTN0", [128, 512], F32, XB + 4096), at("ATTN1", [128, 512], F32, 67584)]
        PB = [at("PB0", [128, 1024], F32, SCB), at("PB1", [128, 1024], F32, SCB + 4096), at("PB2", [128, 1024], F32, off[0] + 4096)]
        ZT = at("ZT", [128, 4, 128], F32, XB + 21504)
        PT = at("PT", [128, 2, 1024], F32, SCB + 8192)
        KSC = at("KSC", [128, 2, 4, HD], F32R, SCB + 16384)
        ATS = at("ATS", [128, 2, 4, 128], F32, off[0])
        CK = at("CK", [128, 5, 128], F32, off[0] + 8192)
        ZH = at("ZH", [128, KD, TOK], F32R, 0)
        ZL = at("ZL", [128, KD, TOK], F32R, 34816)
        MH = at("MH", [128, KD, TOK], F32R, 69632)
        ML = at("ML", [128, KD, TOK], F32R, 104448)
        ZST = [at(f"ZST{g}", [128, KD, GROUPS[g][1]], F32, (WB, WB + 12288, 122880)[g]) for g in range(3)]
        WOH = [at("WOH0", [128, KD, 128], F32R, 135168), at("WOH1", [128, KD, 128], F32R, XB)]
        WOL = [at("WOL0", [128, KD, 128], F32R, 139264), at("WOL1", [128, KD, 128], F32R, XB + 4096)]
        ORAW = at("ORAW", [128, 2, KD, 128], F32, XB + 8192)
        GT = at("GT", [128, 3, 2, 384], F32, XB + 16384)
        TM = at("TM", [128, 2, 3, 384], F32, XB + 25600)
        GATE = at("GATE", [128, 2, D], F32, SCB)
        YW = 256
        NYC = D // YW
        UH = [at("UH0", [128, KD, YW], F32R, SCB + 8192)] + \
             [at(f"UH{i}", [128, KD, YW], F32R, 16384 * (i - 1)) for i in range(1, NYC)]
        UL = [at("UL0", [128, KD, YW], F32R, off[0])] + \
             [at(f"UL{i}", [128, KD, YW], F32R, 16384 * (i - 1) + 8192) for i in range(1, NYC)]
        UQ = [at("UQ0", [128, 2, YW], F32, SCB + 16384), at("UQ1", [128, 2, YW], F32, off[0] + 8192)]
        URAW = [at(f"URAW{i}", [128, KD, YW], F32, XB + 8192 * i) for i in range(2)]
        XR = at("XR", [128, 3, YW], F32, 57344)
        YT = at("YT", [128, 3, YW], F32, 57344 + 3072)
        YO = at("YO", [128, 3, YW], F32, 57344 + 6144)

        snat = nc.dram_tensor("snat", [TOK, NAT_W], F32).ap()
        gz = nc.dram_tensor("gz", [3 * D, TOK], F32).ap()
        attd = nc.dram_tensor("attd", [D, TOK], F32).ap()
        btad = nc.dram_tensor("btad", [128, 8, 1024], F32).ap()
        btbd = nc.dram_tensor("btbd", [128, 8, 256], F32).ap()
        bvd = nc.dram_tensor("bvd", [16, BIAS_L], F32).ap()
        gated = nc.dram_tensor("gated", [2 * KD, 128], F32).ap()

        consts_in = sem("consts_in")
        c_in = sem("c_in")
        cik_in = sem("cik_in")
        x_in = [sem(f"x_in{i}") for i in range(NT)]
        wada_in = [sem(f"wada_in{k}") for k in range(KD)]
        raw_in = [sem(f"raw_in{i}") for i in range(4)]
        ident_ready = sem("ident_ready")
        c_sig = sem("c_sig")
        c_ready = sem("c_ready")
        dve_step = sem("dve_step")
        xn_ready = sem("xn_ready")
        xt_pe = sem("xt_pe")
        xt_evac = sem("xt_evac")
        ada_done = sem("ada_done")
        bias_pe = sem("bias_pe")
        bias_sb = sem("bias_sb")
        mrow_act = sem("mrow_act")
        mrow_ready = sem("mrow_ready")
        mod_pe = sem("mod_pe")
        mod_ready = sem("mod_ready")
        gate_pe = sem("gate_pe")
        gate_rows = sem("gate_rows")
        scratch_out = sem("scratch_out")
        bias_out = sem("bias_out")
        h_ready = sem("h_ready")
        hh_done = sem("hh_done")
        hl_done = sem("hl_done")
        hi_done = sem("hi_done")
        lo_done = sem("lo_done")
        idx_pe = sem("idx_pe")
        idx_evac = sem("idx_evac")
        idx_hi = sem("idx_hi")
        idx_lo = sem("idx_lo")
        idx_t = sem("idx_t")
        idx_tev = sem("idx_tev")
        ik_out = [sem(f"ik_out{i}") for i in range(2)]
        score_pe = sem("score_pe")
        relu_done = sem("relu_done")
        acc_done = sem("acc_done")
        sel_step = sem("sel_step")
        mask_done = sem("mask_done")
        piece_pe = sem("piece_pe")
        piece_ev = sem("piece_ev")
        nat_copied = sem("nat_copied")
        z_pool = sem("z_pool")
        stg2_out = [sem(f"stg2_out{i}") for i in range(2)]
        stg_out = [sem(f"stg_out{i}") for i in range(3)]
        kva_in = sem("kva_in")
        kvb_in = sem("kvb_in")
        kvc_in = sem("kvc_in")
        rest_in = sem("rest_in")
        bta_in = sem("bta_in")
        zt_in = sem("zt_in")
        qkv_in = [sem(f"qkv_in{i}") for i in range(2)]
        rms_ready = sem("rms_ready")
        xg_ready = sem("xg_ready")
        xn4_ready = sem("xn4_ready")
        qs_hi = sem("qs_hi")
        qs_lo = sem("qs_lo")
        k_out = sem("k_out")
        copy_out = sem("copy_out")
        cache_hi = sem("cache_hi")
        cache_lo = sem("cache_lo")
        qk_pe = sem("qk_pe")
        min_done = sem("min_done")
        exp_done = sem("exp_done")
        tr_pe = sem("tr_pe")
        tev_dve = sem("tev_dve")
        tev_act = sem("tev_act")
        pv_pe = sem("pv_pe")
        sink_sum = sem("sink_sum")
        sink_act = sem("sink_act")
        att_done = sem("att_done")
        att_out = [sem(f"att_out{i}") for i in range(2)]
        z_in = [sem(f"z_in{i}") for i in range(3)]
        uq_in = [sem(f"uq_in{i}") for i in range(2)]
        az_hi = sem("az_hi")
        az_lo = sem("az_lo")
        oraw_in = [sem(f"oraw_in{i}") for i in range(2)]
        ow_hi = sem("ow_hi")
        ow_lo = sem("ow_lo")
        g_in = [sem(f"g_in{i}") for i in range(3)]
        o_pe = sem("o_pe")
        m_dve = sem("m_dve")
        m_hi = sem("m_hi")
        m_lo = sem("m_lo")
        gate_in = sem("gate_in")
        uraw_in = [sem(f"uraw_in{i}") for i in range(2)]
        u_hi = sem("u_hi")
        u_lo = sem("u_lo")
        xr_in = [sem(f"xr_in{i}") for i in range(3)]
        y_pe = sem("y_pe")
        y_mul = sem("y_mul")
        y_add = sem("y_add")
        y_out = [sem(f"y_out{i}") for i in range(3)]

        SOFF = {}
        o = 0
        for tt in range(2, NT):
            SOFF[tt] = o
            o += keys_of(tt)
        MOFF = {}
        o = 0
        for tt in range(NT):
            MOFF[tt] = o
            o += keys_of(tt)

        PARTS = [(0, 256), (256, 640), (640, TOK)]

        def tcols(tt):
            return slice(128 * tt, 128 * tt + rows_of(tt))

        CHUNKS = [("idx", 0, IDX_W)]
        CHUNKS += [("nat", IDX_W + CW * i, CW) for i in range(NAT_W // CW)]
        CHUNKS += [("z", IDX_W + NAT_W + CW * i, CW) for i in range(2)]
        CHUNKS += [("g", IDX_W + NAT_W + D + CW * i, CW) for i in range(4)]
        NCH = len(CHUNKS)
        PIECES = []
        for c in range(1, NCH):
            if CHUNKS[c][0] == "nat":
                PIECES += [(c, j, ("nat", j)) for j in range(NT)]
            else:
                PIECES += [(c, j, (CHUNKS[c][0], j // 3, j % 3)) for j in range(12)]
        NP = len(PIECES)
        PEND = [len([1 for c, _, _ in PIECES if c <= e]) for e in range(NCH)]
        ZP = [p for p, (c, j, w) in enumerate(PIECES) if w[0] == "z"]
        NAT0 = 4
        STG_Q = [p - NT for p in range(NP)]
        NST = [len([q for q in STG_Q if q >= 0 and q % 3 == i]) for i in range(3)]

        W_FIRST = 4

        def ibank(i):
            return (0, 1, 4, 5)[i] if i < NAT0 else 0

        def pbank(p):
            return (1, 1, 1, 1, 1, 0, 1, 0, 1)[p] if p < NT else (p - 7) % 4

        ITEMS = NT + PAST // 128
        EARLY_ROUNDS = 8
        SCORED = [tt for tt in range(2, NT)]
        SHEADS = [(tt, h) for tt in SCORED for h in range(4)]

        UNITS = [(tt, br, h) for tt in range(NT) for br in range(2) for h in range(8)]
        NU = len(UNITS)

        OPROJ = [(0, 0), (0, 1), (1, 0), (1, 1), (0, 2), (1, 2)] + [(j, g) for j in range(2, KD) for g in range(3)]

        def unit_keys(u):
            tt, br, _ = UNITS[u]
            return keys_b(tt) if br else keys_of(tt)

        S0, S1 = -23, NU + 9
        TP = {s: [] for s in range(S0, S1)}
        for s in range(S0, S1):
            if 0 <= s - 2 < NU:
                for j in range((unit_keys(s - 2) + 511) // 512):
                    TP[s].append(("P", s - 2, j))
        for tt in range(NT):
            base = 16 * (tt - 1)
            for j in range(4):
                TP[base + 9 + j].append(("Q", tt, j))
            for j in range(2):
                TP[base + 13 + j].append(("K", tt, j))
        for i in range(5):
            TP[16 * (2 + i) + 6].append(("C", i, 0))
        for g in range(2 * NT):
            TP[8 * g + 15].append(("A", g // 2, g % 2))
        TQ = [(s, x) for s in range(S0, S1) for x in TP[s]]
        TIDX = {x: q for q, (_, x) in enumerate(TQ)}
        EARLY_T = 4
        assert all(TQ[n][1] == ("Q", 0, n) for n in range(EARLY_T))
        PREP0 = {16 * (tt - 1): tt for tt in range(NT)}
        CACHE_STEP = {16 * (2 + i): i for i in range(5)}
        LOAD_AT, NORM_AT, SPLIT_AT = -7, -5, 2

        def prep(s, after):
            return PREP0.get(s - after)

        def k_stores(tt):
            return tt + 1 + (tt >= SAMPLE - 1) + (tt >= SAMPLE)

        EV = []
        for q, (_, x) in enumerate(TQ):
            if x[0] == "A":
                EV.append("V")
            elif x[0] == "P" and unit_keys(x[1]) > 512:
                EV.append("SV"[x[2]])
            else:
                EV.append("V" if EV.count("V") <= EV.count("S") else "S")

        def evacs(q):
            return EV[:q + 1].count("V"), EV[:q + 1].count("S")

        def wait_evacs(eng, q):
            v, a = evacs(q)
            if v:
                eng.wait_ge(tev_dve, v)
            if a:
                eng.wait_ge(tev_act, a)

        def wait_evac(eng, q):
            eng.wait_ge(tev_dve if EV[q] == "V" else tev_act, evacs(q)[EV[q] == "S"])

        def last_t(u):
            return TIDX[("P", u, (unit_keys(u) + 511) // 512 - 1)]

        def t_evac(eng, copy, x, done):
            q = TIDX[x]
            eng.wait_ge(tr_pe, q + 1)
            src = bank(4 + q % 2).rearrange("p (b n) -> p b n", b=4)
            if x[0] == "P":
                u, j = x[1], x[2]
                r, nk = rows_of(UNITS[u][0]), unit_keys(u) - 512 * j
                full, part = min(4, nk // 128), nk % 128 if nk < 512 else 0
                dst = PT[:, u % 2, 512 * j:512 * (j + 1)].rearrange("p (b n) -> p b n", b=4)
                if u >= 2:
                    eng.wait_ge(pv_pe, u - 1)
                if full:
                    last = copy(dst[:, 0:full, 0:r], src[:, 0:full, 0:r])
                if part:
                    last = copy(dst[0:part, full, 0:r], src[0:part, full, 0:r])
            elif x[0] == "Q":
                if x[1] == 1:
                    eng.wait_ge(min_done, 8)
                if x[1] >= 2:
                    eng.wait_ge(qk_pe, 16 * (x[1] - 1))
                r = rows_of(x[1])
                last = copy(QT[x[1] % 2][:, 4 * x[2]:4 * x[2] + 4, 0:r], src[:, :, 0:r])
            elif x[0] == "A":
                g, r = 2 * x[1] + x[2], rows_of(x[1])
                if g >= 2:
                    eng.wait_ge(att_out[g % 2], 16 * (g // 2))
                eng.wait_ge(zt_in, 16 * (g + 1))
                last = nc.vector.tensor_tensor(ATS[:, g % 2, :, 0:r], src[:, :, 0:r], ZT[:, :, 0:r], ALU.mult)
            else:
                if x[0] == "C":
                    dst = KTAS[:, :, :, 128 * x[1]:128 * (x[1] + 1)] if x[1] < 4 else KTBS[:, :, :, 0:WIN]
                elif x[1] == SAMPLE:
                    dst = KTBS[:, :, :, WIN:WIN + DEC] if x[2] else KTAS[:, :, :, PAST:PAST + DEC]
                else:
                    dst = (KTB if x[2] else KTA)[:, :, :, tcols(x[1])]
                r = rows_of(x[1]) if x[0] == "K" else 128
                last = copy(dst, bank(4 + q % 2).rearrange("p (a b n) -> p a b n", a=2, b=2)[:, :, :, 0:r])
            last.then_inc(done, 1)

        def rsqrt_chain(link, out, ss, v, i, tmp, scale):
            link(nc.vector.tensor_scalar(v, ss, scale, EPS, ALU.mult, ALU.add))
            link(nc.vector.tensor_scalar(i, v.bitcast(I32), 1, None, ALU.arith_shift_right))
            link(nc.vector.tensor_scalar(i, i, -1.0, float(0x5F3759DF), ALU.mult, ALU.add))
            for step in range(3):
                y = out if step else i.bitcast(F32)
                link(nc.vector.tensor_tensor(tmp, y, y, ALU.mult))
                link(nc.vector.tensor_tensor(tmp, tmp, v, ALU.mult))
                link(nc.vector.tensor_scalar(tmp, tmp, -0.5, 1.5, ALU.mult, ALU.add))
                link(nc.vector.tensor_tensor(out, y, tmp, ALU.mult))

        w_all_v = t["w_all"].rearrange("(k p) n -> p k n", p=128)
        N_SMALL = 7
        block = ctx.enter_context(nc.Block())

        @block.sync
        def _(sp):
            def raw_load(n):
                c, k = n // KD, n % KD
                if c >= NCH:
                    return
                if n >= 4:
                    sp.wait_ge(lo_done, n - 3)
                _, c0, cw = CHUNKS[c]
                sp.dma_start(RAW[:, n % 4, 0:cw], w_all_v[:, k, c0:c0 + cw]).then_inc(raw_in[n % 4], 16)

            def wada_load(k):
                sp.dma_start(WADA[k][:], t["w_ada"][128 * k:128 * (k + 1), :]).then_inc(wada_in[k], 16)

            def xn_load(tt):
                src = t["x_sample"] if tt == SAMPLE else t["x_prompt"][tcols(tt), :]
                sp.dma_start(XNAT[tt][0:rows_of(tt), :], src).then_inc(x_in[tt], 16)

            sp.dma_start(CS[:], t["c_cols"]).then_inc(c_in, 16)
            wada_load(0)
            for dst, src in ((IDF[:], t["ident"]), (NG[:], t["ng_cols"]),
                             (BADA[:], t["bada_cols"]), (RELB[:], t["rel_bias"]), (ONEH[:], t["onehot"]),
                             (GAM[:], t["gammas"]), (SINK[:], t["sinks"])):
                sp.dma_start(dst, src).then_inc(consts_in, 16)
            wada_load(1)
            wada_load(2)
            for k, tiles in ((3, range(0, 4)), (4, range(4, NT)), (5, ()), (6, ()), (7, ())):
                for tt in tiles:
                    xn_load(tt)
                wada_load(k)
            sp.dma_start(CIK[:], t["cache_ik"].rearrange("(n p) c -> p n c", p=128)).then_inc(cik_in, 16)
            for n in range(4):
                raw_load(n)
            sp.wait_ge(bias_sb, 3)
            sp.dma_start(bvd, BV[:, :]).then_inc(scratch_out, 16)
            for n in range(4, 2 * KD):
                raw_load(n)
            sp.wait_ge(gate_rows, 1)
            sp.dma_start(gated, GROW[:]).then_inc(scratch_out, 16)
            for i in range(ITEMS):
                if i < NT:
                    r = rows_of(i)
                    sp.wait_ge(idx_evac, i + 1)
                    dst = t["sa_ik"] if i == SAMPLE else t["pa_ik"][tcols(i), :]
                    sp.dma_start(dst, NIDX[0:r, i % 2, 256:320]).then_inc(ik_out[i % 2], 16)
                j = i - NAT0
                if 0 <= j < NT:
                    sp.wait_ge(nat_copied, j + 1)
                    sp.dma_start(snat[tcols(j), 0:CW], STG2[0:rows_of(j), j % 2, :]).then_inc(stg2_out[j % 2], 16)
                if i < 4:
                    raw_load(2 * KD + i)
                if i >= NT:
                    for n in range(2):
                        raw_load(2 * KD + 4 + 2 * (i - NT) + n)
            for p, (c, j, w) in enumerate(PIECES):
                if c == 1:
                    continue
                q = STG_Q[p]
                if w[0] == "nat":
                    sp.wait_ge(nat_copied, p + 1)
                elif w[0] == "z":
                    sp.wait_ge(z_pool, ZP.index(p) + 1)
                else:
                    sp.wait_ge(piece_ev, p + 1)
                if w[0] == "nat":
                    r = rows_of(j)
                    sp.dma_start(snat[tcols(j), CW * (c - 1):CW * c], STG[0:r, q % 3, :]).then_inc(stg_out[q % 3], 16)
                else:
                    b = 4 * (c - 4) + w[1]
                    g0, gn = GROUPS[w[2]]
                    sp.dma_start(gz[128 * b:128 * (b + 1), g0:g0 + gn], STG[:, q % 3, 0:gn]).then_inc(stg_out[q % 3], 16)
                if j < KD:
                    raw_load(KD * (c + 1) + j + 4)
                if c == 3:
                    if j == 0:
                        sp.wait_ge(scratch_out, 32)
                    if j < 4:
                        sp.dma_start(btad[:, 2 * j:2 * j + 2, :].rearrange("p h j -> h p j"),
                                     bass.AP(bvd.tensor, 2 * BIAS_L * j + 127, [[BIAS_L, 2], [-1, 128], [1, 1024]])).then_inc(bias_out, 16)
                    elif j == 4:
                        sp.dma_start(btbd.rearrange("p h j -> h p j"), bass.AP(bvd.tensor, 8 * BIAS_L + 895, [[BIAS_L, 8], [-1, 128], [1, 256]])).then_inc(bias_out, 16)
                if c == NCH - 1 and j == 0:
                    sp.wait_ge(piece_pe, PEND[NCH - 2])
                    for i in range(3):
                        sp.wait_ge(stg_out[i], 16 * ((PEND[3] - NT) // 3))
                    for i in range(2):
                        sp.wait_ge(stg2_out[i], 16 * ((NT + 1 - i) // 2))
                    for tt in range(2):
                        sp.dma_start(QKV[:, tt, :], snat[tcols(tt), :]).then_inc(qkv_in[tt], 16)
                    for dst, src in ((t["pa_v"], snat[0:SEQ, 640:768]), (t["sa_v"], snat[SEQ:TOK, 640:768]),
                                     (t["pb_v"], snat[SEQ - WIN:SEQ, 1408:1536]),
                                     (t["sb_v"][0:WIN - DEC, :], t["cache_bv"][DEC:WIN, :]),
                                     (t["sb_v"][WIN - DEC:WIN, :], snat[SEQ:TOK, 1408:1536]),
                                     (t["sb_k"][0:WIN - DEC, :], t["cache_bk"][DEC:WIN, :])):
                        sp.dma_start(dst, src).then_inc(copy_out, 16)
                if c == NCH - 1 and j == 9:
                    sp.wait_ge(bias_out, 16 * 5)
                    sp.wait_ge(lo_done, KD * NCH)
                    sp.dma_start(BT0[:], btad[:, :, 896:1024]).then_inc(kva_in, 16)
                    sp.wait_ge(mask_done, NT)
                    sp.dma_start(VA0[:], snat[0:128, 640:768]).then_inc(kva_in, 16)
                if c == NCH - 1 and j == 8:
                    sp.wait_ge(xn4_ready, 1)
                    sp.dma_start(t["pa_k"][tcols(0), :], XNB[:, 8:10, :]).then_inc(k_out, 16)
            sp.wait_ge(piece_pe, NP)
            vp = snat[0:SEQ, :].rearrange("(n p) c -> p n c", p=128)
            sp.dma_start(BTB[:], btbd).then_inc(kvb_in, 16)
            sp.dma_start(VB[:], vp[:, :, 1408:1536]).then_inc(kvb_in, 16)
            sp.dma_start(BTA[:, :, 768:1024], btad[:, :, 768:1024]).then_inc(kvc_in, 16)
            sp.dma_start(VA[:], vp[:, :, 640:768]).then_inc(kvc_in, 16)
            for dst, src in ((CK[:, 0:4, :], t["cache_ak"].rearrange("(n p) c -> p n c", p=128)), (CK[:, 4, :], t["cache_bk"]),
                             (VAS[:, 0:4, :], t["cache_av"].rearrange("(n p) c -> p n c", p=128)),
                             (VAS[0:DEC, 4, :], snat[SEQ:TOK, 640:768]),
                             (VBS[:, 0, :], t["cache_bv"]), (VBS[0:DEC, 1, :], snat[SEQ:TOK, 1408:1536])):
                sp.dma_start(dst, src).then_inc(rest_in, 16)
            for i in range(3):
                sp.wait_ge(stg_out[i], 16 * NST[i])
            wo_v = t["w_o"].rearrange("(k p) n -> p k n", p=128)
            att_v = attd.rearrange("(k p) n -> p k n", p=128)
            wout_v = t["w_out"].rearrange("(k p) n -> p k n", p=128)

            def o_load(j):
                if j >= KD:
                    return
                if j >= 2:
                    sp.wait_ge(ow_lo, j - 1)
                sp.dma_start(ORAW[:, j % 2, :, :], wo_v[:, :, 128 * j:128 * (j + 1)]).then_inc(oraw_in[j % 2], 16)

            def z_load(g):
                for i in range(2):
                    sp.wait_ge(att_out[i], 16 * min(3 * (g + 1), NT))
                g0, gn = GROUPS[g]
                sp.dma_start(ZST[g][:], att_v[:, :, g0:g0 + gn]).then_inc(z_in[g], 16)

            def g_load(i):
                j, g = OPROJ[i]
                g0, gn = GROUPS[g]
                for b in range(2):
                    sp.dma_start(GT[:, i % 3, b, 0:gn], gz[D * (1 + b) + 128 * j:D * (1 + b) + 128 * (j + 1), g0:g0 + gn]).then_inc(g_in[i % 3], 16)

            def early_loads():
                sp.wait_ge(qs_lo, NT)
                sp.wait_ge(tr_pe, TIDX[("K", SAMPLE, 1)] + 1)
                sp.wait_ge(k_out, 16 * k_stores(SAMPLE))
                sp.wait_ge(xn4_ready, NT)
                z_load(0)
                z_load(1)
                for j in range(2):
                    o_load(j)

            for s in range(S0, S1):
                if s == NU - 14:
                    early_loads()
                if s == NU + 1:
                    sp.wait_ge(exp_done, NU)
                    g_load(0)
                if s == 10:
                    sp.dma_start(BTA[:, :, 0:768], btad[:, :, 0:768]).then_inc(bta_in, 16)
                tt = prep(s, LOAD_AT)
                if tt is not None and tt >= 2:
                    sp.wait_ge(xg_ready, tt - 1)
                    sp.dma_start(QKV[0:rows_of(tt), tt % 2, :], snat[tcols(tt), :]).then_inc(qkv_in[tt % 2], 16)
                if s % 8 == 0 and 8 <= s < NU + 8:
                    g = s // 8 - 1
                    if g >= 1:
                        wait_evac(sp, TIDX[("A", (g - 1) // 2, (g - 1) % 2)])
                    sp.dma_start(ZT[:, :, 0:rows_of(g // 2)],
                                 gz[512 * (g % 2):512 * (g % 2) + 512, tcols(g // 2)].rearrange("(b p) n -> p b n", p=128)).then_inc(zt_in, 16)
                tt = prep(s, SPLIT_AT)
                if tt is not None:
                    r = rows_of(tt)
                    if tt >= 1:
                        sp.wait_ge(xn4_ready, tt + 1)
                        dst = t["sa_k"] if tt == SAMPLE else t["pa_k"][tcols(tt), :]
                        sp.dma_start(dst, XNB[0:r, 8:10, :]).then_inc(k_out, 16)
                    if tt == SAMPLE:
                        sp.dma_start(t["sb_k"][WIN - DEC:WIN, :], XNB[0:r, 18:20, :]).then_inc(k_out, 16)
                    if tt == SAMPLE - 1:
                        sp.dma_start(t["pb_k"], XNB[0:r, 18:20, :]).then_inc(k_out, 16)
                for x in TP.get(s - 1, []):
                    if x[0] == "A":
                        tt, br = x[1], x[2]
                        g = 2 * tt + br
                        wait_evac(sp, TIDX[x])
                        sp.dma_start(attd[512 * br:512 * (br + 1), tcols(tt)].rearrange("(b p) n -> p b n", p=128),
                                     ATS[:, g % 2, :, 0:rows_of(tt)]).then_inc(att_out[g % 2], 16)
            z_load(2)
            for i in range(3 * KD):
                j, g = OPROJ[i]
                if i >= 3:
                    sp.wait_ge(m_dve, i - 2)
                if i >= 1:
                    g_load(i)
                if i == 6:
                    for b in range(2):
                        sp.dma_start(GATE[:, b, :], bass.AP(gated.tensor, 128 * b, [[0, 128], [256, KD], [1, 128]])).then_inc(gate_in, 16)
                if g == 2:
                    o_load(j + 2)
                if g == 1 and 2 <= j < 6:
                    q = j - 2
                    if q >= 2:
                        sp.wait_ge(u_lo, 2 * (q - 1))
                    sp.dma_start(UQ[q % 2][:], wout_v[:, 2 * q:2 * q + 2, 0:YW]).then_inc(uq_in[q % 2], 16)
            sp.wait_ge(o_pe, 3 * KD)

            def u_load(c):
                if c >= 3:
                    sp.wait_ge(u_lo, KD * (c - 1))
                sp.dma_start(URAW[c % 2][:], wout_v[:, :, YW * c:YW * (c + 1)]).then_inc(uraw_in[c % 2], 16)

            def x_load(i):
                if i >= NYC * NT:
                    return
                c, tt = i // NT, i % NT
                if i >= 3:
                    sp.wait_ge(y_add, i - 2)
                src = t["x_sample"] if tt == SAMPLE else t["x_prompt"][tcols(tt), :]
                sp.dma_start(XR[0:rows_of(tt), i % 3, :], src[:, YW * c:YW * (c + 1)]).then_inc(xr_in[i % 3], 16)

            for i in range(3):
                x_load(i)
            u_load(1)
            u_load(2)
            for i in range(NYC * NT):
                c, tt = i // NT, i % NT
                if i == NT + 4:
                    u_load(3)
                x_load(i + 3)
                sp.wait_ge(y_add, i + 1)
                dst = t["y_sample"] if tt == SAMPLE else t["y_prompt"][tcols(tt), :]
                sp.dma_start(dst[:, YW * c:YW * (c + 1)], YO[0:rows_of(tt), i % 3, :]).then_inc(y_out[i % 3], 16)
            for i in range(3):
                sp.wait_ge(y_out[i], 16 * NYC * NT // 3)
            sp.wait_ge(ik_out[0], 16 * 5)
            sp.wait_ge(ik_out[1], 16 * 4)
            sp.wait_ge(copy_out, 16 * 6)
            sp.wait_ge(k_out, 16 * k_stores(SAMPLE))

        def u_low(pool, c):
            for k in range(KD):
                pool.wait_ge(u_hi, KD * c + k + 1)
                nc.gpsimd.tensor_tensor(UL[c][:, k, :], URAW[c % 2][:, k, :], UH[c][:, k, :].bitcast(F32), ALU.subtract).then_inc(u_lo, 1)

        @block.gpsimd
        def _(pool):
            def w_lo(n):
                c, k = n // KD, n % KD
                if c >= NCH:
                    return
                cw = CHUNKS[c][2]
                pool.wait_ge(hi_done, n + 1)
                nc.gpsimd.tensor_tensor(WL[c % 2][:, k, 0:cw], RAW[:, n % 4, 0:cw],
                                        WH[c % 2][:, k, 0:cw].bitcast(F32), ALU.subtract).then_inc(lo_done, 1)

            for n in range(KD):
                w_lo(n)
            pool.wait_ge(mod_pe, 1)
            for n in range(KD, KD + W_FIRST):
                w_lo(n)
            for i in range(ITEMS):
                slot = IN2[i % 2]
                r = rows_of(i) if i < NT else 128
                pool.wait_ge(idx_hi, i + 1)
                if i < NT:
                    nc.gpsimd.tensor_tensor(slot[0:r, 0:4, 1, :], NIDX[0:r, i % 2, 0:256].rearrange("p (h d) -> p h d", h=4),
                                            slot[0:r, 0:4, 0, :].bitcast(F32), ALU.subtract)
                    k_nat = NIDX[0:r, i % 2, 256:320]
                else:
                    k_nat = CIK[:, i - NT, :]
                for b in range(2):
                    last = nc.gpsimd.tensor_tensor(slot[0:r, 5, b, :], k_nat, slot[0:r, 4, 0, :].bitcast(F32), ALU.subtract)
                last.then_inc(idx_lo, 1)
                if i < KD - W_FIRST:
                    w_lo(KD + W_FIRST + i)
                if i >= NT:
                    for n in range(2):
                        w_lo(2 * KD + 2 * (i - NT) + n)
            for p, (c, j, w) in enumerate(PIECES):
                if c == 1:
                    continue
                if w[0] == "z":
                    z = ZP.index(p)
                    q = STG_Q[p]
                    gn = GROUPS[w[2]][1]
                    pool.wait_ge(piece_ev, p + 1)
                    pool.wait_ge(stg_out[q % 3], 16 * (q // 3))
                    nc.gpsimd.tensor_tensor(STG[:, q % 3, 0:gn], ZS[:, z % 2, 0:gn], ZC[:, z % 2, 0:gn], ALU.mult).then_inc(z_pool, 1)
                if j < KD:
                    w_lo(KD * (c + 1) + j)
            pool.wait_ge(z_pool, len(ZP))
            pool.wait_ge(rms_ready, 1)
            for s in range(S0, S1):
                tt = prep(s, NORM_AT)
                if tt is not None:
                    r = rows_of(tt)
                    q = QKV[0:r, tt % 2, :]
                    pool.wait_ge(qkv_in[tt % 2], 16 * (tt // 2 + 1))
                    for g, (c0, h0, n) in enumerate(((0, 0, 8), (512, 8, 2), (768, 10, 8), (1280, 18, 2))):
                        last = nc.gpsimd.tensor_tensor(
                            XG[0:r, h0:h0 + n, :], q[:, c0:c0 + 64 * n].rearrange("p (h d) -> p h d", h=n),
                            GAM[0:r, g:g + 1, :].broadcast_to([r, n, HD]), ALU.mult)
                    last.then_inc(xg_ready, 1)
                    pool.wait_ge(xg_ready, tt + 1)
                    if tt >= 1:
                        pool.wait_ge(k_out, 16 * k_stores(tt - 1))
                        pool.wait_ge(qs_lo, tt)
                    nc.gpsimd.tensor_tensor(XNB[0:r, :, :], XG[0:r, :, :],
                                            RYQ[0:r, 20 * tt:20 * tt + 20].unsqueeze(2).broadcast_to([r, 20, HD]), ALU.mult).then_inc(xn4_ready, 1)
                tt = prep(s, SPLIT_AT)
                if tt is not None:
                    r = rows_of(tt)
                    pool.wait_ge(qs_hi, tt + 1)
                    for br in range(2):
                        nc.gpsimd.tensor_tensor(QS[0:r, 8 * br:8 * br + 8, 1, :], XNB[0:r, 10 * br:10 * br + 8, :],
                                                QS[0:r, 8 * br:8 * br + 8, 0, :].bitcast(F32), ALU.subtract)
                    for b in range(2):
                        for br in range(2):
                            last = nc.gpsimd.tensor_tensor(KS[0:r, 2 * br:2 * br + 2, 2 + b, :], XNB[0:r, 10 * br + 8:10 * br + 10, :],
                                                           KS[0:r, 2 * br:2 * br + 2, 0, :].bitcast(F32), ALU.subtract)
                    last.then_inc(qs_lo, 1)
                if s in CACHE_STEP:
                    i = CACHE_STEP[s]
                    pool.wait_ge(cache_hi, i + 1)
                    for b in range(2):
                        last = nc.gpsimd.tensor_tensor(KSC[:, :, 2 + b, :], CK[:, i, :].rearrange("p (h d) -> p h d", h=2),
                                                       KSC[:, :, 0, :].bitcast(F32), ALU.subtract)
                    last.then_inc(cache_lo, 1)
            for j in range(2):
                pool.wait_ge(ow_hi, j + 1)
                nc.gpsimd.tensor_tensor(WOL[j % 2][:], ORAW[:, j % 2, :, :], WOH[j % 2][:].bitcast(F32), ALU.subtract).then_inc(ow_lo, 1)
            for i in range(3 * KD):
                j, g = OPROJ[i]
                g0, gn = GROUPS[g]
                pool.wait_ge(m_hi, i + 1)
                nc.gpsimd.tensor_tensor(ML[:, j, g0:g0 + gn], TM[:, i % 2, 2, 0:gn], MH[:, j, g0:g0 + gn].bitcast(F32), ALU.subtract).then_inc(m_lo, 1)
                if g == 2 and j + 2 < KD:
                    pool.wait_ge(ow_hi, j + 3)
                    nc.gpsimd.tensor_tensor(WOL[j % 2][:], ORAW[:, j % 2, :, :], WOH[j % 2][:].bitcast(F32), ALU.subtract).then_inc(ow_lo, 1)
                if g == 1 and 2 <= j < 6:
                    q = j - 2
                    pool.wait_ge(u_hi, 2 * (q + 1))
                    nc.gpsimd.tensor_tensor(UL[0][:, 2 * q:2 * q + 2, :], UQ[q % 2][:], UH[0][:, 2 * q:2 * q + 2, :].bitcast(F32), ALU.subtract).then_inc(u_lo, 2)
            u_low(pool, 1)
            for i in range(NYC * NT):
                c, tt = i // NT, i % NT
                if tt == 4 and c + 2 < NYC:
                    u_low(pool, c + 2)
                r = rows_of(tt)
                pool.wait_ge(y_mul, i + 1)
                pool.wait_ge(xr_in[i % 3], 16 * (i // 3 + 1))
                if i >= 3:
                    pool.wait_ge(y_out[i % 3], 16 * (i // 3))
                nc.gpsimd.tensor_tensor(YO[0:r, i % 3, :], YT[0:r, i % 3, :], XR[0:r, i % 3, :], ALU.add).then_inc(y_add, 1)

        @block.scalar
        def _(act):
            def w_hi(n):
                c, k = n // KD, n % KD
                if c >= NCH:
                    return
                cw = CHUNKS[c][2]
                act.wait_ge(raw_in[n % 4], 16 * (n // 4 + 1))
                if k == 0 and c == 2:
                    act.wait_ge(idx_pe, NT)
                if k == 0 and c >= 3:
                    act.wait_ge(piece_pe, PEND[c - 2])
                nc.scalar.activation(WH[c % 2][:, k, 0:cw], RAW[:, n % 4, 0:cw], ACT.Copy).then_inc(hi_done, 1)

            act.wait_ge(c_in, 16)
            nc.scalar.activation(CG[:], CS[:], ACT.Sigmoid).then_inc(c_sig, 1)
            for q in range(2 * NT):
                tt, half = q // 2, q % 2
                r = rows_of(tt)
                act.wait_ge(xt_pe, q + 1)
                nc.scalar.activation(XT[:, 4 * half:4 * half + 4, tcols(tt)],
                                     bank(q % 2).rearrange("p (k n) -> p k n", k=4)[:, :, 0:r], ACT.Copy).then_inc(xt_evac, 1)
            for n in range(KD):
                w_hi(n)
            act.wait_ge(ada_done, 1)
            nc.scalar.copy(MROW[:, D:2 * D], PS[0:2, 4:6, :].rearrange("p b n -> p (b n)")).then_inc(mrow_act, 1)
            def idx_out(i):
                r = rows_of(i)
                act.wait_ge(idx_pe, i + 1)
                if i >= 2:
                    act.wait_ge(ik_out[i % 2], 16 * (i // 2))
                    act.wait_ge(idx_lo, i - 1)
                nc.scalar.activation(NIDX[0:r, i % 2, :], bank(ibank(i))[0:r, 0:IDX_W], ACT.Copy).then_inc(idx_evac, 1)

            for part, (a, b) in enumerate(PARTS):
                if part == 2:
                    idx_out(0)
                for k in range(KD):
                    act.wait_ge(h_ready, KD * part + k + 1)
                    nc.scalar.activation(HH[:, k, a:b], XT[:, k, a:b], ACT.Copy).then_inc(hh_done, 1)
                    if part == 1:
                        w_hi(KD + k)
            def relus(tt):
                for h in range(4):
                    n = SHEADS.index((tt, h))
                    r, nk = rows_of(tt), keys_of(tt)
                    act.wait_ge(score_pe, n + 1)
                    v = PS[0:r, 4 + 2 * (n % 2):6 + 2 * (n % 2), :].rearrange("p b n -> p (b n)")[:, 0:nk]
                    nc.scalar.activation(v, v, ACT.Relu, scale=HD ** -0.5 * 0.5).then_inc(relu_done, 1)

            def nat_evac(c, j, p):
                r = rows_of(j)
                dst = STG2[0:r, p % 2, :] if c == 1 else STG[0:r, STG_Q[p] % 3, :]
                if c == 1 and p >= 2:
                    act.wait_ge(stg2_out[p % 2], 16 * (p // 2))
                nc.scalar.activation(dst, bank(pbank(p))[0:r, :], ACT.Copy).then_inc(nat_copied, 1)
                act.wait_ge(nat_copied, p + 1)
                blocks = [b for b in range(8) if (8 * (c - 1) + b) % 12 < 10]
                for b in blocks:
                    f = 8 * (c - 1) + b
                    head = 10 * (f // 12) + f % 12
                    v = bank(pbank(p))[0:r, HD * b:HD * (b + 1)]
                    last = nc.scalar.activation(v, v, ACT.Square, accum_out=SSQ[0:r, 20 * j + head:20 * j + head + 1])
                last.then_inc(piece_ev, 1)

            for i in range(ITEMS + 1):
                if 0 <= i - 1 - NAT0 < NT:
                    act.wait_ge(piece_pe, i - NAT0)
                    nat_evac(1, i - 1 - NAT0, i - 1 - NAT0)
                if 1 <= i < NT:
                    idx_out(i)
                if NT <= i < ITEMS:
                    act.wait_ge(idx_t, i - 1)
                    act.wait_ge(cik_in, 16)
                    nc.scalar.activation(IN2[i % 2][:, 4, 0, :], CIK[:, i - NT, :], ACT.Copy)
                    nc.scalar.activation(IN2[i % 2][:, 4, 1, :], CIK[:, i - NT, :], ACT.Copy).then_inc(idx_hi, 1)
                if NT <= i < ITEMS:
                    for n in range(2):
                        w_hi(2 * KD + 2 * (i - NT) + n)
                if i >= 1:
                    j = i - 1
                    r = rows_of(j) if j < NT else 128
                    act.wait_ge(idx_t, j + 1)
                    if j == 0:
                        act.wait_ge(hl_done, 3 * KD)
                    if j < NT:
                        nc.scalar.activation(IQT[:, :, tcols(j)], bank(2).rearrange("p (h n) -> p h n", h=4)[:, :, 0:r], ACT.Copy)
                    if j < SAMPLE:
                        dst = IKT[:, :, tcols(j)]
                    elif j == SAMPLE:
                        dst = IKTS[:, :, PAST:PAST + DEC]
                    else:
                        dst = IKTS[:, :, 128 * (j - NT):128 * (j - NT + 1)]
                    nc.scalar.activation(dst, bank(3)[:, 0:256].rearrange("p (h n) -> p h n", h=2)[:, :, 0:r], ACT.Copy).then_inc(idx_tev, 1)
                    if 2 <= j < SAMPLE:
                        relus(j)
            relus(SAMPLE)
            def high_parts(tt):
                r = rows_of(tt)
                act.wait_ge(xn4_ready, tt + 1)
                if tt >= 1:
                    act.wait_ge(tr_pe, TIDX[("K", tt - 1, 1)] + 1)
                    act.wait_ge(qs_lo, tt)
                for b in range(2):
                    nc.scalar.activation(QS[0:r, 8 * b:8 * b + 8, 0, :], XNB[0:r, 10 * b:10 * b + 8, :], ACT.Copy)
                    for d in range(2):
                        last = nc.scalar.activation(KS[0:r, 2 * b:2 * b + 2, d, :], XNB[0:r, 10 * b + 8:10 * b + 10, :], ACT.Copy)
                last.then_inc(qs_hi, 1)

            for p, (c, j, w) in enumerate(PIECES):
                if c == 1:
                    continue
                q = STG_Q[p]
                act.wait_ge(piece_pe, p + 1)
                if w[0] != "z" and q >= 3:
                    act.wait_ge(stg_out[q % 3], 16 * (q // 3))
                if w[0] == "nat":
                    nat_evac(c, j, p)
                else:
                    gn = GROUPS[w[2]][1]
                    if w[0] == "g":
                        nc.scalar.activation(STG[:, q % 3, 0:gn], bank(pbank(p))[:, 0:gn], ACT.Sigmoid).then_inc(piece_ev, 1)
                    else:
                        z = ZP.index(p)
                        if z >= 2:
                            act.wait_ge(z_pool, z - 1)
                        nc.scalar.activation(ZS[:, z % 2, 0:gn], bank(pbank(p))[:, 0:gn], ACT.Sigmoid)
                        nc.scalar.activation(ZC[:, z % 2, 0:gn], bank(pbank(p))[:, 0:gn], ACT.Copy).then_inc(piece_ev, 1)
                if j < KD:
                    w_hi(KD * (c + 1) + j)
                if c == NCH - 1 and j == 6:
                    high_parts(0)
                if c == NCH - 1 and j == 9:
                    t_evac(act, nc.scalar.copy, TQ[1][1], tev_act)
            def attention_high(g, half):
                g0, gn = GROUPS[g]
                act.wait_ge(z_in[g], 16)
                ks = slice(4 * half, 4 * half + 4)
                nc.scalar.activation(ZH[:, ks, g0:g0 + gn], ZST[g][:, ks, :], ACT.Copy).then_inc(az_hi, 1)

            for s in range(S0, S1):
                if s == 0:
                    nc.scalar.activation(ES[:, 1, :], IDF[:, 0:8], ACT.Exp)
                    act.wait_ge(mask_done, NT)
                if s == 32:
                    act.wait_ge(rest_in, 96)
                for x in TP[s]:
                    if EV[TIDX[x]] == "S" and TIDX[x] != 1:
                        t_evac(act, nc.scalar.copy, x, tev_act)
                if 0 <= s < NU:
                    u = s
                    tt, br, h = UNITS[u]
                    r, nk = rows_of(tt), unit_keys(u)
                    act.wait_ge(min_done, u + 1)
                    if u >= 3:
                        act.wait_ge(tr_pe, last_t(u - 3) + 1)
                    nc.scalar.activation(PB[u % 3][0:r, 0:nk], LG[u % 2][0:r, 0:nk], ACT.Exp, scale=-1.0,
                                         bias=NM[0:r, br, h:h + 1], accum_out=DEN[0:r, br, h:h + 1]).then_inc(exp_done, 1)
                if s == NU - 3:
                    act.wait_ge(oraw_in[0], 16)
                    act.wait_ge(qk_pe, NU - 16)
                    nc.scalar.activation(WOH[0][:], ORAW[:, 0, :, :], ACT.Copy).then_inc(ow_hi, 1)
                if s in (NU - 1, NU + 1):
                    act.wait_ge(min_done, NU - 8)
                    attention_high(0, int(s == NU + 1))
                if s % 16 == 0 and 16 <= s <= NU:
                    g = s // 16 - 1
                    act.wait_ge(sink_sum, g + 1)
                    nc.scalar.activation(ES[0:rows_of(g), 0, :], SD[0:rows_of(g), :], ACT.Exp).then_inc(sink_act, 1)
                tt = prep(s, SPLIT_AT)
                if tt is not None and tt >= 1:
                    high_parts(tt)
                if s in CACHE_STEP:
                    i = CACHE_STEP[s]
                    if i >= 1:
                        act.wait_ge(tr_pe, TIDX[("C", i - 1, 0)] + 1)
                    for d in range(2):
                        last = nc.scalar.activation(KSC[:, :, d, :], CK[:, i, :].rearrange("p (h d) -> p h d", h=2), ACT.Copy)
                    last.then_inc(cache_hi, 1)
            act.wait_ge(min_done, NU)
            act.wait_ge(pv_pe, NU)
            for half in range(2):
                attention_high(1, half)
            act.wait_ge(oraw_in[1], 16)
            nc.scalar.activation(WOH[1][:], ORAW[:, 1, :, :], ACT.Copy).then_inc(ow_hi, 1)
            for i in range(3 * KD):
                j, g = OPROJ[i]
                g0, gn = GROUPS[g]
                act.wait_ge(m_dve, i + 1)
                nc.scalar.activation(MH[:, j, g0:g0 + gn], TM[:, i % 2, 2, 0:gn], ACT.Copy).then_inc(m_hi, 1)
                if i == 1:
                    for half in range(2):
                        attention_high(2, half)
                if g == 2 and j + 2 < KD:
                    act.wait_ge(oraw_in[j % 2], 16 * (j // 2 + 2))
                    act.wait_ge(o_pe, i + 1)
                    nc.scalar.activation(WOH[j % 2][:], ORAW[:, j % 2, :, :], ACT.Copy).then_inc(ow_hi, 1)
                if g == 1 and 2 <= j < 6:
                    q = j - 2
                    act.wait_ge(uq_in[q % 2], 16 * (q // 2 + 1))
                    nc.scalar.activation(UH[0][:, 2 * q:2 * q + 2, :], UQ[q % 2][:], ACT.Copy).then_inc(u_hi, 2)
            for c in range(1, NYC):
                act.wait_ge(uraw_in[c % 2], 16 * ((c + 1) // 2))
                for k in range(KD):
                    nc.scalar.activation(UH[c][:, k, :], URAW[c % 2][:, k, :], ACT.Copy).then_inc(u_hi, 1)

        @block.vector
        def _(dve):
            V = nc.vector
            steps = [0]

            def link(ins):
                steps[0] += 1
                ins.then_inc(dve_step, 1)
                dve.wait_ge(dve_step, steps[0])

            dve.wait_ge(c_sig, 1)
            V.tensor_tensor(CSIL[:], CS[:], CG[:], ALU.mult).then_inc(c_ready, 1)
            dve.wait_ge(consts_in, 16 * N_SMALL)
            V.tensor_copy(IDR[:], IDF[:])
            V.tensor_copy(IDB[:], IDF[:]).then_inc(ident_ready, 1)
            V.tensor_scalar(NSINK[:], SINK[:], -1.0, None, ALU.mult)
            link(V.memset(SS[:], 1.0))
            V.memset(SSQ[:], 1.0)
            for i in range(3):
                n = min(512, BIAS_L - 512 * i)
                dve.wait_ge(bias_pe, i + 1)
                V.tensor_scalar(BV[:, 512 * i:512 * i + n], bank(i % 2)[0:16, 0:n], -1.0, None, ALU.mult).then_inc(bias_sb, 1)
            for a, b in ((0, 4), (4, NT)):
                for tt in range(a, b):
                    r = rows_of(tt)
                    dve.wait_ge(x_in[tt], 16)
                    link(V.tensor_tensor_reduce(out=SQJ[0:r, :], in0=XNAT[tt][0:r, :], in1=XNAT[tt][0:r, :], scale=1.0,
                                                scalar=0.0, op0=ALU.mult, op1=ALU.add, accum_out=SS[0:r, tt:tt + 1]))
                rsqrt_chain(link, RY[:, a:b], SS[:, a:b], RV[:, a:b], RI[:, a:b], RT[:, a:b], 1.0 / D)
                for tt in range(a, b):
                    r = rows_of(tt)
                    V.tensor_scalar(XNAT[tt][0:r, :], XNAT[tt][0:r, :], RY[0:r, tt:tt + 1], None, ALU.mult).then_inc(xn_ready, 1)
            dve.wait_ge(ada_done, 1)
            V.tensor_copy(MROW[:, 0:D], PS[0:2, 2:4, :].rearrange("p b n -> p (b n)")).then_inc(mrow_ready, 1)
            V.tensor_copy(MROWG[:, :], PS[0:2, 6:8, :].rearrange("p b n -> p (b n)")).then_inc(mrow_ready, 1)
            dve.wait_ge(mod_pe, 1)
            V.tensor_tensor(MOD[:], bank(0)[:, 0:48].rearrange("p (c j) -> p c j", j=2),
                            BADA[:].unsqueeze(2).broadcast_to([128, 24, 2]), ALU.add).then_inc(mod_ready, 1)
            dve.wait_ge(mod_ready, 1)
            steps[0] += 1
            V.scalar_tensor_tensor(out=SCL[:], in0=MOD[:, 8:16, :], scalar=1.0, in1=NG[:].unsqueeze(2).broadcast_to([128, KD, 2]),
                                   op0=ALU.add, op1=ALU.mult).then_inc(dve_step, 1)
            dve.wait_ge(dve_step, steps[0])
            dve.wait_ge(xt_evac, 2 * NT)

            def h_low(part, k):
                a, b = PARTS[part]
                dve.wait_ge(hh_done, KD * part + k + 1)
                V.tensor_tensor(HL[:, k, a:b], XT[:, k, a:b], HH[:, k, a:b].bitcast(F32), ALU.subtract).then_inc(hl_done, 1)

            def idx_high(i):
                r = rows_of(i)
                slot = IN2[i % 2]
                if i >= 2:
                    dve.wait_ge(idx_t, i - 1)
                dve.wait_ge(idx_evac, i + 1)
                V.tensor_copy(slot[0:r, 0:4, 0, :], NIDX[0:r, i % 2, 0:256].rearrange("p (h d) -> p h d", h=4))
                V.tensor_copy(IW[0:r, i, :], NIDX[0:r, i % 2, 320:324])
                V.tensor_copy(slot[0:r, 4, :, :], NIDX[0:r, i % 2, 256:320].unsqueeze(1).broadcast_to([r, 2, HD])).then_inc(idx_hi, 1)

            for part, (a, b) in enumerate(PARTS):
                if part == 2:
                    idx_high(0)
                for k in range(KD):
                    m = min(b, SEQ)
                    last = V.tensor_scalar(XT[:, k, a:m], XT[:, k, a:m], SCL[:, k, 0:1], MOD[:, k, 0:1], ALU.mult, ALU.add)
                    if b == TOK:
                        last = V.tensor_scalar(XT[:, k, SEQ:TOK], XT[:, k, SEQ:TOK], SCL[:, k, 1:2], MOD[:, k, 1:2], ALU.mult, ALU.add)
                    last.then_inc(h_ready, 1)
                    if k >= 1:
                        h_low(part, k - 1)
                h_low(part, KD - 1)
                if part == 1:
                    dve.wait_ge(gate_pe, 1)
                    V.tensor_copy(GROW[:], bank(7)[0:16, 0:128]).then_inc(gate_rows, 1)
            def scores(tt):
                r, nk = rows_of(tt), keys_of(tt)
                out = SC[0:r, SOFF[tt]:SOFF[tt] + nk]
                for h in range(4):
                    n = SHEADS.index((tt, h))
                    v = PS[0:r, 4 + 2 * (n % 2):6 + 2 * (n % 2), :].rearrange("p b n -> p (b n)")[:, 0:nk]
                    dve.wait_ge(relu_done, n + 1)
                    if h == 0:
                        last = V.tensor_scalar(out, v, IW[0:r, tt, 0:1], None, ALU.mult)
                    else:
                        dve.wait_ge(acc_done, n)
                        last = V.scalar_tensor_tensor(out=out, in0=v, scalar=IW[0:r, tt, h:h + 1], in1=out, op0=ALU.mult, op1=ALU.add)
                    last.then_inc(acc_done, 1)
                if tt != SAMPLE:
                    dve.wait_ge(acc_done, SHEADS.index((tt, 3)) + 1)
                    link(V.memset(SC[0:CHUNK, SOFF[tt] + nk - CHUNK:SOFF[tt] + nk], -NEG_BIG))

            def pick_rounds(tiles, rounds, unroll, last=True):
                n = len(tiles)
                with dve.Fori(0, rounds // unroll):
                    for un in range(unroll):
                        for a, tt in enumerate(tiles):
                            r, w = rows_of(tt), SC[0:rows_of(tt), SOFF[tt]:SOFF[tt] + keys_of(tt)]
                            if un > 0:
                                dve.wait_ge(sel_step, 2 * n * un - n + a + 1)
                            V.max(M8[0:r, a, :], w).then_inc(sel_step, 1)
                        for a, tt in enumerate(tiles):
                            r, w = rows_of(tt), SC[0:rows_of(tt), SOFF[tt]:SOFF[tt] + keys_of(tt)]
                            dve.wait_ge(sel_step, 2 * n * un + a + 1)
                            V.match_replace(w, M8[0:r, a, :], w, TAKEN).then_inc(sel_step, 1)
                    dve.wait_ge(sel_step, 2 * n * unroll)
                    dve.sem_clear(sel_step)
                if last:
                    for tt in tiles:
                        mask(tt)

            def mask(tt):
                r, nk = rows_of(tt), keys_of(tt)
                V.tensor_scalar(MASK[0:r, MOFF[tt]:MOFF[tt] + nk], SC[0:r, SOFF[tt]:SOFF[tt] + nk],
                                -2.0e38, NEG_BIG, ALU.is_gt, ALU.mult).then_inc(mask_done, 1)

            for i in range(1, NT + 1):
                if i < NT:
                    idx_high(i)
                if 2 <= i - 1 < SAMPLE:
                    scores(i - 1)
            dve.wait_ge(acc_done, SHEADS.index((SAMPLE - 1, 3)) + 1)
            pick_rounds((2, 3), EARLY_ROUNDS, 4, last=False)
            scores(SAMPLE)
            dve.wait_ge(acc_done, len(SHEADS))
            for tt in range(2):
                nk = keys_of(tt)
                link(V.memset(MASK[:, MOFF[tt]:MOFF[tt] + nk], 0.0))
                V.memset(MASK[0:CHUNK, MOFF[tt] + nk - CHUNK:MOFF[tt] + nk], NEG_BIG).then_inc(mask_done, 1)
            for i in range(2):
                dve.wait_ge(stg2_out[i], 16 * ((NT + 1 - i) // 2))
            pick_rounds((2, 3), KSEL // 8 - EARLY_ROUNDS, 4)
            for pair in ((4, 5), (6, 7)):
                pick_rounds(pair, KSEL // 8, 4)
            dve.wait_ge(piece_ev, PEND[3])
            rsqrt_chain(link, RYQ[:], SSQ[:], RVQ[:], RIQ[:], RTQ[:], 1.0 / HD)
            ry = RYQ[:].rearrange("p (t h) -> p t h", h=10)[:, :, 0:8]
            V.tensor_scalar(ry, ry, -HD ** -0.5, None, ALU.mult).then_inc(rms_ready, 1)
            pick_rounds((SAMPLE,), KSEL_S // 8, 3)
            def attention_low(q):
                g, ks = q // 2, slice(4 * (q % 2), 4 * (q % 2) + 4)
                g0, gn = GROUPS[g]
                dve.wait_ge(az_hi, q + 1)
                V.tensor_tensor(ZL[:, ks, g0:g0 + gn], ZST[g][:, ks, :], ZH[:, ks, g0:g0 + gn].bitcast(F32), ALU.subtract).then_inc(az_lo, 1)

            for s in range(S0, S1):
                if s == NU + 2:
                    dve.wait_ge(qk_pe, NU)
                    attention_low(0)
                if s == NU + 4:
                    attention_low(1)
                if s == 0:
                    dve.wait_ge(kva_in, 32)
                    for i in range(3):
                        dve.wait_ge(stg_out[i], 16 * NST[i])
                    dve.wait_ge(mask_done, NT)
                if s == 6:
                    dve.wait_ge(kvb_in, 32)
                    V.memset(BTB[0:CHUNK, :, 192:256], NEG_BIG)
                    link(V.memset(BTB[CHUNK:128, :, 0:64], NEG_BIG))
                if s == 16:
                    dve.wait_ge(kvc_in, 32)
                if s == 32:
                    dve.wait_ge(bta_in, 16)
                if 0 <= s < NU:
                    u = s
                    tt, br, h = UNITS[u]
                    r, nk = rows_of(tt), unit_keys(u)
                    if br == 0:
                        j0 = 384 if tt == SAMPLE else 896 - 128 * tt
                        bias, init = BTA[0:r, h, j0:j0 + nk] if tt else BT0[:, h, :], 3.0e38
                    else:
                        j0 = 128 if tt == 0 else 0
                        bias, init = BTB[0:r, h, j0:j0 + nk], NSINK[0:r, h:h + 1]
                    dve.wait_ge(qk_pe, u + 1)
                    if u >= 2:
                        dve.wait_ge(exp_done, u - 1)
                    v = PS[0:r, 2 * (u % 2):2 * (u % 2) + 2, :].rearrange("p b n -> p (b n)")[:, 0:nk]
                    V.tensor_tensor_reduce(out=LG[u % 2][0:r, 0:nk], in0=v, in1=bias, scale=1.0, scalar=init,
                                           op0=ALU.add, op1=ALU.min, accum_out=NM[0:r, br, h:h + 1]).then_inc(min_done, 1)
                if s % 16 == 0 and 16 <= s <= NU:
                    g = s // 16 - 1
                    r = rows_of(g)
                    dve.wait_ge(min_done, 16 * (g + 1))
                    if g >= 1:
                        dve.wait_ge(sink_act, g)
                    V.tensor_tensor(SD[0:r, :], NM[0:r, 1, :], SINK[0:r, :], ALU.add).then_inc(sink_sum, 1)
                for x in TP[s]:
                    if EV[TIDX[x]] == "V":
                        t_evac(dve, V.tensor_copy, x, tev_dve)
                if (s - 11) % 8 == 0 and 11 <= s <= NU + 3:
                    g = (s - 11) // 8
                    tt, br = g // 2, g % 2
                    r = rows_of(tt)
                    dve.wait_ge(exp_done, 8 * (g + 1))
                    if br:
                        dve.wait_ge(sink_act, tt + 1)
                        link(V.tensor_tensor(DEN[0:r, 1, :], DEN[0:r, 1, :], ES[0:r, 0, :], ALU.add))
                    link(V.reciprocal(RDEN[0:r, :], DEN[0:r, br, :]))
                    dve.wait_ge(pv_pe, 8 * (g + 1))
                    if g >= 2:
                        dve.wait_ge(tr_pe, TIDX[("A", (g - 2) // 2, br)] + 1)
                    V.tensor_tensor(ATTN[br][0:r, :].rearrange("p (h d) -> p h d", h=8),
                                    bank(6 + br)[0:r, :].rearrange("p (h d) -> p h d", h=8),
                                    RDEN[0:r, :].unsqueeze(2).broadcast_to([r, 8, HD]), ALU.mult).then_inc(att_done, 1)
            for q in range(2, 4):
                attention_low(q)
            for i in range(3 * KD):
                j, g = OPROJ[i]
                gn = GROUPS[g][1]
                dve.wait_ge(o_pe, i + 1)
                dve.wait_ge(g_in[i % 3], 32 * (i // 3 + 1))
                if i >= 2:
                    dve.wait_ge(m_lo, i - 1)
                V.tensor_tensor(TM[:, i % 2, 0, 0:gn], bank(2 * (i % 2))[:, 0:gn], GT[:, i % 3, 0, 0:gn], ALU.mult)
                link(V.tensor_tensor(TM[:, i % 2, 1, 0:gn], bank(2 * (i % 2) + 1)[:, 0:gn], GT[:, i % 3, 1, 0:gn], ALU.mult))
                V.tensor_tensor(TM[:, i % 2, 2, 0:gn], TM[:, i % 2, 0, 0:gn], TM[:, i % 2, 1, 0:gn], ALU.add).then_inc(m_dve, 1)
                if i == 1:
                    for q in range(4, 6):
                        attention_low(q)
            dve.wait_ge(gate_in, 32)
            for i in range(NYC * NT):
                c, tt = i // NT, i % NT
                r = rows_of(tt)
                dve.wait_ge(y_pe, i + 1)
                if i >= 3:
                    dve.wait_ge(y_add, i - 2)
                V.tensor_tensor(YT[0:r, i % 3, :], bank(4 + i % 3)[0:r, 0:YW],
                                GATE[0:r, int(tt == SAMPLE), YW * c:YW * (c + 1)], ALU.mult).then_inc(y_mul, 1)

        @block.tensor
        def _(pe):
            T = nc.tensor

            def three(out, wh, wl, mh, ml, first, last):
                T.matmul(out, wh, mh, start=first, stop=False)
                T.matmul(out, wh, ml, start=False, stop=False)
                return T.matmul(out, wl, mh, start=False, stop=last)

            def ada(k):
                pe.wait_ge(wada_in[k], 16)
                for c in range(6):
                    last = T.matmul(bank(2 + c)[0:2, :], CSIL[:, k, :], WADA[k][:, 512 * c:512 * (c + 1)],
                                    start=(k == 0), stop=(k == KD - 1))
                return last

            def bias_rows(i):
                n = min(512, BIAS_L - 512 * i)
                if i == 2:
                    pe.wait_ge(bias_sb, 1)
                T.matmul(bank(i % 2)[0:16, 0:n], RELB[:], ONEH[:, 512 * i:512 * i + n], start=True, stop=True).then_inc(bias_pe, 1)

            def x_transposes(tt):
                r = rows_of(tt)
                pe.wait_ge(xn_ready, tt + 1)
                for half in range(2):
                    q = 2 * tt + half
                    if q >= 2:
                        pe.wait_ge(xt_evac, q - 1)
                    for b in range(4):
                        k = 4 * half + b
                        last = T.transpose(bank(q % 2)[:, 128 * b:128 * b + r], XNAT[tt][0:r, 128 * k:128 * (k + 1)], IDF[0:r, 0:r])
                    last.then_inc(xt_pe, 1)

            pe.wait_ge(c_ready, 1)
            ada(0)
            pe.wait_ge(consts_in, 16 * N_SMALL)
            bias_rows(0)
            bias_rows(1)
            ada(1)
            bias_rows(2)
            ada(2)
            ada(3)
            pe.wait_ge(bias_sb, 3)
            for tt in range(4):
                x_transposes(tt)
            for k in range(4, 6):
                ada(k)
            for tt in range(4, NT):
                x_transposes(tt)
            ada(6)
            last = ada(7)
            last.then_inc(ada_done, 1)
            pe.wait_ge(xt_evac, 2 * NT)
            for c in range(24):
                if c == 0:
                    pe.wait_ge(mrow_ready, 1)
                if c == 8:
                    pe.wait_ge(mrow_act, 1)
                if c == 16:
                    pe.wait_ge(mrow_ready, 2)
                src = MROW[:, 128 * c:128 * (c + 1)] if c < 16 else MROWG[:, 128 * (c - 16):128 * (c - 15)]
                last = T.transpose(bank(0)[:, 2 * c:2 * c + 2], src, IDF[0:2, 0:2])
            last.then_inc(mod_pe, 1)
            def score_head(tt, h):
                r, nk = rows_of(tt), keys_of(tt)
                keys = IKTS if tt == SAMPLE else IKT
                n = SHEADS.index((tt, h))
                if n >= 2:
                    pe.wait_ge(acc_done, n - 1)
                for b in range(0, nk, 512):
                    m = min(512, nk - b)
                    out = PS[0:r, 4 + 2 * (n % 2) + b // 512, 0:m]
                    for part in range(2):
                        last = T.matmul(out, IQT[:, h, tcols(tt)], keys[:, part, b:b + m], start=(part == 0), stop=(part == 1))
                last.then_inc(score_pe, 1)

            def piece(p, quarters=range(4)):
                c, j, w = PIECES[p]
                if quarters[0] == 0:
                    if j == 0:
                        pe.wait_ge(lo_done, KD * (c + 1))
                    if p == 0:
                        pe.wait_ge(idx_evac, NAT0)
                    elif p < 6:
                        pe.wait_ge(piece_ev, p if p < 5 else 4)
                        if p == 5:
                            pe.wait_ge(idx_evac, NT)
                    else:
                        pe.wait_ge(piece_ev, p - 1 if p < NT else p - 3)
                H, L = WH[c % 2], WL[c % 2]
                for k in range(2 * quarters[0], 2 * quarters[-1] + 2):
                    if w[0] == "nat":
                        last = three(bank(pbank(p))[0:rows_of(j), :], HH[:, k, tcols(j)], HL[:, k, tcols(j)],
                                     H[:, k, :], L[:, k, :], k == 0, k == KD - 1)
                    else:
                        g0, gn = GROUPS[w[2]]
                        bc = slice(128 * w[1], 128 * (w[1] + 1))
                        last = three(bank(pbank(p))[:, 0:gn], H[:, k, bc], L[:, k, bc],
                                     HH[:, k, g0:g0 + gn], HL[:, k, g0:g0 + gn], k == 0, k == KD - 1)
                if quarters[-1] == 3:
                    last.then_inc(piece_pe, 1)

            def score(tt, p):
                for h in range(4):
                    if h == 0:
                        if p is not None:
                            piece(p, [0])
                        pe.wait_ge(idx_tev, ITEMS if tt == SAMPLE else tt + 1)
                    score_head(tt, h)
                    if p is not None and h >= 1:
                        piece(p, [h])

            def project(i):
                r = rows_of(i)
                part = [q for q in range(3) if PARTS[q][1] >= 128 * i + r][0]
                pe.wait_ge(hl_done, KD * (part + 1))
                if i >= NAT0:
                    pe.wait_ge(idx_evac, 1 if i == NAT0 else i)
                for k in range(KD):
                    last = three(bank(ibank(i))[0:r, 0:IDX_W], HH[:, k, tcols(i)], HL[:, k, tcols(i)],
                                 WH[0][:, k, 0:IDX_W], WL[0][:, k, 0:IDX_W], k == 0, k == KD - 1)
                last.then_inc(idx_pe, 1)

            pe.wait_ge(mod_ready, 1)
            T.transpose(bank(7)[0:16, 0:128], MOD[:, 16:24, :].rearrange("p k j -> p (k j)"), IDF[:]).then_inc(gate_pe, 1)
            pe.wait_ge(lo_done, KD)
            pe.wait_ge(ident_ready, 1)
            for i in range(ITEMS + 1):
                if i == 0:
                    project(0)
                if i + 1 < NAT0:
                    project(i + 1)
                if NAT0 <= i < NT:
                    project(i)
                if i >= 1:
                    j = i - 1
                    r = rows_of(j) if j < NT else 128
                    pe.wait_ge(idx_lo, j + 1)
                    if j >= 1:
                        pe.wait_ge(idx_tev, j)
                    slot = IN2[j % 2]
                    for h in range(6):
                        if h < 4 and j >= NT:
                            continue
                        dst = bank(2)[:, 128 * h:128 * h + r] if h < 4 else bank(3)[:, 128 * (h - 4):128 * (h - 4) + r]
                        last = T.transpose(dst.bitcast(F32R), slot[0:r, h, :, :].rearrange("p a d -> p (a d)"), IDR[0:r, 0:r])
                    last.then_inc(idx_t, 1)
                    p = i - NAT0 if 0 <= i - NAT0 < NT else None
                    if j == 2:
                        pe.wait_ge(gate_rows, 1)
                        pe.wait_ge(idx_evac, NAT0)
                    if 2 <= j < SAMPLE:
                        score(j, p)
                    elif p is not None:
                        piece(p)
            score(SAMPLE, NT)
            def transposes(x):
                q = TIDX[x]
                if q >= 2:
                    wait_evac(pe, q - 2)
                out = bank(4 + q % 2)
                if x[0] == "P":
                    u = x[1]
                    tt = UNITS[u][0]
                    r, nk = rows_of(tt), unit_keys(u)
                    pe.wait_ge(exp_done, u + 1)
                    for b in range(4 * x[2], min(4 * x[2] + 4, (nk + 127) // 128)):
                        m = min(128, nk - 128 * b)
                        last = T.transpose(out[0:m, 128 * (b % 4):128 * (b % 4) + r], PB[u % 3][0:r, 128 * b:128 * b + m], IDF[0:r, 0:r])
                elif x[0] == "A":
                    g, r = 2 * x[1] + x[2], rows_of(x[1])
                    pe.wait_ge(att_done, g + 1)
                    for b in range(4):
                        last = T.transpose(out[:, 128 * b:128 * b + r], ATTN[x[2]][0:r, 128 * b:128 * (b + 1)], IDF[0:r, 0:r])
                else:
                    if x[0] == "C":
                        r = 128
                        pe.wait_ge(cache_lo, x[1] + 1)
                        src = [KSC[:, kv, 2 * p:2 * p + 2, :] for kv in range(2) for p in range(2)]
                    else:
                        r = rows_of(x[1])
                        pe.wait_ge(qs_lo, x[1] + 1)
                        if x[0] == "Q":
                            src = [QS[0:r, 4 * x[2] + b, :, :] for b in range(4)]
                        else:
                            src = [KS[0:r, 2 * x[2] + kv, 2 * p:2 * p + 2, :] for kv in range(2) for p in range(2)]
                    for b in range(4):
                        last = T.transpose(out[:, 128 * b:128 * b + r].bitcast(F32R), src[b].rearrange("p a d -> p (a d)"), IDR[0:r, 0:r])
                last.then_inc(tr_pe, 1)

            for p in range(NT + 1, NP):
                piece(p)
                for n in {NP - 4: (0, 1), NP - 2: (2, 3)}.get(p, ()):
                    transposes(TQ[n][1])
            pe.wait_ge(piece_ev, NP)
            pe.wait_ge(mask_done, NT)
            for s in range(S0, S1):
                if s == 0:
                    pe.wait_ge(kva_in, 32)
                if s == 8:
                    pe.wait_ge(kvb_in, 32)
                if s == 16:
                    pe.wait_ge(kvc_in, 32)
                if s == 32:
                    pe.wait_ge(rest_in, 96)
                if 0 <= s < NU:
                    u = s
                    tt, br, h = UNITS[u]
                    r, nk = rows_of(tt), unit_keys(u)
                    if h == 0:
                        wait_evacs(pe, TIDX[("K", tt, 1)])
                    if u >= 2:
                        pe.wait_ge(min_done, u - 1)
                    if br == 0:
                        keys, k0 = (KTAS if tt == SAMPLE else KTA), 0
                    else:
                        keys, k0 = (KTBS, 0) if tt == SAMPLE else (KTB, 128 * max(tt - 1, 0))
                    for b in range(0, nk, 512):
                        m = min(512, nk - b)
                        out = PS[0:r, 2 * (u % 2) + b // 512, 0:m]
                        for part in range(2):
                            last = T.matmul(out, QT[tt % 2][:, 8 * br + h, 0:r], keys[:, h // 4, part, k0 + b:k0 + b + m],
                                            start=(part == 0), stop=(part == 1 and br == 1))
                        if br == 0:
                            last = T.matmul(out, IDB[0:r, 0:r], MASK[0:r, MOFF[tt] + b:MOFF[tt] + b + m], start=False, stop=True)
                    last.then_inc(qk_pe, 1)
                for x in TP[s]:
                    if TIDX[x] >= EARLY_T:
                        transposes(x)
                if 0 <= s - 3 < NU:
                    u = s - 3
                    tt, br, h = UNITS[u]
                    r, nk = rows_of(tt), unit_keys(u)
                    wait_evacs(pe, last_t(u))
                    g = 2 * tt + br
                    if h == 0 and g >= 2:
                        pe.wait_ge(att_done, g - 1)
                    kb = (nk + 127) // 128
                    kv = slice(HD * (h // 4), HD * (h // 4) + HD)
                    for b in range(kb):
                        m = min(128, nk - 128 * b)
                        if br == 0:
                            v = VAS[0:m, b, kv] if tt == SAMPLE else VA[0:m, b, kv] if tt else VA0[:, kv]
                        else:
                            v = VBS[0:m, b, kv] if tt == SAMPLE else VB[0:m, max(tt - 1, 0) + b, kv]
                        last = T.matmul(bank(6 + br)[0:r, HD * h:HD * (h + 1)], PT[0:m, u % 2, 128 * b:128 * b + r], v,
                                        start=(b == 0), stop=(b == kb - 1))
                    last.then_inc(pv_pe, 1)
            for i in range(3 * KD):
                j, g = OPROJ[i]
                g0, gn = GROUPS[g]
                if g == 0:
                    pe.wait_ge(ow_lo, j + 1)
                if j == 0:
                    pe.wait_ge(az_lo, 2 * (g + 1))
                if i >= 2:
                    pe.wait_ge(m_dve, i - 1)
                for b in range(2):
                    for k in range(4 * b, 4 * b + 4):
                        last = three(bank(2 * (i % 2) + b)[:, 0:gn], WOH[j % 2][:, k, :], WOL[j % 2][:, k, :],
                                     ZH[:, k, g0:g0 + gn], ZL[:, k, g0:g0 + gn], k == 4 * b, k == 4 * b + 3)
                last.then_inc(o_pe, 1)
            for i in range(NYC * NT):
                c, tt = i // NT, i % NT
                if c == 0 and tt % 3 == 0:
                    pe.wait_ge(m_lo, 3 * (KD - 1) + tt // 3 + 1)
                if tt == 0:
                    pe.wait_ge(u_lo, KD * (c + 1))
                if i >= 3:
                    pe.wait_ge(y_mul, i - 2)
                for k in range(KD):
                    last = three(bank(4 + i % 3)[0:rows_of(tt), 0:YW], MH[:, k, tcols(tt)], ML[:, k, tcols(tt)],
                                 UH[c][:, k, :], UL[c][:, k, :], k == 0, k == KD - 1)
                last.then_inc(y_pe, 1)

    return nc


_OUTS = [((1, SEQ, D)), ((1, DEC, D)),
         (1, 1, SEQ, 2, HD), (1, 1, SEQ, 2, HD), (1, 1, SEQ, HD), (1, 1, WIN, 2, HD), (1, 1, WIN, 2, HD),
         (1, 1, DEC, 2, HD), (1, 1, DEC, 2, HD), (1, 1, DEC, HD), (1, 1, WIN, 2, HD), (1, 1, WIN, 2, HD)]
_OUT_NAMES = ["y_prompt", "y_sample", "pa_k", "pa_v", "pa_ik", "pb_k", "pb_v", "sa_k", "sa_v", "sa_ik", "sb_k", "sb_v"]
_OUT_SHAPES = [(SEQ, D), (DEC, D), (SEQ, 128), (SEQ, 128), (SEQ, HD), (WIN, 128), (WIN, 128),
               (DEC, 128), (DEC, 128), (DEC, HD), (WIN, 128), (WIN, 128)]


def kernel(**inputs):
    import numpy as np
    import concourse.bacc as bacc
    from concourse.bass_utils import run_bass_kernel_spmd

    f = np.float32
    x = {n: np.ascontiguousarray(a) for n, a in inputs.items()}
    w_in = x["w_in"][0]
    spans = ((1280, 1604), (0, 768), (1604, 2372), (768, 1280), (2372, 2884), (2884, 4932))

    def cols(v):
        return np.ascontiguousarray(v.reshape(-1, 128).T)

    rel = np.arange(BIAS_L) - (SEQ - 1)
    n = np.abs(rel)
    large = 8 + (np.log(np.maximum(n, 1).astype(f) / f(8)) / f(np.log(128.0)) * f(8)).astype(np.int32)
    bucket = (rel > 0) * 16 + np.where(n < 8, n, np.minimum(large, 15))
    onehot = (np.arange(32)[:, None] == bucket[None, :]).astype(f)
    arrays = {
        "x_prompt": x["x_prompt"][0], "x_sample": x["x_sample"][0],
        "w_all": np.concatenate([w_in[:, a:b] for a, b in spans], axis=1),
        "w_ada": x["w_ada"][0], "w_o": np.concatenate([x["w_oa"][0], x["w_ob"][0]], axis=0), "w_out": x["w_out"][0],
        "cache_ak": x["cache_a_k"].reshape(PAST, 128), "cache_av": x["cache_a_v"].reshape(PAST, 128),
        "cache_ik": x["cache_a_ik"].reshape(PAST, HD),
        "cache_bk": x["cache_b_k"].reshape(WIN, 128), "cache_bv": x["cache_b_v"].reshape(WIN, 128),
        "c_cols": np.ascontiguousarray(np.stack([cols(x["c_prompt"]), cols(x["c_sample"])], axis=2)),
        "ng_cols": cols(x["norm_g"]), "bada_cols": cols(x["b_ada"]),
        "gammas": np.ascontiguousarray(np.broadcast_to(
            np.stack([x[k][0] for k in ("a_q_norm", "a_k_norm", "b_q_norm", "b_k_norm")])[None], (128, 4, HD))),
        "sinks": np.ascontiguousarray(np.broadcast_to(x["b_sinks"], (128, 8))),
        "rel_bias": x["rel_bias"], "ident": np.eye(128, dtype=f), "onehot": onehot,
    }
    nc = bacc.Bacc("TRN2", target_bir_lowering=False, num_devices=1)
    t, ins = {}, {}
    for name, a in arrays.items():
        a = np.ascontiguousarray(a)
        ins[f"in_{name}"] = a
        t[name] = nc.dram_tensor(f"in_{name}", a.shape, mybir.dt.from_np(a.dtype), kind="ExternalInput").ap()
    for name, shape in zip(_OUT_NAMES, _OUT_SHAPES):
        t[name] = nc.dram_tensor(f"out_{name}", shape, F32, kind="ExternalOutput").ap()
    build_program(nc, t)
    r = run_bass_kernel_spmd(nc, [ins], core_ids=[0]).results[0]
    return tuple(np.asarray(r[f"out_{name}"]).reshape(shape) for name, shape in zip(_OUT_NAMES, _OUTS))
```
